# Optimizing a Trainium2 kernel written in Bass

```python
import math
import jax
import jax.numpy as jnp
from jax import lax
import numpy as np

D_MODEL = 1024
BATCH = 1
SEQ = 256
DEPTH = 2

GRID_W = 64
CTX_LEN = 256
CHUNK = 64
EPS = 1e-6
H_A = 4
DH_A = 128
W_A = H_A * DH_A
H_B = 4
DH_B = 128
W_B = H_B * DH_B
CONV_K = 5
H_C = 8
DK_C = 128
DV_C = 128
C_K = H_C * DK_C
C_V = H_C * DV_C
N_EXPERTS = 16
N_GROUPS = 4
EXPERTS_PER_GROUP = N_EXPERTS // N_GROUPS
GROUP_SCORE_K = 2
TOP_K = 2
D_FF_EXPERT = 512
N_EVEN = (DEPTH + 1) // 2
N_ODD = DEPTH // 2
AB_SPLITS = (W_A, W_A, W_A, W_A, W_B, W_B, W_B, W_B, 2 * H_A, 2 * H_A, 2 * H_B, 2 * H_B)
P_AB = sum(AB_SPLITS)
C_SPLITS = (C_K, C_K, C_K, C_V, C_V)
P_C = sum(C_SPLITS)

kernel_name = 'hybrid_mlstm_gdn_hgrn2_moe_prefix_dit'

def rms_norm(x, gain):
    xf = x.astype(jnp.float32)
    y = xf * lax.rsqrt(jnp.mean(jnp.square(xf), axis=-1, keepdims=True) + EPS)
    return (y * gain.astype(jnp.float32)).astype(x.dtype)

def head_rms_norm(h, gain):
    b, l, nh, dh = h.shape
    y = h * lax.rsqrt(jnp.mean(jnp.square(h), axis=-1, keepdims=True) + EPS)
    return y.reshape(b, l, nh * dh) * gain.astype(jnp.float32)

def l2_normalize(t):
    return t * lax.rsqrt(jnp.sum(jnp.square(t), axis=-1, keepdims=True) + EPS)

def split_cols(p, sizes):
    return jnp.split(p, np.cumsum(sizes)[:-1].tolist(), axis=-1)

def seg_flip(t, n_ctx):
    return jnp.concatenate([jnp.flip(t[:, :n_ctx], 1), jnp.flip(t[:, n_ctx:], 1)], axis=1)

def stack_dirs(t_fwd, t_bwd, n_ctx):
    return jnp.concatenate([t_fwd, seg_flip(t_bwd, n_ctx)], axis=0)

def merge_dirs(y, n_ctx):
    nb = y.shape[0] // 2
    return y[:nb] + seg_flip(y[nb:], n_ctx)

def grid_transpose(t, r, w):
    b, _, ch = t.shape
    return t.reshape(b, r, w, ch).transpose(0, 2, 1, 3).reshape(b, r * w, ch)

def centred_dwconv(x, w):
    k, ch = w.shape
    pad = (k - 1) // 2
    return lax.conv_general_dilated(x, w.astype(x.dtype)[:, None, :], window_strides=(1,),
                                    padding=[(pad, pad)], dimension_numbers=('NWC', 'WIO', 'NWC'),
                                    feature_group_count=ch)

def to_chunks(t):
    n, l, nh = t.shape[:3]
    t = t.reshape((n, l // CHUNK, CHUNK, nh) + t.shape[3:])
    return jnp.moveaxis(t, (1, 3), (0, 2))

def from_chunks(t):
    t = jnp.moveaxis(t, (0, 2), (1, 3))
    return t.reshape((t.shape[0], t.shape[1] * t.shape[2]) + t.shape[3:])

def mlstm_chunkwise(q, k, v, log_i, log_f):
    n, l, nh, dk = q.shape
    dv = v.shape[-1]
    incl = jnp.tril(jnp.ones((CHUNK, CHUNK), dtype=bool))
    qc, kc, vc = to_chunks(q), to_chunks(k * dk ** -0.5), to_chunks(v)
    li = to_chunks(log_i)
    bcum = jnp.cumsum(to_chunks(log_f), axis=-1)
    d_log = jnp.where(incl, bcum[..., :, None] - bcum[..., None, :] + li[..., None, :], -jnp.inf)
    m_intra = jnp.max(d_log, axis=-1)
    qk = jnp.einsum('znhtd,znhsd->znhts', qc, kc)

    def step(carry, xs):
        c_st, n_st, m_st = carry
        q_, k_, v_, li_, b_, dl_, mi_, qk_ = xs
        m_inter = b_ + m_st[..., None]
        m_t = jnp.maximum(m_inter, mi_)
        w_inter = jnp.exp(m_inter - m_t)
        w_intra = jnp.exp(dl_ - m_t[..., None]) * qk_
        num = w_inter[..., None] * jnp.einsum('nhtd,nhde->nhte', q_, c_st) + jnp.einsum('nhts,nhse->nhte', w_intra, v_)
        den = w_inter * jnp.einsum('nhtd,nhd->nht', q_, n_st) + jnp.sum(w_intra, axis=-1)
        h = num / jnp.maximum(jnp.abs(den), jnp.exp(-m_t))[..., None]
        m_new = m_t[..., -1]
        a = jnp.exp(b_[..., -1:] - b_ + li_ - m_new[..., None])
        ka = k_ * a[..., None]
        carry_decay = jnp.exp(b_[..., -1] + m_st - m_new)
        c_new = carry_decay[..., None, None] * c_st + jnp.einsum('nhsd,nhse->nhde', ka, v_)
        n_new = carry_decay[..., None] * n_st + jnp.sum(ka, axis=-2)
        return (c_new, n_new, m_new), h

    init = (jnp.zeros((n, nh, dk, dv), q.dtype), jnp.zeros((n, nh, dk), q.dtype), jnp.zeros((n, nh), q.dtype))
    _, h = lax.scan(step, init, (qc, kc, vc, li, bcum, d_log, m_intra, qk))
    return from_chunks(h)

def gated_delta_chunkwise(q, k, v, beta, g):
    n, l, nh, dk = q.shape
    dv = v.shape[-1]
    incl = jnp.tril(jnp.ones((CHUNK, CHUNK), dtype=bool))
    strict = jnp.tril(jnp.ones((CHUNK, CHUNK), dtype=bool), -1)
    qc, kc, vc = to_chunks(q * dk ** -0.5), to_chunks(k), to_chunks(v)
    bc = to_chunks(beta)
    gc = jnp.cumsum(to_chunks(g), axis=-1)
    decay = jnp.exp(jnp.where(incl, gc[..., :, None] - gc[..., None, :], -jnp.inf))
    kb = kc * bc[..., None]
    a_strict = jnp.where(strict, jnp.einsum('znhtd,znhsd->znhts', kb, kc) * decay, 0.0)
    tmat = jnp.eye(CHUNK, dtype=q.dtype) + a_strict
    u = lax.linalg.triangular_solve(tmat, vc * bc[..., None], left_side=True, lower=True, unit_diagonal=True)
    w = lax.linalg.triangular_solve(tmat, kb * jnp.exp(gc)[..., None], left_side=True, lower=True, unit_diagonal=True)
    att = jnp.einsum('znhtd,znhsd->znhts', qc, kc) * decay
    q_dec = qc * jnp.exp(gc)[..., None]
    k_dec = kc * jnp.exp(gc[..., -1:] - gc)[..., None]
    g_last = jnp.exp(gc[..., -1])

    def step(s, xs):
        u_, w_, att_, qd_, kd_, gl_ = xs
        v_new = u_ - jnp.einsum('nhtd,nhde->nhte', w_, s)
        o = jnp.einsum('nhtd,nhde->nhte', qd_, s) + jnp.einsum('nhts,nhse->nhte', att_, v_new)
        s_new = gl_[..., None, None] * s + jnp.einsum('nhsd,nhse->nhde', kd_, v_new)
        return s_new, o

    _, o = lax.scan(step, jnp.zeros((n, nh, dk, dv), q.dtype), (u, w, att, q_dec, k_dec, g_last))
    return from_chunks(o)

def gla_chunkwise(q, k, v, g):
    n, l, nh, dk = q.shape
    dv = v.shape[-1]
    incl = jnp.tril(jnp.ones((CHUNK, CHUNK), dtype=bool))
    qc, kc, vc = to_chunks(q), to_chunks(k), to_chunks(v)
    gc = jnp.cumsum(to_chunks(g), axis=-2)
    q_dec = qc * jnp.exp(gc)
    k_dec = kc * jnp.exp(gc[..., -1:, :] - gc)
    g_last = jnp.exp(gc[..., -1, :])

    def step(s, xs):
        q_, k_, v_, gc_, qd_, kd_, gl_ = xs
        rel = jnp.exp(jnp.where(incl[..., None], gc_[..., :, None, :] - gc_[..., None, :, :], -jnp.inf))
        att = jnp.einsum('nhtd,nhsd,nhtsd->nhts', q_, k_, rel)
        o = jnp.einsum('nhtd,nhde->nhte', qd_, s) + jnp.einsum('nhts,nhse->nhte', att, v_)
        s_new = gl_[..., :, None] * s + jnp.einsum('nhsd,nhse->nhde', kd_, v_)
        return s_new, o

    _, o = lax.scan(step, jnp.zeros((n, nh, dk, dv), q.dtype), (qc, kc, vc, gc, q_dec, k_dec, g_last))
    return from_chunks(o)

def mixer_ab(u, n_ctx, w_in, i_bias, f_bias, conv_w, a_log, dt_bias, norm_a, norm_b):
    b, l, _ = u.shape
    p = (u @ w_in).astype(jnp.float32)
    qa, ka, va, oa, qb, kb, vb, zb, ia, fa, bb, ab = split_cols(p, AB_SPLITS)
    heads_a = lambda t: t.reshape(b, l, H_A, DH_A)
    log_i = (ia + i_bias.astype(jnp.float32).reshape(-1)).reshape(b, l, 2, H_A)
    log_f = jax.nn.log_sigmoid(fa + f_bias.astype(jnp.float32).reshape(-1)).reshape(b, l, 2, H_A)
    qa, ka, va = heads_a(qa), heads_a(ka), heads_a(va)
    h_a = merge_dirs(mlstm_chunkwise(stack_dirs(qa, qa, n_ctx), stack_dirs(ka, ka, n_ctx), stack_dirs(va, va, n_ctx),
                                     stack_dirs(log_i[:, :, 0], log_i[:, :, 1], n_ctx),
                                     stack_dirs(log_f[:, :, 0], log_f[:, :, 1], n_ctx)), n_ctx)
    y_a = head_rms_norm(h_a, norm_a) * jax.nn.sigmoid(oa)
    qkv = jnp.concatenate([qb, kb, vb], axis=-1)
    qkv = jax.nn.silu(jnp.concatenate([centred_dwconv(qkv[:, :n_ctx], conv_w),
                                       centred_dwconv(qkv[:, n_ctx:], conv_w)], axis=1))
    qb, kb, vb = jnp.split(qkv, 3, axis=-1)
    heads_b = lambda t: t.reshape(b, l, H_B, DH_B)
    qb, kb, vb = l2_normalize(heads_b(qb)), l2_normalize(heads_b(kb)), heads_b(vb)
    beta = jax.nn.sigmoid(bb).reshape(b, l, 2, H_B)
    g = (-jnp.exp(a_log.astype(jnp.float32).reshape(-1))
         * jax.nn.softplus(ab + dt_bias.astype(jnp.float32).reshape(-1))).reshape(b, l, 2, H_B)
    o_b = merge_dirs(gated_delta_chunkwise(stack_dirs(qb, qb, n_ctx), stack_dirs(kb, kb, n_ctx), stack_dirs(vb, vb, n_ctx),
                                           stack_dirs(beta[:, :, 0], beta[:, :, 1], n_ctx),
                                           stack_dirs(g[:, :, 0], g[:, :, 1], n_ctx)), n_ctx)
    y_b = head_rms_norm(o_b, norm_b) * jax.nn.silu(zb)
    return jnp.concatenate([y_a, y_b], axis=-1)

def mixer_c(u, n_ctx, rows, column_major, w_in, f_bias, lb, norm_c):
    b, l, _ = u.shape
    p = (u @ w_in).astype(jnp.float32)
    if column_major:
        p = jnp.concatenate([p[:, :n_ctx], grid_transpose(p[:, n_ctx:], rows, GRID_W)], axis=1)
    q, zf, zb, vi, og = split_cols(p, C_SPLITS)
    heads_k = lambda t: t.reshape(b, l, H_C, DK_C)
    heads_v = lambda t: t.reshape(b, l, H_C, DV_C)
    fb = f_bias.astype(jnp.float32)

    def gates(z, lb_d):
        f = lb_d + (1.0 - lb_d) * jax.nn.sigmoid(z)
        key = (1.0 - lb_d) * jax.nn.sigmoid(-z)
        return heads_k(jnp.log(f)), heads_k(key)

    lf_f, k_f = gates(zf + fb[0], lb[0])
    lf_b, k_b = gates(zb + fb[1], lb[1])
    q = heads_k(jax.nn.silu(q))
    vi = heads_v(vi)
    o = merge_dirs(gla_chunkwise(stack_dirs(q, q, n_ctx), stack_dirs(k_f, k_b, n_ctx),
                                 stack_dirs(vi, vi, n_ctx), stack_dirs(lf_f, lf_b, n_ctx)), n_ctx)
    y = head_rms_norm(o, norm_c) * jax.nn.silu(og)
    if column_major:
        y = jnp.concatenate([y[:, :n_ctx], grid_transpose(y[:, n_ctx:], GRID_W, rows)], axis=1)
    return y

def moe_ffn(h, w_router, router_bias, w1, w3, w2):
    t = h.shape[0]
    scores = jax.nn.sigmoid(jnp.dot(h.astype(jnp.float32), w_router.astype(jnp.float32)))
    sel = scores + router_bias.astype(jnp.float32)
    group_score = jnp.sum(lax.top_k(sel.reshape(t, N_GROUPS, EXPERTS_PER_GROUP), GROUP_SCORE_K)[0], axis=-1)
    best_group = jnp.argmax(group_score, axis=-1)
    expert_group = jnp.arange(N_EXPERTS) // EXPERTS_PER_GROUP
    sel = jnp.where(expert_group[None, :] == best_group[:, None], sel, -jnp.inf)
    _, idx = lax.top_k(sel, TOP_K)
    wts = jnp.take_along_axis(scores, idx, axis=-1)
    wts = wts / jnp.sum(wts, axis=-1, keepdims=True)
    gate = jnp.sum(jax.nn.one_hot(idx, N_EXPERTS, dtype=jnp.float32) * wts[..., None], axis=1)
    out = jnp.zeros(h.shape, jnp.float32)
    for e in range(N_EXPERTS):
        a = jax.nn.silu(h @ w1[e]) * (h @ w3[e])
        out = out + gate[:, e:e + 1] * (a @ w2[e]).astype(jnp.float32)
    return out.astype(h.dtype)

def setup_inputs(seed: int = 0) -> dict:
    key = jax.random.key(seed)
    ks = iter(jax.random.split(key, 32))
    f32 = jnp.float32
    nrm = lambda shape, scale: jax.random.normal(next(ks), shape, f32) * scale
    x = nrm((BATCH, SEQ, D_MODEL), 1.0)
    c = nrm((BATCH, D_MODEL), 1.0)
    ctx = nrm((BATCH, CTX_LEN, D_MODEL), 1.0)
    c_ctx = nrm((D_MODEL,), 1.0)
    w_mod = nrm((DEPTH, D_MODEL, 6 * D_MODEL), 0.5 * D_MODEL ** -0.5)
    b_mod = nrm((DEPTH, 6 * D_MODEL), 0.01)
    norm_mix = 1.0 + nrm((DEPTH, D_MODEL), 0.05)
    norm_ffn = 1.0 + nrm((DEPTH, D_MODEL), 0.05)
    norm_final = 1.0 + nrm((D_MODEL,), 0.05)
    ab_w_in = nrm((N_EVEN, D_MODEL, P_AB), D_MODEL ** -0.5)
    ab_i_bias = nrm((N_EVEN, 2, H_A), 0.1)
    ab_f_bias = jnp.linspace(3.0, 6.0, H_A, dtype=f32) + nrm((N_EVEN, 2, H_A), 0.1)
    ab_conv = nrm((N_EVEN, CONV_K, 3 * W_B), CONV_K ** -0.5)
    ab_a_log = jnp.log(jax.random.uniform(next(ks), (N_EVEN, 2, H_B), f32, 1.0, 16.0))
    dt = jnp.exp(jax.random.uniform(next(ks), (N_EVEN, 2, H_B), f32, math.log(1e-3), math.log(1e-1)))
    ab_dt_bias = dt + jnp.log(-jnp.expm1(-dt))
    ab_norm_a = 1.0 + nrm((N_EVEN, W_A), 0.05)
    ab_norm_b = 1.0 + nrm((N_EVEN, W_B), 0.05)
    ab_w_out = nrm((N_EVEN, W_A + W_B, D_MODEL), (W_A + W_B) ** -0.5)
    c_w_in = nrm((N_ODD, D_MODEL, P_C), D_MODEL ** -0.5)
    c_f_bias = nrm((N_ODD, 2, C_K), 0.1)
    c_lb_raw = nrm((N_ODD, 2, C_K), 0.5)
    c_norm = 1.0 + nrm((N_ODD, C_V), 0.05)
    c_w_out = nrm((N_ODD, C_V, D_MODEL), C_V ** -0.5)
    w_router = nrm((D_MODEL, N_EXPERTS), D_MODEL ** -0.5)
    router_bias = nrm((N_EXPERTS,), 0.01)
    w1 = nrm((DEPTH, N_EXPERTS, D_MODEL, D_FF_EXPERT), D_MODEL ** -0.5)
    w3 = nrm((DEPTH, N_EXPERTS, D_MODEL, D_FF_EXPERT), D_MODEL ** -0.5)
    w2 = nrm((DEPTH, N_EXPERTS, D_FF_EXPERT, D_MODEL), D_FF_EXPERT ** -0.5)
    return {'x': x, 'c': c, 'ctx': ctx, 'c_ctx': c_ctx, 'w_mod': w_mod, 'b_mod': b_mod,
            'norm_mix': norm_mix, 'norm_ffn': norm_ffn, 'norm_final': norm_final,
            'ab_w_in': ab_w_in, 'ab_i_bias': ab_i_bias, 'ab_f_bias': ab_f_bias, 'ab_conv': ab_conv,
            'ab_a_log': ab_a_log, 'ab_dt_bias': ab_dt_bias, 'ab_norm_a': ab_norm_a, 'ab_norm_b': ab_norm_b,
            'ab_w_out': ab_w_out, 'c_w_in': c_w_in, 'c_f_bias': c_f_bias, 'c_lb_raw': c_lb_raw,
            'c_norm': c_norm, 'c_w_out': c_w_out, 'w_router': w_router, 'router_bias': router_bias,
            'w1': w1, 'w3': w3, 'w2': w2}

def reference(x, c, ctx, c_ctx, w_mod, b_mod, norm_mix, norm_ffn, norm_final,
              ab_w_in, ab_i_bias, ab_f_bias, ab_conv, ab_a_log, ab_dt_bias, ab_norm_a, ab_norm_b, ab_w_out,
              c_w_in, c_f_bias, c_lb_raw, c_norm, c_w_out, w_router, router_bias, w1, w3, w2):
    bsz, seq, d = x.shape
    n_ctx = ctx.shape[1]
    rows = seq // GRID_W
    lb_p = jax.nn.softmax(c_lb_raw.astype(jnp.float32), axis=0)
    lb_all = jnp.cumsum(lb_p, axis=0) - lb_p[0:1]
    silu_c = jax.nn.silu(c)
    silu_cc = jax.nn.silu(c_ctx)
    lat, cx = x, ctx
    for layer in range(DEPTH):
        last = layer == DEPTH - 1
        sh1, sc1, g1, sh2, sc2, g2 = jnp.split((silu_c @ w_mod[layer] + b_mod[layer])[:, None, :], 6, axis=-1)
        sh1c, sc1c, g1c, sh2c, sc2c, g2c = jnp.split(silu_cc @ w_mod[layer] + b_mod[layer], 6, axis=-1)
        u = jnp.concatenate([rms_norm(cx, norm_mix[layer]) * (1 + sc1c) + sh1c,
                             rms_norm(lat, norm_mix[layer]) * (1 + sc1) + sh1], axis=1)
        j = layer // 2
        if layer % 2 == 0:
            feats = mixer_ab(u, n_ctx, ab_w_in[j], ab_i_bias[j], ab_f_bias[j], ab_conv[j], ab_a_log[j],
                             ab_dt_bias[j], ab_norm_a[j], ab_norm_b[j])
            w_out = ab_w_out[j]
        else:
            feats = mixer_c(u, n_ctx, rows, j % 2 == 1, c_w_in[j], c_f_bias[j], lb_all[j], c_norm[j])
            w_out = c_w_out[j]
        feats = feats.astype(x.dtype)
        lat = lat + g1 * (feats[:, n_ctx:] @ w_out)
        hl = rms_norm(lat, norm_ffn[layer]) * (1 + sc2) + sh2
        if last:
            lat = lat + g2 * moe_ffn(hl.reshape(-1, d), w_router, router_bias, w1[layer], w3[layer],
                                     w2[layer]).reshape(bsz, seq, d)
        else:
            cx = cx + g1c * (feats[:, :n_ctx] @ w_out)
            hc = rms_norm(cx, norm_ffn[layer]) * (1 + sc2c) + sh2c
            y = moe_ffn(jnp.concatenate([hc, hl], axis=1).reshape(-1, d), w_router, router_bias,
                        w1[layer], w3[layer], w2[layer]).reshape(bsz, n_ctx + seq, d)
            cx = cx + g2c * y[:, :n_ctx]
            lat = lat + g2 * y[:, n_ctx:]
    return rms_norm(lat, norm_final)


_drawn_inputs = setup_inputs


def setup_inputs(seed=0):
    import zlib

    import numpy as np

    out = dict(_drawn_inputs(seed))
    spreads = {}
    factors = {'ab_i_bias': 35.971,
     'ab_norm_a': 3.666,
     'c_f_bias': 39.331,
     'ab_norm_b': 4.283,
     'c_norm': 3.382}
    for name, (base, spread) in spreads.items():
        noise = np.random.default_rng([zlib.crc32(name.encode()), seed]).standard_normal(out[name].shape)
        drawn = base * np.exp(spread * noise) if base else spread * noise
        out[name] = jnp.asarray(drawn.astype(out[name].dtype))
    for name, factor in factors.items():
        out[name] = (out[name] * factor).astype(out[name].dtype)
    return out
```

```python
from contextlib import ExitStack

import concourse.bass as bass
from concourse import mybir

F32 = mybir.dt.float32
I32 = mybir.dt.int32
ALU = mybir.AluOpType
ACT = mybir.ActivationFunctionType
AX = mybir.AxisListType
ds = bass.ds

P = 128
D = 1024
J = D // P
N_CTX = 256
N_LAT = 256
T = N_CTX + N_LAT
C = T // P
C_CTX = N_CTX // P
H_A = 4
H_C = 8
CONV = 5
E = 16
GROUPS = 4
F = 512
FT = F // P
WORK = 12334
EPS = 1e-6
FAR = 1e30
N_PARAMS = 8
N_TURNED = 16
PASSES = 24
RING = 6
ORDER = ([0, 1, 2, 3], [1, 0, 3, 2])
IN_GROUPS = ([0, 1, 2, 3, 7, 4, 5, 6], [0, 2, 4, 6, 8, 1, 3, 5, 7, 9])
LEVELS = [1, 2, 4, 8, 16, 32, 64]
GATE_I, GATE_F, GATE_B, GATE_A = range(4)
Q_G, Q_WI, Q_EM, Q_AS, Q_NGC, Q_EGC, Q_NEGC, Q_EKD, Q_BETA, Q_BKD = range(10)
ROWQ = 8


def hybrid_block(nc, x, c, ctx, c_ctx, w_mod, b_mod, norm_mix, norm_ffn, norm_final,
                 ab_w_in, ab_i_bias, ab_f_bias, ab_conv, ab_a_log, ab_dt_bias, ab_norm_a, ab_norm_b,
                 ab_w_out, c_w_in, c_f_bias, c_lb_raw, c_norm, c_w_out, w_router, router_bias,
                 w1, w3, w2, out):
    with ExitStack() as stack:
        def sb(name, shape, dt=F32):
            return stack.enter_context(nc.sbuf_tensor(name, shape, dt))

        def sem(name):
            return stack.enter_context(nc.semaphore(name))

        bank = [stack.enter_context(nc.psum_tensor(f"bank{i}", [P, 512], F32)) for i in range(8)]

        ring = [sb(f"ring{i}", [P, 4096]) for i in range(RING)]
        xT = sb("xT", [P, J, T])
        uT = sb("uT", [P, J, T])
        featsT = sb("featsT", [P, 8, T])
        ident = sb("ident", [P, P])
        ones = sb("ones", [P, P])
        ahead = sb("ahead", [P, 2, P])
        level = sb("level", [P, 2, len(LEVELS), P])
        slot_of = sb("slot_of", [P, C, 2], I32)
        craw = sb("craw", [P, 2, J])
        csil = sb("csil", [P, J, 2])
        modv = sb("modv", [P, 2, 6, 2, J])
        bmod = sb("bmod", [P, 2, 6, J])
        nmix = sb("nmix", [P, 2, J])
        nffn = sb("nffn", [P, 2, J])
        nfin = sb("nfin", [P, J])
        coef = sb("coef", [P, 2, J])
        rstd = sb("rstd", [P, T])
        gbias = sb("gbias", [H_A, 4, 2])
        ends = sb("ends", [H_A, 4, 2, C])
        cols = sb("cols", [P, 10 * 32])
        taps_w = sb("taps_w", [P, CONV, 12])
        gain_h = sb("gain_h", [P, 8])
        gain_c = sb("gain_c", [P, 8])
        ssq = sb("ssq", [P, 8 * C])
        small = sb("small", [P, 48])
        epsv = sb("epsv", [P, 1])
        forget = sb("forget", [P, 4, 2, H_C])
        w_r = sb("w_r", [P, J, E])
        bias_r = sb("bias_r", [P, E])
        steps = sb("steps", [1, 2, PASSES + 4], I32)
        work = sb("work", [P, WORK])

        def area(start, *shape):
            n = 1
            for s in shape:
                n *= s
            flat = work[:, start:start + n]
            names = "abcd"[:len(shape)]
            if len(shape) == 1:
                return flat
            return flat.rearrange("p (%s) -> p %s" % (" ".join(names), " ".join(names)),
                                  **{k: v for k, v in zip(names, shape)})

        modrow = work[0:2, 0:6 * D]
        modrow_now = rstd[0:2, :]
        gate = featsT[:, :, :].rearrange("p h (c e) -> p h c e", c=C)
        qT = area(0, H_A, T)
        kT = area(2048, H_A, T)
        va = area(4096, C, H_A, P + 1)
        vb = area(4096, C, H_A, P)
        bc = area(6160, 2, 1032)
        qh = area(8224, T)
        kh = area(8736, T)
        w_gate = featsT[:, 0, 0:J * 32].rearrange("p (k n) -> p k n", k=J)
        grow = rstd[0:32, :]
        grow4 = area(8224, 4, 2, T)[0:H_A]
        rows_low = featsT[0:H_A, :, :].rearrange("h (k d) t -> h k d t", d=2)
        rows_high = area(4096, 4, 2, T)[0:H_A]

        def row(kind):
            return rows_low[:, kind, :, :] if kind < 4 else rows_high[:, kind - 4, :, :]

        ka = area(9248, 6, P)
        cell = area(10016, 2, 3, P + 1)
        num = area(10790, 8, P + 1)
        hsum = area(11822, C, P)
        raw = area(6160, 2, 2, 260)
        taps = area(7200, 2, 512)
        turned_v = area(9248, 2, 512)
        ktok = area(9248, C, P)
        lower = area(9760, 2, C, P)
        state_b = area(10784, 2, P)
        z_b = area(11040, 2, P)
        vn_b = area(11296, 2, P)
        vd_b = area(11552, 2, P)
        osum = area(11808, C, P)
        u_flat = uT[:, :, :].rearrange("p a b -> p (a b)")
        inv = u_flat[:, 0:2048].rearrange("p (d x c e) -> p d x c e", d=2, x=2, c=C)
        masked = u_flat[:, 2048:3072].rearrange("p (d c e) -> p d c e", d=2, c=C)
        half = u_flat[:, 3072:4096].rearrange("p (d c e) -> p d c e", d=2, c=C)
        x_in = uT[:, :, :].rearrange("p a b -> p (a b)").rearrange("p (a b) -> p a b", a=C)

        q1 = area(0, 4, N_LAT)
        z1 = area(1024, 2, 4, T)
        v1 = area(5120, C, 4, P)
        decay = area(7168, 2, T)
        ks = area(8192, 2, T)
        qp = area(9216, 2, N_LAT)
        tot = area(9728, 2, T)
        att1 = area(10752, 2, 2, P)
        kd1 = area(7168, 2, 3, P)
        state1 = area(11264, 2, 3, P)
        o1 = area(12032, 2, P)
        out_sb = area(0, 2, D)

        h_tok = featsT[:, :, :].rearrange("p h t -> p (h t)").rearrange("p (c j e) -> p c j e", c=C, j=J)
        h_row = featsT[:, :, :].rearrange("p h t -> p (h t)").rearrange("p (c n) -> p c n", c=C)
        back = (h_row, uT[:, :, :].rearrange("p a b -> p (a b)").rearrange("p (c n) -> p c n", c=C))
        he = area(0, 2, J, P)
        xs = area(2048, 2, D)
        act_e = area(5120, FT, P)
        silu_e = area(5632, FT, P)
        ye = area(6144, 2, D)
        table = area(8440, PASSES + 2)
        r_rows = area(8500, T)[0:E]
        scores = area(9012, C, E)
        sel = area(9076, C, E)
        first = area(9140, C, E)
        second = area(9204, C, E)
        tmp = area(9268, C, E)
        tmp2 = area(9332, C, E)
        taken = area(9396, C, E)
        rank = area(9460, C, E)
        pairs = area(9524, C * GROUPS, 6)
        g_score = area(9620, C, GROUPS)
        g_pick = area(9636, C, GROUPS)
        top = area(9652, C)
        low = area(9656, C)
        count = area(9660, E)
        n_pass = area(9676, E)
        upto_e = area(9692, E)
        start_e = area(9708, E)
        pos = area(9724, C, 2)
        wts = area(9732, C, 2)
        total = area(9740, C)
        ids_f = area(10170, (PASSES + 2), E)
        before = area(10600, P)
        iota = area(10728, P)

        slot_in = [sem(f"slot_in{i}") for i in range(RING)]
        x_loaded = sem("x_loaded")
        c_loaded = sem("c_loaded")
        ident_ready = sem("ident_ready")
        params_loaded = sem("params_loaded")
        const_step = sem("const_step")
        consts_ready = sem("consts_ready")
        x_turned = sem("x_turned")
        turned_loaded = sem("turned_loaded")
        group_taken = sem("group_taken")
        taps_step = sem("taps_step")
        conv_done = sem("conv_done")
        gates_summed = sem("gates_summed")
        gates_copied = sem("gates_copied")
        gates_moved = sem("gates_moved")
        row_dve = sem("row_dve")
        row_act = sem("row_act")
        rows_ready = sem("rows_ready")
        rows_stored = sem("rows_stored")
        cols_turned = sem("cols_turned")
        cols_act = sem("cols_act")
        cols_dve = sem("cols_dve")
        va_ones = sem("va_ones")
        qk_staged = sem("qk_staged")
        bc_loaded = [sem(f"bc_loaded{i}") for i in range(2)]
        scores_ready = sem("scores_ready")
        kh_turned = sem("kh_turned")
        ka_ready = sem("ka_ready")
        arg_ready = sem("arg_ready")
        exp_ready = sem("exp_ready")
        w_ready = sem("w_ready")
        update_ready = sem("update_ready")
        cell_step = sem("cell_step")
        intra_ready = sem("intra_ready")
        inter_ready = sem("inter_ready")
        intra_copied = sem("intra_copied")
        joined = sem("joined")
        head_step = sem("head_step")
        raw_zeroed = sem("raw_zeroed")
        silu_done = sem("silu_done")
        v_turned = sem("v_turned")
        v_taken = sem("v_taken")
        qk_squared = sem("qk_squared")
        qk_summed = sem("qk_summed")
        qk_root = sem("qk_root")
        qk_step = sem("qk_step")
        qk_normed = sem("qk_normed")
        ktok_ready = sem("ktok_ready")
        lower_ready = sem("lower_ready")
        att_ready = sem("att_ready")
        mask_ready = sem("mask_ready")
        x0_turned = sem("x0_turned")
        x0_ready = sem("x0_ready")
        bx_ready = sem("bx_ready")
        bx_copied = sem("bx_copied")
        xbx_ready = sem("xbx_ready")
        inv_ready = sem("inv_ready")
        carried_ready = sem("carried_ready")
        z_ready = sem("z_ready")
        xz_ready = sem("xz_ready")
        v_ready = sem("v_ready")
        outer_ready = sem("outer_ready")
        state_ready = sem("state_ready")
        o_step = sem("o_step")
        ms_ready = sem("ms_ready")
        ms_root = sem("ms_root")
        y_step = sem("y_step")
        y_ready = sem("y_ready")
        y_turned = sem("y_turned")
        feats_ready = sem("feats_ready")
        out_summed = sem("out_summed")
        x_updated = sem("x_updated")
        forget_step = sem("forget_step")
        forget_act = sem("forget_act")
        sig_ready = sem("sig_ready")
        f_ready = sem("f_ready")
        tot_step = sem("tot_step")
        level_ready = sem("level_ready")
        qp_updated = sem("qp_updated")
        ks_updated = sem("ks_updated")
        cp_done = sem("cp_done")
        att1_zeroed = sem("att1_zeroed")
        kd_turned = sem("kd_turned")
        kd_ready = sem("kd_ready")
        update1_ready = sem("update1_ready")
        state1_step = sem("state1_step")
        o1_ready = sem("o1_ready")
        o1_copied = sem("o1_copied")
        out_turned = sem("out_turned")
        out_copied = sem("out_copied")
        out_stored = sem("out_stored")
        head_done = sem("head_done")
        xT_act = sem("xT_act")
        xT_dve = sem("xT_dve")
        csil_ready = sem("csil_ready")
        mod_summed = sem("mod_summed")
        row_copied = sem("row_copied")
        mod_spread = sem("mod_spread")
        tile_summed = sem("tile_summed")
        mod_ready = sem("mod_ready")
        coef_step = sem("coef_step")
        coef_ready = sem("coef_ready")
        sq_ready = sem("sq_ready")
        ssq_ready = sem("ssq_ready")
        root_ready = sem("root_ready")
        rstd_step = sem("rstd_step")
        xn_ready = sem("xn_ready")
        u_ready = sem("u_ready")

        expert_in = [sem(f"expert_in{i}") for i in range(RING)]
        logits_summed = sem("logits_summed")
        scored = sem("scored")
        logits_copied = sem("logits_copied")
        logits_turned = sem("logits_turned")
        route_step = sem("route_step")
        chosen = sem("chosen")
        counted = sem("counted")
        tabled = sem("tabled")
        tok_turned = sem("tok_turned")
        tok_copied = sem("tok_copied")
        iota_ready = sem("iota_ready")
        pass_filled = sem("pass_filled")
        tok_stored = sem("tok_stored")
        xs_in = [sem(f"xs_in{i}") for i in range(2)]
        xs_turned = sem("xs_turned")
        ye_stored = sem("ye_stored")
        back_in = [sem(f"back_in{i}") for i in range(C)]
        weighed = sem("weighed")
        both_ready = sem("both_ready")
        both_turned = sem("both_turned")
        he_copied = sem("he_copied")
        up_summed = sem("up_summed")
        silu_ready = sem("silu_ready")
        gated = sem("gated")
        down_summed = sem("down_summed")
        ye_copied = sem("ye_copied")

        def by_feature(w):
            return w.rearrange("(p k) n -> p k n", k=J)

        slots = []
        mods = [[("mod", layer, g, 0, by_feature(w_mod[layer])[:, :, 512 * g:512 * g + 512]) for g in range(12)]
                for layer in range(2)]
        slots += mods[0]
        for layer in range(2):
            wi = by_feature((ab_w_in if layer == 0 else c_w_in)[0])
            groups = IN_GROUPS[layer]
            slots += [("in", layer, g, 0, wi[:, :, 512 * g:512 * g + 512]) for g in groups]
            if layer == 0:
                slots += mods[1]
            wo = (ab_w_out if layer == 0 else c_w_out)[0].rearrange("(h p) n -> p h n", p=P)
            slots += [("out", layer, h, 0, wo[:, 4 * h:4 * h + 4, :]) for h in range(2)]
        slot_at = {s[:4]: n for n, s in reversed(list(enumerate(slots)))}

        def slot(n, k):
            return ring[n % RING][:, :].rearrange("p (k m) -> p k m", k=k)

        def slot_arrived(eng, n, turn=0):
            eng.wait_ge(slot_in[n % RING], 16 * (n // RING + 1) + 16 * turn)

        def shift(n):
            return modv[:, n // 2, 0 if n % 2 == 0 else 3, :, :]

        def slot_free(eng, n):
            kind, layer, g = slots[n][:3]
            if kind == "mod":
                eng.wait_ge(mod_summed, 12 * layer + g + 1)
            elif kind == "in" and layer == 0:
                eng.wait_ge(tile_summed, 4 * (IN_GROUPS[0].index(g) + 1))
            elif kind == "in":
                k = IN_GROUPS[1].index(g)
                eng.wait_ge(tile_summed, 32 + 18 * (k // 5) + (4, 8, 12, 16, 18)[k % 5])
            elif kind == "out":
                eng.wait_ge(out_summed, 8 * layer + 8)

        pass_in = nc.dram_tensor("pass_in", [P * PASSES, D], F32, kind="Internal").ap()
        pass_out = nc.dram_tensor("pass_out", [P * PASSES, D], F32, kind="Internal").ap()
        row_dram = nc.dram_tensor("row_dram", [2, H_A, 1032], F32, kind="Internal").ap()

        def col(q, d, ch, h):
            return cols[:, ds(32 * q + 16 * d + 4 * ch + h, 1)]

        def tot_at(l):
            return T - (T >> (l - 1))

        def by_block(t, l):
            return t.rearrange("p (j two r) -> p j two r", two=2, r=1 << l)

        def totals_of(d, l, lat=False):
            t = decay[:, d, :] if l == 0 else tot[:, d, tot_at(l):tot_at(l) + (T >> l)]
            t = t.rearrange("p (j two) -> p j two", two=2)
            return t[:, N_CTX >> (l + 1):, :] if lat else t

        expert_slots = [[(slot_at["in", 1, 0, 0] + 3 * half + k) % RING for k in range(3)] for half in range(2)]
        assert slot_at["in", 1, 0, 0] % RING == len(slots) % RING

        def seen(layer):
            return C_CTX * layer, N_CTX * layer

        def pairs_of(eng, layer):
            lo, hi = E // 2, PASSES // 2
            end = eng.value_load(steps[0:1, layer, PASSES + 2:PASSES + 3], min_val=lo * (layer + 1), max_val=hi * (layer + 1))
            if layer == 0:
                return 0, end
            return eng.value_load(steps[0:1, 0, PASSES + 2:PASSES + 3], min_val=lo, max_val=hi), end

        def within(eng, i, first):
            if isinstance(first, int):
                return i
            return eng.snap(nc.s_assert_within(i - 2 * first, 0, PASSES - 1,
                                               skip_runtime_bounds_check_because="a layer has no more than PASSES passes"))

        block = stack.enter_context(nc.Block())

        @block.sync
        def _(sp):
            for half, src in ((0, ctx), (1, x)):
                sp.dma_start(x_in[:, 2 * half:2 * half + 2, :],
                             src[0].rearrange("(a p) d -> p a d", p=P)).then_inc(x_loaded, 16)

            def load(n):
                if n >= RING:
                    slot_free(sp, n - RING)
                sp.dma_start(slot(n, slots[n][4].shape[1]), slots[n][4]).then_inc(slot_in[n % RING], 16)

            def fill_passes():
                sp.wait_ge(bc_loaded[1], 16 * 3)
                for rows in (pass_in, pass_out):
                    for n in range(PASSES // 4):
                        sp.dma_start(rows[4 * P * n:4 * P * n + 4 * P, :].rearrange("(p a) d -> p (a d)", p=P),
                                     xT[:, :, :].rearrange("p j t -> p (j t)")).then_inc(pass_filled, 16)

            for n in range(slot_at["in", 1, 0, 0]):
                if n == slot_at["mod", 1, 0, 0] + RING:
                    fill_passes()
                load(n)
            def load_expert(layer, e, half, what):
                w, k = ((w1, J), (w3, J), (w2, FT))[what]
                r = expert_slots[half][what]
                if isinstance(e, int):
                    src = w[layer, e]
                else:
                    src = w[layer, ds(e, 1)].rearrange("o d f -> (o d) f")
                sp.dma_start(ring[r][:, :], src.rearrange("(p k) f -> p (k f)", k=k)).then_inc(expert_in[r], 16)

            def experts(layer, last_slot):
                for what in range(3):
                    slot_free(sp, last_slot - RING + 1 + what)
                    load_expert(layer, 0, 0, what)
                for what in range(3):
                    slot_free(sp, last_slot - RING + 4 + what)
                sp.wait_ge(tabled, layer + 1)
                sp.wait_ge(tok_stored, 16 * (8 + 4 * layer))
                for half in range(2):
                    sp.dma_start(xs[:, half, :], pass_in[P * half:P * half + P, :]).then_inc(xs_in[half], 16)
                e = sp.value_load(steps[0:1, layer, 1:2], min_val=0, max_val=E - 1)
                for what in range(3):
                    load_expert(layer, e, 1, what)
                first, end = pairs_of(sp, layer)
                with sp.Fori(first + 1, end) as m:
                    for half in range(2):
                        e = sp.value_load(steps[0:1, layer, ds(within(sp, 2 * m + half, first), 1)], min_val=0, max_val=E - 1)
                        sp.wait_ge(xs_turned, 2 * m + half - 1 + layer)
                        sp.dma_start(xs[:, half, :], pass_in[ds(within(sp, 2 * m + half, first) * P, P), :]).then_inc(
                            xs_in[half], 16)
                        sp.wait_ge(up_summed, 2 * m + half - 1)
                        for what in range(2):
                            load_expert(layer, e, half, what)
                        sp.wait_ge(down_summed, 2 * m + half - 1)
                        load_expert(layer, e, half, 2)
                sp.wait_ge(xs_turned, 2 * end + layer)
                sp.dma_start(xs[:, 0, :], pass_in[0:P, :]).then_inc(xs_in[0], 16)

            experts(0, 33)
            sp.wait_ge(x_updated, 9)
            for n in range(34, 46):
                if n - RING >= 34:
                    slot_free(sp, n - RING)
                sp.dma_start(slot(n, slots[n][4].shape[1]), slots[n][4]).then_inc(slot_in[n % RING], 16)
            experts(1, 45)
            for ch in range(2):
                sp.wait_ge(out_copied, 2 * ch + 2)
                sp.dma_start(out[0, P * ch:P * ch + P, :], out_sb[:, ch, :]).then_inc(out_stored, 16)
            sp.wait_ge(out_stored, 32)

        @block.gpsimd
        def _(pool):
            n_step = [0]

            def step(ins):
                ins.then_inc(const_step, 1)
                n_step[0] += 1

            def after_step():
                pool.wait_ge(const_step, n_step[0])

            step(pool.memset(ident[:, :], 0.0))
            after_step()
            pool.affine_select(out=ident[:, :], in_=ident[:, :], compare_op=ALU.not_equal, fill=1.0,
                               base=0, pattern=[[-1, P]], channel_multiplier=1).then_inc(ident_ready, 1)
            pool.memset(ones[:, :], 1.0)
            step(pool.memset(ahead[:, :, :], 0.0))
            step(pool.memset(level[:, :, :, :], 0.0))
            after_step()
            for b in LEVELS:
                v = level[:, :, LEVELS.index(b), :].rearrange("p d (j h r) -> p d j h r", h=2, r=b)
                step(pool.memset(v[:, 0, :, 1, :], 1.0))
                step(pool.memset(v[:, 1, :, 0, :], 1.0))
            step(pool.affine_select(out=ahead[:, 0, :], in_=ahead[:, 0, :], compare_op=ALU.is_ge, fill=-FAR,
                                    base=0, pattern=[[1, P]], channel_multiplier=-1))
            step(pool.affine_select(out=ahead[:, 1, :], in_=ahead[:, 1, :], compare_op=ALU.is_ge, fill=-FAR,
                                    base=0, pattern=[[-1, P]], channel_multiplier=1))
            after_step()
            for b in LEVELS:
                n = P // (2 * b)
                v = level[:, :, LEVELS.index(b), :].rearrange("p d (j h r) -> p d j h r", h=2, r=b)
                for d, lo in ((0, 0), (1, b)):
                    part = v[:, d, :, 1 - d, :]
                    step(pool.affine_select(out=part, in_=part, compare_op=ALU.is_ge, fill=0.0, base=-lo,
                                            pattern=[[-2 * b, n], [0, b]], channel_multiplier=1))
            after_step()
            for b in LEVELS:
                n = P // (2 * b)
                v = level[:, :, LEVELS.index(b), :].rearrange("p d (j h r) -> p d j h r", h=2, r=b)
                for d, lo in ((0, 0), (1, b)):
                    part = v[:, d, :, 1 - d, :]
                    step(pool.affine_select(out=part, in_=part, compare_op=ALU.is_ge, fill=0.0, base=lo + b - 1,
                                            pattern=[[2 * b, n], [0, b]], channel_multiplier=-1))
            after_step()
            pool.memset(epsv[:, :], EPS)
            pool.memset(ssq[:, :], 0.0).then_inc(consts_ready, 1)

            def stage_heads(base, free, free_per_head):
                with pool.Fori(0, H_A) as h:
                    pool.wait_ge(free, free_per_head * h)
                    pool.tensor_copy(kh, kT[:, ds(h, 1), :].rearrange("p a t -> p (a t)")).then_inc(qk_staged, 1)
                    pool.tensor_copy(qh, qT[:, ds(h, 1), :].rearrange("p a t -> p (a t)")).then_inc(qk_staged, 1)

            pool.wait_ge(cols_turned, 1)
            pool.wait_ge(rows_stored, 64)
            pool.memset(va[:, :, :, P:P + 1], 1.0).then_inc(va_ones, 1)
            pool.wait_ge(group_taken, 12)
            stage_heads(0, inter_ready, 2)

            def delta():
                with pool.Fori(0, H_A) as h:
                    pool.wait_ge(outer_ready, 8 * h)
                    pool.tensor_copy(kh, kT[:, ds(h, 1), :].rearrange("p a t -> p (a t)")).then_inc(qk_staged, 1)
                    pool.tensor_copy(qh, qT[:, ds(h, 1), :].rearrange("p a t -> p (a t)")).then_inc(qk_staged, 1)
                    for l in range(len(LEVELS)):
                        for d in range(2):
                            if l == 0:
                                pool.wait_ge(lower_ready, 8 * h + 4 * d + 4)
                                pool.wait_ge(bx_ready, 12 * h)
                            elif l == 1:
                                pool.wait_ge(inv_ready, 14 * h + d + 1)
                            else:
                                pool.wait_ge(bx_ready, 12 * h + 2 * (l - 2) + d + 1)
                            pool.tensor_tensor(masked[:, d, :, :], lower[:, d, :, :],
                                               level[:, d, l, :].unsqueeze(1).broadcast_to([P, C, P]),
                                               ALU.mult).then_inc(mask_ready, 1)

            pool.wait_ge(head_done, H_A)
            pool.wait_ge(intra_ready, H_A)
            for b in range(2):
                for o in (0, 258):
                    ins = pool.memset(raw[:, b, :, o:o + 2], 0.0)
            ins.then_inc(raw_zeroed, 1)
            for j in range(8):
                if j == 0:
                    pool.wait_ge(tile_summed, 32)
                pool.wait_ge(silu_done, j + 1)
                t = (qT, kT)[j // 4][:, j % 4, :]
                pool.tensor_tensor(uT[:, j, :], t, t, ALU.mult).then_inc(qk_squared, 1)
            pool.wait_ge(qk_normed, 8)
            delta()

            def experts(layer):
                c0 = seen(layer)[0]
                pool.wait_ge(x_updated, 2 * J * layer + J)
                pool.iota(iota, [[1, P]], base=0, channel_multiplier=0, allow_small_or_imprecise_dtypes=True)
                pool.affine_select(out=before, in_=ones[:, :], compare_op=ALU.is_gt, fill=0.0,
                                   base=0, pattern=[[1, P]], channel_multiplier=-1).then_inc(iota_ready, 1)
                pool.wait_ge(tabled, layer + 1)
                pool.wait_ge(pass_filled, 16 * PASSES // 2)
                for ch in range(c0, C):
                    pool.wait_ge(tok_copied, 8 * layer + 2 * (ch - c0) + 2)
                    for k in range(2):
                        pool.indirect_dma_start(pass_in[:, :], bass.IndirectOffsetOnAxis(ap=slot_of[:, ch, k:k + 1], axis=0),
                                                h_row[:, ch, :], None).then_inc(tok_stored, 16)
                end = pairs_of(pool, layer)[1]
                pool.wait_ge(ye_stored, 32 * end)
                pool.tensor_tensor(small[:, 46:47], epsv[:, :], epsv[:, :], ALU.mult)
                pool.wait_ge(tok_stored, 16 * (8 + 4 * layer))
                for ch in range(c0, C):
                    for k in range(2):
                        pool.indirect_dma_start(back[k][:, ch, :], None, pass_out[:, :],
                                                bass.IndirectOffsetOnAxis(ap=slot_of[:, ch, k:k + 1], axis=0)).then_inc(
                                                    back_in[ch], 16)

            def hgrn(part):
                with pool.Fori(0, 4) as i:
                    h = 4 * part + i
                    pool.wait_ge(f_ready, 6 * h + 6)
                    pool.wait_ge(state1_step, 6 * h)
                    for l in range(1, len(LEVELS) + 1):
                        src = decay if l == 1 else tot[:, :, tot_at(l - 1):]
                        n = T >> l
                        if l > 1:
                            pool.wait_ge(tot_step, 7 * h + l - 1)
                        pool.tensor_tensor(tot[:, :, tot_at(l):tot_at(l) + n], src[:, :, 0:2 * n:2], src[:, :, 1:2 * n:2],
                                           ALU.mult).then_inc(tot_step, 1)
                    for l in range(len(LEVELS)):
                        pool.wait_ge(level_ready, 8 * h + l + 2)
                        if l:
                            pool.wait_ge(ks_updated, 7 * h + l)
                        else:
                            pool.wait_ge(tot_step, 7 * h + 7)
                        for d in range(2):
                            blocks, totals = by_block(ks[:, d, :], l), totals_of(d, l)
                            ins = pool.tensor_tensor(blocks[:, :, d, :], blocks[:, :, d, :],
                                                     totals[:, :, 1 - d:2 - d].broadcast_to([P, T >> (l + 1), 1 << l]), ALU.mult)
                        ins.then_inc(ks_updated, 1)

            experts(0)
            pool.wait_ge(x_updated, 16)
            pool.memset(att1[:, :, :, :], 0.0).then_inc(att1_zeroed, 1)
            hgrn(0)
            hgrn(1)
            experts(1)

        @block.scalar
        def _(act):
            loads = [(bmod[:, 0, :, :], b_mod[0].rearrange("(s p j) -> p s j", s=6, j=J)),
                     (bmod[:, 1, :, :], b_mod[1].rearrange("(s p j) -> p s j", s=6, j=J)),
                     (nmix[:, :, :], norm_mix.rearrange("l (p j) -> p l j", j=J)),
                     (nffn[:, :, :], norm_ffn.rearrange("l (p j) -> p l j", j=J)),
                     (nfin[:, :], norm_final.rearrange("(p j) -> p j", j=J)),
                     (w_r[:, :, :], by_feature(w_router)),
                     (bias_r[:, :], router_bias.unsqueeze(0).broadcast_to([P, E])),
                     (w_gate[:, :, :], by_feature(ab_w_in[0])[:, :, 4096:4128])]
            turned = [(gbias[:, 0, :], ab_i_bias[0].rearrange("d h -> h d")),
                      (gbias[:, 1, :], ab_f_bias[0].rearrange("d h -> h d")),
                      (gbias[:, 2, :], ab_dt_bias[0].rearrange("d h -> h d")),
                      (gbias[:, 3, :], ab_a_log[0].rearrange("d h -> h d")),
                      (gain_h[:, 0:4], ab_norm_a[0].rearrange("(h p) -> p h", p=P)),
                      (gain_h[:, 4:8], ab_norm_b[0].rearrange("(h p) -> p h", p=P)),
                      (gain_c[:, :], c_norm[0].rearrange("(h p) -> p h", p=P))]
            for d in range(2):
                turned += [(forget[:, 0, d, :], c_f_bias[0, d].rearrange("(h p) -> p h", p=P)),
                           (forget[:, 2, d, :], c_lb_raw[0, d].rearrange("(h p) -> p h", p=P))]
            turned += [(taps_w[:, k, :], ab_conv[0, k].rearrange("(g p) -> p g", p=P)) for k in range(CONV)]
            assert len(loads) == N_PARAMS
            act.dma_start(craw[:, 0, :], c[0].rearrange("(p j) -> p j", j=J)).then_inc(c_loaded, 16)
            act.dma_start(craw[:, 1, :], c_ctx.rearrange("(p j) -> p j", j=J)).then_inc(c_loaded, 16)
            for dst, src in loads:
                act.dma_start(dst, src).then_inc(params_loaded, 16)
            for dst, src in turned:
                act.dma_start(dst, src, allow_slow_non_contiguous=True).then_inc(turned_loaded, 16)
            assert len(turned) == N_TURNED
            act.wait_ge(c_loaded, 32)
            act.activation(csil[:, :, :], craw[:, :, :].rearrange("p w j -> p j w"), ACT.Silu).then_inc(csil_ready, 1)
            for j in range(0, J, 2):
                act.wait_ge(x_turned, j + 1)
                act.activation(xT[:, j, :], bank[j % 4][:, :], ACT.Copy).then_inc(xT_act, 1)

            def norm(n, t0):
                for j in range(J):
                    if n == 0 and j == 0:
                        act.wait_ge(x_turned, J)
                        act.wait_ge(xT_act, J // 2)
                        act.wait_ge(xT_dve, J // 2)
                    if n:
                        act.wait_ge(x_updated, J * (n - 1) + j + 1)
                    act.activation(uT[:, j, t0:], xT[:, j, t0:], ACT.Square).then_inc(sq_ready, 1)
                act.wait_ge(rstd_step, 2 * n + 1)
                act.activation(rstd[:, t0:], rstd[:, t0:], ACT.Sqrt).then_inc(root_ready, 1)
                for j in range(J):
                    act.wait_ge(xn_ready, J * n + j + 1)
                    act.wait_ge(coef_ready, n + 1)
                    for who, a, b in ((1, t0, N_CTX), (0, N_CTX, T)):
                        if a < b:
                            ins = act.activation(uT[:, j, a:b], uT[:, j, a:b], ACT.Identity,
                                                 scale=coef[:, who, j:j + 1], bias=shift(n)[:, who, j:j + 1])
                    ins.then_inc(u_ready, 1)

            def modulation():
                with act.Fori(0, 12 // RING) as i:
                    for r in range(RING):
                        act.wait_ge(mod_summed, RING * i + r + 1)
                        act.activation(modrow[:, ds((RING * i + r) * 512, 512)], bank[r][0:2, :],
                                       ACT.Copy).then_inc(row_copied, 1)
                act.wait_ge(row_copied, 12)
                for v in range(6):
                    for w in range(2):
                        act.dma_start(modv[:, 0, v, w, :], modrow[w:w + 1, D * v:D * v + D].rearrange(
                            "w (p j) -> w p j", j=J)).then_inc(mod_spread, 16)

            def modulation_row(i, s_):
                n = RING * i + s_
                act.wait_ge(mod_summed, 12 + n + 1)
                act.wait_ge(mod_spread, 16 * (12 + 2 * n))
                act.activation(modrow_now, bank[6 + s_ % 2][0:2, :], ACT.Copy).then_inc(row_copied, 1)
                act.wait_ge(row_copied, 12 + n + 1)
                o = 64 * (s_ % 2)
                for w in range(2):
                    act.dma_start(modv[o:o + 64, 1, ds(3 * i + s_ // 2, 1), w, :], modrow_now[w:w + 1, :].rearrange(
                        "w (p v j) -> w p v j", j=J, v=1)).then_inc(mod_spread, 16)

            def take(n, dst, func=ACT.Copy, scale=1.0):
                act.wait_ge(tile_summed, n + 1)
                act.activation(dst, bank[n % 2][:, :], func, scale=scale).then_inc(group_taken, 1)

            def gate_rows():
                act.wait_ge(gates_summed, 1)
                act.activation(grow[:, :], bank[2][0:32, :], ACT.Copy).then_inc(gates_copied, 1)
                act.wait_ge(gates_copied, 1)
                act.wait_ge(mod_spread, 16 * 12)
                for kind in range(4):
                    for d in range(2):
                        act.dma_start(grow4[:, kind, d, :], grow[8 * kind + 4 * d:8 * kind + 4 * d + 4, :]).then_inc(gates_moved, 16)
                act.wait_ge(gates_moved, 16 * 8)
                act.activation(row(6), grow4[:, GATE_B, :, :], ACT.Sigmoid).then_inc(row_act, 1)
                act.activation(gbias[:, 3, :], gbias[:, 3, :], ACT.Exp).then_inc(row_act, 1)
                act.wait_ge(row_dve, 5)
                act.activation(rows_low[:, 0:2, :, :], rows_low[:, 0:2, :, :], ACT.Exp, scale=-1.0).then_inc(row_act, 1)
                act.wait_ge(row_act, 3)
                act.activation(rows_low[:, 0:2, :, :], rows_low[:, 0:2, :, :], ACT.Ln, bias=1.0).then_inc(row_act, 1)

            def store_rows():
                act.wait_ge(rows_ready, 1)
                for kind, which, end in ((0, 7, 0), (1, 4, 3)):
                    act.dma_start(row_dram[kind, :, 0:2 * T], row(which).rearrange("h d t -> h (d t)")).then_inc(
                        rows_stored, 16)
                    act.dma_start(row_dram[kind, :, 2 * T:2 * T + 8], ends[:, end, :, :].rearrange("h d c -> h (d c)")).then_inc(
                        rows_stored, 16)

            def gate_cols():
                act.wait_ge(cols_turned, 1)
                src = bank[3][:, 0:224]
                act.activation(cols[:, 32 * Q_G:32 * Q_G + 32], src[:, 0:32], ACT.Copy).then_inc(cols_act, 1)
                act.activation(cols[:, 32 * Q_NGC:32 * Q_NGC + 32], src[:, 128:160], ACT.Copy, scale=-1.0).then_inc(cols_act, 1)
                act.activation(cols[:, 32 * Q_BETA:32 * Q_BETA + 32], src[:, 192:224], ACT.Copy).then_inc(cols_act, 1)
                act.activation(cols[:, 32 * Q_WI:32 * Q_WI + 96], src[:, 32:128], ACT.Exp).then_inc(cols_act, 1)
                act.activation(cols[:, 32 * Q_EGC:32 * Q_EGC + 32], src[:, 128:160], ACT.Exp).then_inc(cols_act, 1)
                act.activation(cols[:, 32 * Q_EKD:32 * Q_EKD + 32], src[:, 160:192], ACT.Exp).then_inc(cols_act, 1)

            def load_rows(kind, h, half, n, free, count):
                act.wait_ge(free, count)
                act.dma_start(bc[:, half, :], row_dram[kind, ds(h, 1), :].broadcast_to([P, 1032])).then_inc(bc_loaded[half], 16)

            def mlstm():
                act.wait_ge(rows_stored, 64)
                with act.Fori(0, H_A // 2) as i:
                    for half in range(2):
                        act.wait_ge(intra_ready, 2 * i)
                        act.wait_ge(cell_step, 12 * i)
                        act.dma_start(bc[:, half, :], row_dram[0, ds(2 * i + half, 1), :].broadcast_to([P, 1032])).then_inc(
                            bc_loaded[half], 16)
                    for half in range(2):
                        h = 2 * i + half
                        act.wait_ge(bc_loaded[half], 16 * i + 16)
                        act.activation(bc[:, half, 1024:1032], bc[:, half, 1024:1032], ACT.Exp).then_inc(exp_ready, 1)
                        act.wait_ge(kh_turned, h + 1)
                        act.wait_ge(update_ready, 2 * h)
                        for d in range(2):
                            for step in range(3):
                                ch = ORDER[d][step]
                                act.activation(ka[:, 3 * d + step, :], bank[3][:, P * ch:P * ch + P], ACT.Copy,
                                               scale=col(Q_AS, d, ch, h)).then_inc(ka_ready, 1)
                        for d in range(2):
                            act.wait_ge(arg_ready, 8 * h + 4 * d + 4)
                            part = bc[:, half, 512 * d:512 * d + 512]
                            act.activation(part, part, ACT.Exp).then_inc(exp_ready, 1)
                        act.wait_ge(intra_ready, h + 1)
                        act.wait_ge(head_done, h)
                        for b in range(3):
                            n = 3 if b < 2 else 2
                            act.activation(num[:, 3 * b:3 * b + n, :],
                                           bank[b][:, 0:129 * n].rearrange("p (n e) -> p n e", n=n),
                                           ACT.Copy).then_inc(intra_copied, 1)

            modulation()
            norm(0, 0)
            gate_rows()
            for g in range(2):
                for n in range(4):
                    take(4 * g + n, (qT, kT)[g][:, n, :], scale=(P ** -0.5, 1.0)[g])
            store_rows()
            gate_cols()
            act.wait_ge(va_ones, 1)
            for n in range(4):
                act.wait_ge(tile_summed, 8 + n + 1)
                act.activation(va[:, n, :, 0:P], bank[n % 2][:, :].rearrange("p (h e) -> p h e", h=H_A),
                               ACT.Copy).then_inc(group_taken, 1)
            for n in range(4):
                act.wait_ge(tile_summed, 12 + n + 1)
                act.activation(gate[:, 0:4, n, :], bank[n % 2][:, :].rearrange("p (h e) -> p h e", h=H_A),
                               ACT.Sigmoid).then_inc(group_taken, 1)
            mlstm()

            def project_b():
                act.wait_ge(head_done, H_A)
                act.wait_ge(qk_staged, 2 * H_A)
                for n in range(4):
                    act.wait_ge(tile_summed, 16 + n + 1)
                    act.activation(gate[:, 4:8, n, :], bank[n % 2][:, :].rearrange("p (h e) -> p h e", h=H_A),
                                   ACT.Silu).then_inc(group_taken, 1)
                act.wait_ge(raw_zeroed, 1)

                def silu(m):
                    act.wait_ge(conv_done, m + 1)
                    if m >= 10:
                        act.wait_ge(v_turned, m - 9)
                    dst = qT[:, m, :] if m < 4 else kT[:, m - 4, :] if m < 8 else turned_v[:, m % 2, :]
                    act.activation(dst, taps[:, m % 2, :], ACT.Silu).then_inc(silu_done, 1)

                def v_out(m):
                    act.wait_ge(v_turned, m - 7)
                    act.activation(vb[:, :, m - 8, :], bank[2 + m % 2][:, :].rearrange("p (c e) -> p c e", c=C),
                                   ACT.Copy).then_inc(v_taken, 1)

                for m in range(12):
                    act.wait_ge(tile_summed, 20 + m + 1)
                    if m >= 2:
                        act.wait_ge(conv_done, m - 1)
                    act.activation(raw[:, m % 2, :, 2:258], bank[m % 2][:, :].rearrange("p (s t) -> p s t", s=2),
                                   ACT.Copy).then_inc(group_taken, 1)
                    if m >= 1:
                        silu(m - 1)
                    if m >= 10:
                        v_out(m - 2)
                silu(11)
                v_out(10)
                v_out(11)
                for j in range(8):
                    act.wait_ge(qk_summed, j + 1)
                    act.activation(uT[:, j, :], bank[j][:, :], ACT.Sqrt, bias=epsv[:, 0:1]).then_inc(qk_root, 1)

            def delta():
                with act.Fori(0, H_A // 2) as i:
                    for half_ in range(2):
                        if half_ == 0:
                            act.wait_ge(head_done, H_A + 2 * i)
                        for b in range(2) if half_ == 0 else ():
                            act.dma_start(bc[:, b, :], row_dram[1, ds(2 * i + b, 1), :].broadcast_to([P, 1032])).then_inc(
                                bc_loaded[b], 16)
                        h = 2 * i + half_
                        act.wait_ge(bc_loaded[half_], 32 + 16 * i + 16)
                        act.activation(bc[:, half_, 1024:1032], bc[:, half_, 1024:1032], ACT.Exp).then_inc(exp_ready, 1)
                        act.wait_ge(kh_turned, H_A + h + 1)
                        act.wait_ge(head_done, H_A + h)
                        act.activation(ktok, bank[2][:, :].rearrange("p (c e) -> p c e", c=C), ACT.Copy).then_inc(ktok_ready, 1)
                        for d in range(2):
                            act.wait_ge(arg_ready, 32 + 8 * h + 4 * d + 4)
                            part = bc[:, half_, 512 * d:512 * d + 512]
                            act.activation(part, part, ACT.Exp).then_inc(exp_ready, 1)
                        for d in range(2):
                            act.wait_ge(x0_turned, 2 * h + d + 1)
                            act.activation(inv[:, d, 0, :, :], bank[3 * d][:, :].rearrange("p (c e) -> p c e", c=C),
                                           ACT.Copy).then_inc(x0_ready, 1)
                        for l in range(1, len(LEVELS)):
                            for d in range(2):
                                act.wait_ge(bx_ready, 12 * h + 2 * (l - 1) + d + 1)
                                act.activation(half[:, d, :, :], bank[3 * d][:, :].rearrange("p (c e) -> p c e", c=C),
                                               ACT.Copy).then_inc(bx_copied, 1)
                            if l in (3, 5):
                                modulation_row(i, 3 * half_ + (l - 3) // 2)
                        modulation_row(i, 3 * half_ + 2)
                        for s in range(C):
                            for d in range(2):
                                ch = ORDER[d][s]
                                act.wait_ge(xz_ready, 8 * h + 2 * s + d + 1)
                                xz = bank[3 * d][:, P:2 * P]
                                act.activation(vn_b[:, d, :], xz, ACT.Copy, scale=col(Q_BETA, d, ch, h))
                                act.activation(vd_b[:, d, :], xz, ACT.Copy, scale=col(Q_BKD, d, ch, h)).then_inc(v_ready, 1)

            def finish_heads(layer, n_heads, gain, toks):
                act.wait_ge(ms_ready, layer + 1)
                act.activation(ssq[:, :], ssq[:, :], ACT.Sqrt).then_inc(ms_root, 1)
                for h in range(n_heads):
                    act.wait_ge(y_turned, 8 * layer + h + 1)
                    act.activation(featsT[:, h, 0:toks], bank[h % 4][:, 0:toks], ACT.Copy,
                                   scale=gain[:, h:h + 1]).then_inc(feats_ready, 1)

            def experts(layer):
                c0, t0 = seen(layer)
                act.wait_ge(logits_summed, layer + 1)
                act.activation(r_rows[:, t0:], bank[1][0:E, t0:], ACT.Copy).then_inc(logits_copied, 1)
                act.wait_ge(logits_turned, layer + 1)
                act.activation(scores[:, c0:, :], bank[2][:, 0:E * (C - c0)].rearrange("p (c e) -> p c e", e=E),
                               ACT.Sigmoid).then_inc(scored, 1)
                for n, (ch, b) in enumerate((ch, b) for ch in range(c0, C) for b in range(2)):
                    act.wait_ge(tok_turned, 8 * layer + n + 1)
                    act.activation(h_tok[:, ch, 4 * b:4 * b + 4, :], bank[4 + n % 4][:, :].rearrange("p (j e) -> p j e", e=P),
                                   ACT.Copy).then_inc(tok_copied, 1)

                def he_out(i, half):
                    act.wait_ge(xs_turned, layer + i + 1)
                    for b in range(2):
                        act.activation(he[:, half, 4 * b:4 * b + 4, :], bank[b][:, :].rearrange("p (j e) -> p j e", e=P),
                                       ACT.Copy).then_inc(he_copied, 1)

                act.wait_ge(tabled, layer + 1)
                first, end = pairs_of(act, layer)
                he_out(2 * first, 0)
                with act.Fori(first, end) as m:
                    for half_ in range(2):
                        i = 2 * m + half_
                        act.wait_ge(up_summed, i + 1)
                        act.activation(silu_e[:, :, :], bank[2][:, :].rearrange("p (k e) -> p k e", e=P), ACT.Silu).then_inc(
                            silu_ready, 1)
                        he_out(i + 1, 1 - half_)
                        act.wait_ge(down_summed, i + 1)
                        act.wait_ge(ye_stored, 32 * m)
                        for b in range(2):
                            act.activation(ye[:, half_, 512 * b:512 * b + 512], bank[4 + b][:, :], ACT.Copy).then_inc(
                                ye_copied, 1)
                        act.wait_ge(ye_copied, 2 * i + 2)
                        act.dma_start(pass_out[ds(within(act, i, first) * P, P), :], ye[:, half_, :]).then_inc(ye_stored, 16)
                for ch in range(c0, C):
                    act.wait_ge(back_in[ch], 32 * (1 if ch < C_CTX else layer + 1))
                    act.activation(back[0][:, ch, :], back[0][:, ch, :], ACT.Copy, scale=wts[:, ch, 0:1]).then_inc(weighed, 1)

            project_b()
            delta()
            finish_heads(0, 8, gain_h, T)
            def project_c(part):
                n0 = 32 + 18 * part
                for n in range(18):
                    act.wait_ge(tile_summed, n0 + n + 1)
                    b = bank[n % 2]
                    kind, m = ("q", n) if n < 4 else ("z", n - 4) if n < 12 else ("v", n - 12) if n < 16 else ("g", n - 16)
                    if kind == "q":
                        ins = act.activation(q1[:, m, :], b[:, N_CTX:], ACT.Silu)
                    elif kind == "z":
                        ins = act.activation(z1[:, m // 4, m % 4, :], b[:, :], ACT.Copy)
                    elif kind == "v":
                        ins = act.activation(v1[:, m, :, :], b[:, :].rearrange("p (h e) -> p h e", h=4), ACT.Copy)
                    else:
                        ins = act.activation(featsT[:, 4 * part:4 * part + 4, P * m:P * m + P],
                                             b[:, :].rearrange("p (h e) -> p h e", h=4), ACT.Silu)
                    ins.then_inc(group_taken, 1)

            def hgrn(part):
                with act.Fori(0, 4) as i:
                    h = 4 * part + i
                    act.wait_ge(update1_ready, 2 * h)
                    for d in range(2):
                        z = z1[:, d, ds(i, 1), :].rearrange("p o t -> p (o t)")
                        act.activation(decay[:, d, :], z, ACT.Sigmoid, bias=forget[:, 0, d, ds(h, 1)]).then_inc(sig_ready, 1)
                        act.activation(ks[:, d, :], z, ACT.Sigmoid, scale=-1.0, bias=forget[:, 1, d, ds(h, 1)]).then_inc(sig_ready, 1)
                    for d in range(2):
                        act.wait_ge(kd_turned, 2 * h + d + 1)
                        act.activation(kd1[:, d, :, :], bank[5 + d][:, 0:384].rearrange("p (s e) -> p s e", s=3),
                                       ACT.Copy).then_inc(kd_ready, 1)
                    act.wait_ge(o1_ready, h + 1)
                    act.wait_ge(head_done, 8 + h)
                    act.activation(o1[:, :, :], bank[7][:, 0:2 * P].rearrange("p (c e) -> p c e", c=2), ACT.Copy).then_inc(
                        o1_copied, 1)

            def final_norm():
                for j in range(J):
                    act.wait_ge(x_updated, 3 * J + j + 1)
                    act.activation(uT[:, j, N_CTX:], xT[:, j, N_CTX:], ACT.Square).then_inc(sq_ready, 1)
                act.wait_ge(rstd_step, 9)
                act.activation(rstd[:, N_CTX:], rstd[:, N_CTX:], ACT.Sqrt).then_inc(root_ready, 1)
                for j in range(J):
                    act.wait_ge(xn_ready, 4 * J + j + 1)
                    act.activation(uT[:, j, N_CTX:], uT[:, j, N_CTX:], ACT.Copy, scale=nfin[:, j:j + 1]).then_inc(u_ready, 1)
                for ch in range(2):
                    for b in range(2):
                        act.wait_ge(out_turned, 2 * ch + b + 1)
                        act.activation(out_sb[:, ch, :].rearrange("p (e j) -> p j e", j=J)[:, 4 * b:4 * b + 4, :],
                                       bank[4 + 2 * ch + b][:, :].rearrange("p (j e) -> p j e", e=P), ACT.Copy).then_inc(out_copied, 1)

            norm(1, 0)
            experts(0)
            act.wait_ge(forget_step, 1)
            act.activation(forget[:, 3, :, :], forget[:, 3, :, :], ACT.Exp).then_inc(forget_act, 1)
            norm(2, 0)
            project_c(0)
            hgrn(0)
            act.wait_ge(head_done, 12)
            project_c(1)
            hgrn(1)
            finish_heads(1, 8, gain_c, N_LAT)
            norm(3, N_CTX)
            experts(1)
            final_norm()

        @block.vector
        def _(dve):
            for j in range(1, J, 2):
                dve.wait_ge(x_turned, j + 1)
                dve.tensor_copy(xT[:, j, :], bank[j % 4][:, :]).then_inc(xT_dve, 1)

            def modulation(layer):
                dve.wait_ge(mod_spread, 16 * (12, 36)[layer])
                dve.wait_ge(params_loaded, 16 * N_PARAMS)
                for w in range(2):
                    ins = dve.tensor_tensor(modv[:, layer, :, w, :], modv[:, layer, :, w, :], bmod[:, layer, :, :], ALU.add)
                ins.then_inc(mod_ready, 1)

            def coefficients(n, gain, s):
                dve.wait_ge(mod_ready, n // 2 + 1)
                if n:
                    dve.wait_ge(u_ready, J * n)
                dve.tensor_scalar(coef[:, :, :], modv[:, n // 2, s, :, :], 1.0, None, ALU.add).then_inc(coef_step, 1)
                dve.wait_ge(coef_step, n + 1)
                dve.tensor_tensor(coef[:, :, :], coef[:, :, :], gain.unsqueeze(1).broadcast_to([P, 2, J]),
                                  ALU.mult).then_inc(coef_ready, 1)

            def norm(n, t0):
                dve.wait_ge(ssq_ready, n + 1)
                if n == 0:
                    dve.wait_ge(consts_ready, 1)
                dve.tensor_scalar(rstd[:, t0:], bank[0][:, t0:], 1.0 / D, EPS, ALU.mult, ALU.add).then_inc(rstd_step, 1)
                dve.wait_ge(root_ready, n + 1)
                dve.reciprocal(rstd[:, t0:], rstd[:, t0:]).then_inc(rstd_step, 1)
                dve.wait_ge(rstd_step, 2 * n + 2)
                for j in range(J):
                    dve.tensor_tensor(uT[:, j, t0:], xT[:, j, t0:], rstd[:, t0:], ALU.mult).then_inc(xn_ready, 1)

            def gate_rows():
                n = [0]

                def step(ins):
                    ins.then_inc(row_dve, 1)
                    n[0] += 1
                    dve.wait_ge(row_dve, n[0])

                def last(ins):
                    ins.then_inc(row_dve, 1)
                    n[0] += 1

                dve.wait_ge(gates_moved, 16 * 8)
                dve.wait_ge(turned_loaded, 16 * N_TURNED)
                dve.wait_ge(consts_ready, 1)
                fa, ia, aa = grow4[:, GATE_F, :, :], grow4[:, GATE_I, :, :], grow4[:, GATE_A, :, :]
                for d in range(2):
                    last(dve.tensor_scalar(fa[:, d, :], fa[:, d, :], gbias[:, 1, d:d + 1], -1.0, ALU.add, ALU.mult))
                    last(dve.tensor_scalar(aa[:, d, :], aa[:, d, :], gbias[:, 2, d:d + 1], None, ALU.add))
                dve.wait_ge(row_dve, n[0])
                dve.scalar_tensor_tensor(row(0), fa, -1.0, fa, ALU.mult, ALU.max)
                last(dve.scalar_tensor_tensor(row(1), aa, -1.0, aa, ALU.mult, ALU.max))
                for d in range(2):
                    last(dve.tensor_scalar(ia[:, d, :], ia[:, d, :], gbias[:, 0, d:d + 1], None, ALU.add))
                dve.wait_ge(row_act, 4)
                step(dve.scalar_tensor_tensor(row(0), fa, 0.0, row(0), ALU.max, ALU.add))
                step(dve.scalar_tensor_tensor(row(1), aa, 0.0, row(1), ALU.max, ALU.add))
                step(dve.tensor_scalar(row(0), row(0), -1.0, None, ALU.mult))
                for d in range(2):
                    step(dve.tensor_scalar(row(1)[:, d, :], row(1)[:, d, :], gbias[:, 3, d:d + 1], -1.0,
                                           ALU.mult, ALU.mult))
                for kind, dst in ((0, 2), (1, 4)):
                    for d in range(2):
                        for ch in range(C):
                            o = slice(P * ch, P * ch + P)
                            src, to = row(kind)[:, d, o], row(dst)[:, d, o]
                            if d:
                                src, to = src[:, ::-1], to[:, ::-1]
                            last(dve.tensor_tensor_scan(to, ones[0:H_A, :], src, 0.0, ALU.mult, ALU.add))
                dve.wait_ge(row_dve, n[0])
                step(dve.tensor_tensor(row(0), ia, row(2), ALU.subtract))
                step(dve.memset(ends[:, 0, :, :], 0.0))

                def at_end(kind, d):
                    return row(kind)[:, d, (P - 1 if d == 0 else 0)::P]

                for d in range(2):
                    last(dve.tensor_copy(ends[:, 2, d, :], at_end(2, d)))
                    last(dve.tensor_copy(ends[:, 3, d, :], at_end(4, d)))
                dve.wait_ge(row_dve, n[0])
                for s in range(C):
                    for d in range(2):
                        ch = ORDER[d][s]
                        a, b = P * ch, P * ch + P
                        g, m = row(0)[:, d, a:b], row(3)[:, d, a:b]
                        if d:
                            g, m = g[:, ::-1], m[:, ::-1]
                        step(dve.tensor_tensor_scan(m, g, g, ends[:, 0, d, ch:ch + 1], ALU.max, ALU.max))
                        step(dve.tensor_copy(ends[:, 1, d, ch:ch + 1], at_end(3, d)[:, ch:ch + 1]))
                        if s < C - 1:
                            nxt = ORDER[d][s + 1]
                            step(dve.tensor_tensor(ends[:, 0, d, nxt:nxt + 1], ends[:, 1, d, ch:ch + 1],
                                                   ends[:, 2, d, ch:ch + 1], ALU.add))

                def by_chunk(kind):
                    return row(kind).rearrange("h d (c t) -> h (d c) t", c=C)

                def spread(k):
                    return ends[:, k, :, :].rearrange("h d c -> h (d c)").unsqueeze(2).broadcast_to([H_A, 2 * C, P])

                step(dve.tensor_scalar(row(7), row(3), -1.0, None, ALU.mult))
                step(dve.tensor_tensor(by_chunk(1), by_chunk(7), spread(0), ALU.add))
                step(dve.tensor_tensor(by_chunk(2), by_chunk(7), by_chunk(2), ALU.subtract))
                step(dve.tensor_tensor(by_chunk(3), by_chunk(0), spread(1), ALU.subtract))
                step(dve.tensor_tensor(by_chunk(5), spread(3), by_chunk(4), ALU.subtract))
                dve.wait_ge(row_act, 1)
                dve.tensor_tensor(ends[:, 0, :, :], ends[:, 0, :, :], ends[:, 1, :, :], ALU.subtract).then_inc(rows_ready, 1)

            def gate_cols():
                dve.wait_ge(cols_act, 6)
                dve.tensor_scalar(cols[:, 32 * Q_NEGC:32 * Q_NEGC + 32], cols[:, 32 * Q_EGC:32 * Q_EGC + 32], -1.0, None,
                                  ALU.mult).then_inc(cols_dve, 1)
                dve.tensor_tensor(cols[:, 32 * Q_BKD:32 * Q_BKD + 32], cols[:, 32 * Q_EKD:32 * Q_EKD + 32],
                                  cols[:, 32 * Q_BETA:32 * Q_BETA + 32], ALU.mult).then_inc(cols_dve, 1)
                dve.wait_ge(cols_dve, 2)

            def mlstm():
                with dve.Fori(0, H_A // 2) as i:
                    for half in range(2):
                        h = 2 * i + half
                        dve.wait_ge(bc_loaded[half], 16 * i + 16)
                        for d in range(2):
                            for ch in range(C):
                                part = bc[:, half, 512 * d + P * ch:512 * d + P * ch + P]
                                dve.scalar_tensor_tensor(part, part, col(Q_G, d, ch, h), ahead[:, d, :],
                                                         ALU.add, ALU.add).then_inc(arg_ready, 1)
                        dve.wait_ge(scores_ready, h + 1)
                        for d in range(2):
                            dve.wait_ge(exp_ready, 3 * h + 2 + d)
                            part = bc[:, half, 512 * d:512 * d + 512]
                            dve.tensor_tensor(part, part, bank[0][:, :], ALU.mult).then_inc(w_ready, 1)
                        dve.wait_ge(inter_ready, 2 * h)
                        for d in range(2):
                            dve.wait_ge(update_ready, 2 * h + d + 1)
                            for s in range(3):
                                new = bank[4 + d][:, 129 * s:129 * s + 129]
                                if s == 0:
                                    ins = dve.tensor_copy(cell[:, d, 0, :], new)
                                else:
                                    dve.wait_ge(cell_step, 6 * h + 3 * d + s)
                                    k = 1024 + 4 * d + ORDER[d][s]
                                    ins = dve.scalar_tensor_tensor(cell[:, d, s, :], cell[:, d, s - 1, :], bc[:, half, k:k + 1],
                                                                   new, ALU.mult, ALU.add)
                                ins.then_inc(cell_step, 1)
                        dve.wait_ge(intra_copied, 3 * h + 3)
                        for d in range(2):
                            dve.wait_ge(inter_ready, 2 * h + d + 1)
                            for s in range(1, C):
                                ch = ORDER[d][s]
                                u = 4 * d + ch
                                dve.scalar_tensor_tensor(num[:, u, :], bank[6 + d][:, 129 * s - 129:129 * s],
                                                         col(Q_WI, d, ch, h), num[:, u, :], ALU.mult, ALU.add).then_inc(joined, 1)
                        dve.wait_ge(joined, 6 * h + 6)
                        den = num[:, :, P:P + 1].rearrange("p u o -> p (u o)")
                        dve.scalar_tensor_tensor(small[:, 0:8], den, -1.0, den, ALU.mult, ALU.max).then_inc(head_step, 1)
                        dve.wait_ge(head_step, 12 * h + 1)
                        dve.tensor_tensor(small[:, 8:16], small[:, 0:8], cols[:, ds(32 * Q_EM + h, 8, 4)],
                                          ALU.max).then_inc(head_step, 1)
                        dve.wait_ge(head_step, 12 * h + 2)
                        dve.reciprocal(small[:, 16:24], small[:, 8:16]).then_inc(head_step, 1)
                        dve.wait_ge(head_step, 12 * h + 3)
                        for ch in range(C):
                            dve.tensor_scalar(hsum[:, ch, :], num[:, ch, 0:P], small[:, 16 + ch:17 + ch], None,
                                              ALU.mult).then_inc(head_step, 1)
                        for ch in range(C):
                            dve.wait_ge(head_step, 12 * h + 4 + ch)
                            dve.scalar_tensor_tensor(hsum[:, ch, :], num[:, 4 + ch, 0:P], small[:, 20 + ch:21 + ch],
                                                     hsum[:, ch, :], ALU.mult, ALU.add).then_inc(head_step, 1)
                        dve.wait_ge(head_step, 12 * h + 11)
                        head_out(h, 0, hsum, num, C, 12 * h + 12)

            def convolve():
                for m in range(12):
                    dve.wait_ge(group_taken, 20 + m + 1)
                    if m >= 2:
                        dve.wait_ge(silu_done, m - 1)
                    dst = taps[:, m % 2, :].rearrange("p (s t) -> p s t", s=2)
                    for k in range(CONV):
                        src = raw[:, m % 2, :, k:k + 256]
                        w = taps_w[:, k, m:m + 1]
                        if k == 0:
                            dve.tensor_scalar(dst, src, w, None, ALU.mult).then_inc(taps_step, 1)
                        else:
                            dve.wait_ge(taps_step, 4 * m + k)
                            dve.scalar_tensor_tensor(dst, src, w, dst, ALU.mult, ALU.add).then_inc(
                                taps_step if k < CONV - 1 else conv_done, 1)

            def normalise_qk():
                for j in range(8):
                    dve.wait_ge(qk_root, j + 1)
                    dve.reciprocal(uT[:, j, :], uT[:, j, :]).then_inc(qk_step, 1)
                for j in range(8):
                    dve.wait_ge(qk_step, j + 1)
                    t = (qT, kT)[j // 4][:, j % 4, :]
                    dve.scalar_tensor_tensor(t, t, (P ** -0.5, 1.0)[j // 4], uT[:, j, :], ALU.mult, ALU.mult).then_inc(qk_normed, 1)

            def delta():
                with dve.Fori(0, H_A // 2) as i:
                    for half_ in range(2):
                        h = 2 * i + half_
                        dve.wait_ge(bc_loaded[half_], 32 + 16 * i + 16)
                        for d in range(2):
                            for ch in range(C):
                                part = bc[:, half_, 512 * d + P * ch:512 * d + P * ch + P]
                                dve.scalar_tensor_tensor(part, part, col(Q_NGC, d, ch, h), ahead[:, d, :],
                                                         ALU.add, ALU.add).then_inc(arg_ready, 1)
                        dve.wait_ge(scores_ready, H_A + h + 1)
                        for d in range(2):
                            dve.wait_ge(exp_ready, 12 + 3 * h + 2 + d)
                            dve.wait_ge(mask_ready, 14 * h)
                            for ch in range(C):
                                o = slice(P * ch, P * ch + P)
                                dve.scalar_tensor_tensor(lower[:, d, ch, :], bank[0][:, o], col(Q_BETA, d, ch, h),
                                                         bc[:, half_, 512 * d + P * ch:512 * d + P * ch + P],
                                                         ALU.mult, ALU.mult).then_inc(lower_ready, 1)
                        for d in range(2):
                            dve.wait_ge(lower_ready, 8 * h + 4 * d + 4)
                            part = bc[:, half_, 512 * d:512 * d + 512]
                            dve.tensor_tensor(part, part, bank[1][:, :], ALU.mult).then_inc(att_ready, 1)
                        for d in range(2):
                            dve.wait_ge(mask_ready, 14 * h + d + 1)
                            dve.wait_ge(xz_ready, 8 * h)
                            dve.tensor_tensor(inv[:, d, 1, :, :], ident[:, :].unsqueeze(1).broadcast_to([P, C, P]),
                                              masked[:, d, :, :], ALU.subtract).then_inc(inv_ready, 1)
                        for l in range(1, len(LEVELS)):
                            for d in range(2):
                                dve.wait_ge(xbx_ready, 12 * h + 2 * (l - 1) + d + 1)
                                for x_ in (0, 1) if l < len(LEVELS) - 1 else (1,):
                                    ins = dve.tensor_tensor(inv[:, d, x_, :, :], inv[:, d, x_, :, :],
                                                            bank[3 * d + 1 + x_][:, :].rearrange("p (c e) -> p c e", c=C),
                                                            ALU.subtract)
                                ins.then_inc(inv_ready, 1)
                        for s in range(C):
                            for d in range(2) if s else ():
                                ch = ORDER[d][s]
                                dve.wait_ge(carried_ready, 6 * h + 2 * (s - 1) + d + 1)
                                dve.scalar_tensor_tensor(z_b[:, d, :], bank[3 * d][:, 0:P], col(Q_NEGC, d, ch, h),
                                                         vb[:, ch, ds(h, 1), :].rearrange("p o e -> p (o e)"),
                                                         ALU.mult, ALU.add).then_inc(z_ready, 1)
                            for d in range(2):
                                ch = ORDER[d][s]
                                dve.wait_ge(outer_ready, 8 * h + 2 * s + d + 1)
                                k = 1024 + 4 * d + ch
                                if s == 0:
                                    dve.tensor_copy(state_b[:, d, :], bank[3 * d + 2][:, 0:P]).then_inc(state_ready, 1)
                                elif s < C - 1:
                                    dve.scalar_tensor_tensor(state_b[:, d, :], state_b[:, d, :], bc[:, half_, k:k + 1],
                                                             bank[3 * d + 2][:, 0:P], ALU.mult, ALU.add).then_inc(state_ready, 1)
                                n = 14 * h + max(0, 4 * s - 2) + (1 if s == 0 else 2) * d
                                within, carried = bank[3 * d + 1][:, P:2 * P], bank[3 * d + 1][:, 0:P]
                                if s in (0, 2):
                                    dve.tensor_copy(osum[:, ch, :], within).then_inc(o_step, 1)
                                else:
                                    dve.wait_ge(o_step, n)
                                    dve.tensor_tensor(osum[:, ch, :], osum[:, ch, :], within, ALU.add).then_inc(o_step, 1)
                                if s:
                                    dve.wait_ge(o_step, n + 1)
                                    dve.scalar_tensor_tensor(osum[:, ch, :], carried, col(Q_EGC, d, ch, h), osum[:, ch, :],
                                                             ALU.mult, ALU.add).then_inc(o_step, 1)
                        dve.wait_ge(o_step, 14 * h + 14)
                        head_out(h, 4, osum, lower[:, 0, :, :], C, 48 + h + 1)

            def finish_heads(layer, n_heads, chunks):
                dve.wait_ge(head_done, 8 * layer + 8)
                dve.tensor_scalar(ssq[:, :], ssq[:, :], 1.0 / P, EPS, ALU.mult, ALU.add).then_inc(ms_ready, 1)
                dve.wait_ge(ms_root, layer + 1)
                dve.reciprocal(ssq[:, :], ssq[:, :]).then_inc(y_step, 1)
                dve.wait_ge(y_step, layer + 1)
                for h in range(n_heads):
                    g = featsT[:, h, 0:P * chunks].rearrange("p (c e) -> p c e", c=chunks)
                    r = ssq[:, C * h:C * h + chunks].unsqueeze(2).broadcast_to([P, chunks, P])
                    dve.tensor_tensor(g, g, r, ALU.mult).then_inc(y_ready, 1)

            def mix_out(layer, who):
                dve.wait_ge(pass_filled, 16 * PASSES // 2)
                for j in range(J):
                    dve.wait_ge(out_summed, 8 * layer + j + 1)
                    for w in who:
                        o = slice(0, N_CTX) if w else slice(N_CTX, T)
                        ins = dve.scalar_tensor_tensor(xT[:, j, o], bank[4 + j % 4][:, o], modv[:, layer, 2, w, j:j + 1],
                                                       xT[:, j, o], ALU.mult, ALU.add)
                    ins.then_inc(x_updated, 1)

            n_route_steps = [0]

            def route(layer):
                n = [n_route_steps[0]]
                c0, nc_ = seen(layer)[0], C - seen(layer)[0]

                def step(ins):
                    ins.then_inc(route_step, 1)
                    n[0] += 1
                    dve.wait_ge(route_step, n[0])

                def best(vals, out_, m):
                    t, t2 = tmp[:, c0:, 0:m], tmp2[:, c0:, 0:m]
                    step(dve.tensor_reduce(top[:, c0:], vals, AX.X, ALU.max))
                    step(dve.tensor_tensor(t, vals, top[:, c0:].unsqueeze(2).broadcast_to([P, nc_, m]), ALU.is_ge))
                    step(dve.scalar_tensor_tensor(t2, t, -64.0, iota[:, 0:m].unsqueeze(1).broadcast_to([P, nc_, m]),
                                                  ALU.mult, ALU.add))
                    step(dve.tensor_reduce(low[:, c0:], t2, AX.X, ALU.min))
                    step(dve.tensor_tensor(out_, t2, low[:, c0:].unsqueeze(2).broadcast_to([P, nc_, m]), ALU.is_equal))

                dve.wait_ge(scored, layer + 1)
                dve.wait_ge(iota_ready, layer + 1)
                sc, se = scores[:, c0:, :], sel[:, c0:, :]
                step(dve.tensor_tensor(se, sc, bias_r[:, :].unsqueeze(1).broadcast_to([P, nc_, E]), ALU.add))
                a = se.rearrange("p c (g e) -> p (c g) e", g=GROUPS)
                pr = pairs[:, GROUPS * c0:, :]
                step(dve.tensor_tensor(pr[:, :, 0:3], a[:, :, 0:3], a[:, :, 1:4], ALU.add))
                step(dve.tensor_tensor(pr[:, :, 3:5], a[:, :, 0:2], a[:, :, 2:4], ALU.add))
                step(dve.tensor_tensor(pr[:, :, 5:6], a[:, :, 0:1], a[:, :, 3:4], ALU.add))
                step(dve.tensor_reduce(g_score[:, c0:, :].rearrange("p c g -> p (c g)"), pr, AX.X, ALU.max))
                best(g_score[:, c0:, :], g_pick[:, c0:, :], GROUPS)
                gp = g_pick[:, c0:, :]
                step(dve.tensor_scalar(gp, gp, FAR, -FAR, ALU.mult, ALU.add))
                step(dve.tensor_tensor(a, a, gp.rearrange("p c g -> p (c g)").unsqueeze(2).broadcast_to(
                    [P, GROUPS * nc_, E // GROUPS]), ALU.add))
                fi, sd, tk = first[:, c0:, :], second[:, c0:, :], taken[:, c0:, :]
                best(se, fi, E)
                step(dve.scalar_tensor_tensor(se, fi, -3 * FAR, se, ALU.mult, ALU.add))
                best(se, sd, E)
                for k, oh in ((0, fi), (1, sd)):
                    step(dve.tensor_tensor(tmp[:, c0:, :], oh, sc, ALU.mult))
                    step(dve.tensor_reduce(wts[:, c0:, k], tmp[:, c0:, :], AX.X, ALU.add))
                step(dve.tensor_tensor(total[:, c0:], wts[:, c0:, 0], wts[:, c0:, 1], ALU.add))
                step(dve.reciprocal(total[:, c0:], total[:, c0:]))
                step(dve.tensor_tensor(wts[:, c0:, :], wts[:, c0:, :], total[:, c0:].unsqueeze(2).broadcast_to([P, nc_, 2]),
                                       ALU.mult))
                dve.tensor_tensor(tk, fi, sd, ALU.add).then_inc(chosen, 1)
                dve.wait_ge(counted, layer + 1)
                rk = bank[3][:, 0:E * C].rearrange("p (c e) -> p c e", e=E)
                cn = bank[3][:, E * C:2 * E * C].rearrange("p (c e) -> p c e", e=E)
                step(dve.tensor_copy(count[:, :], cn[:, c0, :]))
                step(dve.tensor_copy(rank[:, c0, :], rk[:, c0, :]))
                for ch in range(c0 + 1, C):
                    step(dve.tensor_tensor(rank[:, ch, :], rk[:, ch, :], count[:, :], ALU.add))
                    step(dve.tensor_tensor(count[:, :], count[:, :], cn[:, ch, :], ALU.add))
                step(dve.tensor_scalar(n_pass[:, :], count[:, :], 128.0, 1.0, ALU.is_gt, ALU.add))
                for m in (256.0, 384.0):
                    step(dve.scalar_tensor_tensor(n_pass[:, :], count[:, :], m, n_pass[:, :], ALU.is_gt, ALU.add))
                step(dve.tensor_tensor_scan(upto_e[:, :], ones[:, 0:E], n_pass[:, :], 0.0, ALU.mult, ALU.add))
                step(dve.tensor_tensor(start_e[:, :], upto_e[:, :], n_pass[:, :], ALU.subtract))
                step(dve.scalar_tensor_tensor(rank[:, c0:, :], start_e[:, :].unsqueeze(1).broadcast_to([P, nc_, E]), 128.0,
                                              rank[:, c0:, :], ALU.mult, ALU.add))
                for k, oh in ((0, fi), (1, sd)):
                    step(dve.tensor_tensor(tmp[:, c0:, :], oh, rank[:, c0:, :], ALU.mult))
                    step(dve.tensor_reduce(pos[:, c0:, k], tmp[:, c0:, :], AX.X, ALU.add))
                np_ = PASSES + 2
                step(dve.tensor_copy(slot_of[:, c0:, :], pos[:, c0:, :]))
                i0 = ids_f[0:1, :, :]
                step(dve.tensor_tensor(i0, upto_e[0:1, :].unsqueeze(1).broadcast_to([1, np_, E]),
                                       iota[0:1, 0:np_].unsqueeze(2).broadcast_to([1, np_, E]), ALU.is_le))
                step(dve.tensor_reduce(table[0:1, :], i0, AX.X, ALU.add))
                step(dve.tensor_scalar(steps[:, layer, 0:np_], table[0:1, :], float(E - 1), None, ALU.min))
                step(dve.tensor_scalar(table[0:1, 0:16], iota[0:1, 0:16], 2.0, None, ALU.mult))
                step(dve.tensor_scalar(table[0:1, 0:16], table[0:1, 0:16], upto_e[0:1, E - 1:E], None, ALU.is_lt))
                step(dve.tensor_reduce(table[0:1, 16:17], table[0:1, 0:16], AX.X, ALU.add))
                if layer == 0:
                    step(dve.tensor_copy(small[0:1, 47:48], table[0:1, 16:17]))
                else:
                    step(dve.tensor_tensor(table[0:1, 16:17], table[0:1, 16:17], small[0:1, 47:48], ALU.add))
                dve.tensor_copy(steps[:, layer, np_:np_ + 1], table[0:1, 16:17]).then_inc(tabled, 1)
                n_route_steps[0] = n[0]

            def experts(layer, who):
                c0 = seen(layer)[0]
                dve.wait_ge(tabled, layer + 1)
                first, end = pairs_of(dve, layer)
                with dve.Fori(first, end) as m:
                    for half_ in range(2):
                        i = 2 * m + half_
                        dve.wait_ge(silu_ready, i + 1)
                        dve.wait_ge(down_summed, i)
                        dve.tensor_tensor(act_e[:, :, :], silu_e[:, :, :], bank[3][:, :].rearrange("p (k e) -> p k e", e=P),
                                          ALU.mult).then_inc(gated, 1)
                for ch in range(c0, C):
                    n = C * layer + ch - c0
                    dve.wait_ge(weighed, n + 1)
                    dve.wait_ge(back_in[ch], 32 * (1 if ch < C_CTX else layer + 1))
                    dve.scalar_tensor_tensor(back[0][:, ch, :], back[1][:, ch, :], wts[:, ch, 1:2], back[0][:, ch, :],
                                             ALU.mult, ALU.add).then_inc(both_ready, 1)
                for j in range(J):
                    dve.wait_ge(both_turned, J * layer + j + 1)
                    for w in who:
                        o = slice(0, N_CTX) if w else slice(N_CTX, T)
                        ins = dve.scalar_tensor_tensor(xT[:, j, o], bank[j][:, o], modv[:, layer, 5, w, j:j + 1],
                                                       xT[:, j, o], ALU.mult, ALU.add)
                    ins.then_inc(x_updated, 1)

            def head_out(h, first, summed, dead, n, steps):
                for ch in range(n):
                    ins = dve.tensor_tensor_reduce(dead[:, ch, 0:P], summed[:, ch, :], summed[:, ch, :], 1.0, 0.0,
                                                   ALU.mult, ALU.add, small[:, 24 + ch:25 + ch])
                ins.then_inc(head_step, 1)
                g = featsT[:, ds(first + h, 1), 0:P * n].rearrange("p o (c e) -> p (o c) e", c=n)
                dve.tensor_tensor(g, g, summed, ALU.mult)
                dve.wait_ge(head_step, steps)
                dve.tensor_copy(ssq[:, ds((first + h) * C, n)], small[:, 24:24 + n]).then_inc(head_done, 1)

            def lower_bounds():
                n = [0]

                def step(ins):
                    ins.then_inc(forget_step, 1)
                    n[0] += 1
                    dve.wait_ge(forget_step, n[0])

                raw_, p_ = forget[:, 2, :, :], forget[:, 3, :, :]
                step(dve.tensor_tensor(p_, raw_, raw_, ALU.subtract))
                step(dve.tensor_scalar(forget[:, 1, :, :], forget[:, 0, :, :], -1.0, None, ALU.mult))
                dve.wait_ge(forget_act, 1)
                step(dve.reciprocal(raw_, p_))
                step(dve.tensor_tensor(p_, p_, raw_, ALU.mult))
                step(dve.tensor_tensor(raw_, p_, p_, ALU.subtract))
                step(dve.tensor_scalar(p_, raw_, -1.0, 1.0, ALU.mult, ALU.add))

            def hgrn(part):
                with dve.Fori(0, 4) as i:
                    h = 4 * part + i
                    q = q1[:, ds(i, 1), :].rearrange("p o t -> p (o t)")
                    dve.wait_ge(o1_ready, h)
                    for d in range(2):
                        lb, rest = forget[:, 2, d, ds(h, 1)], forget[:, 3, d, ds(h, 1)]
                        dve.wait_ge(sig_ready, 4 * h + 2 * d + 2)
                        dve.tensor_scalar(decay[:, d, :], decay[:, d, :], rest, lb, ALU.mult, ALU.add).then_inc(f_ready, 1)
                        dve.tensor_scalar(ks[:, d, :], ks[:, d, :], rest, None, ALU.mult).then_inc(f_ready, 1)
                        dve.wait_ge(f_ready, 6 * h + 3 * d + 1)
                        dve.tensor_tensor(qp[:, d, :], q, decay[:, d, N_CTX:], ALU.mult).then_inc(f_ready, 1)
                    for l in range(len(LEVELS)):
                        dve.wait_ge(level_ready, 8 * h + l + 2)
                        if l:
                            dve.wait_ge(tot_step, 7 * h + l)
                            dve.wait_ge(qp_updated, 7 * h + l)
                            dve.wait_ge(cp_done, 8 * h + l + 1)
                        for d in range(2):
                            blocks, totals = by_block(qp[:, d, :], l), totals_of(d, l, lat=True)
                            if l == 0 and d == 1:
                                dve.copy_predicated(att1[:, :, :, :].rearrange("p d c t -> p (d c) t"),
                                                    ident[:, :].bitcast(I32).unsqueeze(1).broadcast_to([P, 4, P]),
                                                    bank[2][:, :].rearrange("p (a t) -> p a t", a=4)).then_inc(cp_done, 1)
                                dve.wait_ge(cp_done, 8 * h + 1)
                            ins = dve.tensor_tensor(blocks[:, :, 1 - d, :], blocks[:, :, 1 - d, :],
                                                    totals[:, :, d:d + 1].broadcast_to([P, N_LAT >> (l + 1), 1 << l]), ALU.mult)
                        ins.then_inc(qp_updated, 1)
                        dve.copy_predicated(att1[:, :, :, :],
                                            level[:, :, l, :].bitcast(I32).unsqueeze(2).broadcast_to([P, 2, 2, P]),
                                            bank[2 + (l + 1) % 3][:, :].rearrange("p (d c t) -> p d c t", d=2, c=2)).then_inc(
                                                cp_done, 1)
                    for d in range(2):
                        dve.wait_ge(update1_ready, 2 * h + d + 1)
                        for s in range(3):
                            new = bank[5 + d][:, P * s:P * s + P]
                            if s == 0:
                                ins = dve.tensor_copy(state1[:, d, 0, :], new)
                            else:
                                dve.wait_ge(state1_step, 6 * h + 3 * d + s)
                                k = tot_at(7) + ORDER[d][s]
                                ins = dve.scalar_tensor_tensor(state1[:, d, s, :], state1[:, d, s - 1, :], tot[:, d, k:k + 1],
                                                               new, ALU.mult, ALU.add)
                            ins.then_inc(state1_step, 1)
                    dve.wait_ge(o1_copied, h + 1)
                    head_out(h, 0, o1, state1[:, 0, :, :], 2, 52 + h + 1)

            modulation(0)
            coefficients(0, nmix[:, 0, :], 1)
            norm(0, 0)
            gate_rows()
            gate_cols()
            mlstm()
            convolve()
            normalise_qk()
            delta()
            finish_heads(0, 8, C)
            modulation(1)
            mix_out(0, (0, 1))
            coefficients(1, nffn[:, 0, :], 4)
            norm(1, 0)
            route(0)
            experts(0, (0, 1))
            lower_bounds()
            coefficients(2, nmix[:, 1, :], 1)
            norm(2, 0)
            hgrn(0)
            hgrn(1)
            finish_heads(1, 8, 2)
            mix_out(1, (0,))
            coefficients(3, nffn[:, 1, :], 4)
            norm(3, N_CTX)
            route(1)
            experts(1, (0,))
            norm(4, N_CTX)

        @block.tensor
        def _(pe):
            pe.wait_ge(ident_ready, 1)
            pe.wait_ge(x_loaded, 32)
            for j in range(J):
                if j >= 4:
                    pe.wait_ge((xT_act, xT_dve)[j % 2], j // 2 - 1)
                for t in range(C):
                    mm = pe.transpose(bank[j % 4][:, P * t:P * t + P], x_in[:, t, j::J], ident[:, :])
                mm.then_inc(x_turned, 1)

            def modulation():
                pe.wait_ge(csil_ready, 1)
                pe.wait_ge(xT_act, J // 2)
                pe.wait_ge(xT_dve, J // 2)
                with pe.Fori(0, 12 // RING) as i:
                    for r in range(RING):
                        pe.wait_ge(slot_in[r], 16 * i + 16)
                        pe.wait_ge(row_copied, RING * i)
                        w = slot(r, J)
                        for k in range(J):
                            mm = pe.matmul(bank[r][0:2, :], csil[:, k, :], w[:, k, :], start=(k == 0), stop=(k == J - 1))
                        mm.then_inc(mod_summed, 1)

            def norm(n, t0):
                pe.wait_ge(consts_ready, 1)
                for j in range(J):
                    pe.wait_ge(sq_ready, J * n + j + 1)
                    mm = pe.matmul(bank[0][:, t0:], ones[:, :], uT[:, j, t0:], start=(j == 0), stop=(j == J - 1))
                mm.then_inc(ssq_ready, 1)

            modulation()
            norm(0, 0)

            def project(layer, g, n0, turned, t0=0):
                at = slot_at["in", layer, g, 0]
                slot_arrived(pe, at)
                w = slot(at, J)
                tiles = range(4) if turned or t0 == 0 else range(t0 // P, C)
                for m, n in enumerate(tiles):
                    if n0 + m >= 2:
                        pe.wait_ge(group_taken, n0 + m - 1)
                    for k in range(J):
                        if turned:
                            mm = pe.matmul(bank[(n0 + m) % 2][:, t0:], w[:, k, P * n:P * n + P], uT[:, k, t0:],
                                           start=(k == 0), stop=(k == J - 1))
                        else:
                            mm = pe.matmul(bank[(n0 + m) % 2][:, :], uT[:, k, P * n:P * n + P], w[:, k, :],
                                           start=(k == 0), stop=(k == J - 1))
                    mm.then_inc(tile_summed, 1)

            def gate_rows():
                pe.wait_ge(params_loaded, 16 * N_PARAMS)
                for k in range(J):
                    pe.wait_ge(u_ready, k + 1)
                    mm = pe.matmul(bank[2][0:32, :], w_gate[:, k, :], uT[:, k, :], start=(k == 0), stop=(k == J - 1))
                mm.then_inc(gates_summed, 1)

            def gate_cols():
                pe.wait_ge(rows_ready, 1)
                pe.wait_ge(row_act, 1)
                for kind in range(7):
                    for d in range(2):
                        for ch in range(C):
                            o = 32 * kind + 16 * d + 4 * ch
                            mm = pe.transpose(bank[3][:, o:o + H_A], row(kind)[:, d, P * ch:P * ch + P],
                                              ident[0:H_A, 0:H_A])
                mm.then_inc(cols_turned, 1)

            def mlstm():
                pe.wait_ge(group_taken, 16)
                pe.wait_ge(cols_dve, 2)
                with pe.Fori(0, H_A // 2) as i:
                    for half in range(2):
                        h = 2 * i + half

                        def v(ch):
                            return va[:, ch, ds(h, 1), :].rearrange("p o e -> p (o e)")

                        pe.wait_ge(qk_staged, 2 * h + 2)
                        pe.wait_ge(joined, 6 * h)
                        pe.wait_ge(intra_copied, 3 * h)
                        pe.wait_ge(ka_ready, 6 * h)
                        for ch in range(C):
                            o = slice(P * ch, P * ch + P)
                            mm = pe.matmul(bank[0][:, o], kh[:, o], qh[:, o], start=True, stop=True)
                        mm.then_inc(scores_ready, 1)
                        for ch in range(C):
                            mm = pe.transpose(bank[3][:, P * ch:P * ch + P], kh[:, P * ch:P * ch + P], ident[:, :])
                        mm.then_inc(kh_turned, 1)
                        pe.wait_ge(cell_step, 6 * h)
                        for d in range(2):
                            pe.wait_ge(ka_ready, 6 * h + 3 * d + 3)
                            for s in range(3):
                                mm = pe.matmul(bank[4 + d][:, 129 * s:129 * s + 129], ka[:, 3 * d + s, :], v(ORDER[d][s]),
                                               start=True, stop=True)
                            mm.then_inc(update_ready, 1)
                        pe.wait_ge(w_ready, 2 * h + 2)
                        for d in range(2):
                            for ch in range(C):
                                u = 4 * d + ch
                                o = 512 * d + P * ch
                                mm = pe.matmul(bank[u // 3][:, 129 * (u % 3):129 * (u % 3) + 129], bc[:, half, o:o + P], v(ch),
                                               start=True, stop=True)
                        mm.then_inc(intra_ready, 1)
                        for d in range(2):
                            pe.wait_ge(cell_step, 6 * h + 3 * d + 3)
                            for s in range(1, C):
                                ch = ORDER[d][s]
                                mm = pe.matmul(bank[6 + d][:, 129 * s - 129:129 * s], qh[:, P * ch:P * ch + P],
                                               cell[:, d, s - 1, :], start=True, stop=True)
                            mm.then_inc(inter_ready, 1)

            gate_rows()
            for k in range(J):
                pe.wait_ge(u_ready, k + 1)
            for n, g in enumerate(IN_GROUPS[0][:4]):
                if n == 2:
                    gate_cols()
                project(0, g, 4 * n, turned=n < 2)
            mlstm()

            def project_b():
                for m, g in enumerate(IN_GROUPS[0][4:]):
                    if m == 0:
                        pe.wait_ge(intra_copied, 12)
                        project(0, g, 16, turned=False)
                        continue
                    project(0, g, 16 + 4 * m, turned=True)
                for m in range(4):
                    pe.wait_ge(silu_done, 8 + m + 1)
                    if m >= 2:
                        pe.wait_ge(v_taken, m - 1)
                    for ch in range(C):
                        mm = pe.transpose(bank[2 + m % 2][:, P * ch:P * ch + P], turned_v[:, m % 2, P * ch:P * ch + P],
                                          ident[:, :])
                    mm.then_inc(v_turned, 1)
                pe.wait_ge(v_taken, 4)
                pe.wait_ge(group_taken, 32)
                for j in range(8):
                    pe.wait_ge(qk_squared, j + 1)
                    pe.matmul(bank[j][:, :], ones[:, :], uT[:, j, :], start=True, stop=True).then_inc(qk_summed, 1)

            def modulation_part(i, s_, part):
                n = RING * i + s_
                at = slot_at["mod", 1, 0, 0] + s_
                if part == 0:
                    pe.wait_ge(slot_in[at % RING], 16 * (at // RING + 1) + 16 * i)
                    pe.wait_ge(row_copied, 12 + n - 1)
                for k in (2 * part, 2 * part + 1):
                    mm = pe.matmul(bank[6 + s_ % 2][0:2, :], csil[:, k, :], slot(at, J)[:, k, :], start=(k == 0), stop=(k == J - 1))
                if part == 3:
                    mm.then_inc(mod_summed, 1)

            def delta():
                pe.wait_ge(qk_root, 8)
                with pe.Fori(0, H_A // 2) as i:
                    for half_ in range(2):
                        h = 2 * i + half_
                        pe.wait_ge(qk_staged, 2 * H_A + 2 * h + 2)
                        pe.wait_ge(head_done, H_A + h)
                        for ch in range(C):
                            o = slice(P * ch, P * ch + P)
                            pe.matmul(bank[0][:, o], kh[:, o], kh[:, o], start=True, stop=True)
                        for ch in range(C):
                            o = slice(P * ch, P * ch + P)
                            mm = pe.matmul(bank[1][:, o], kh[:, o], qh[:, o], start=True, stop=True)
                        mm.then_inc(scores_ready, 1)
                        for ch in range(C):
                            mm = pe.transpose(bank[2][:, P * ch:P * ch + P], kh[:, P * ch:P * ch + P], ident[:, :])
                        mm.then_inc(kh_turned, 1)
                        pe.wait_ge(att_ready, 2 * h + 2)
                        pe.wait_ge(ktok_ready, h + 1)
                        for d in range(2):
                            pe.wait_ge(inv_ready, 14 * h + d + 1)
                            for ch in range(C):
                                mm = pe.transpose(bank[3 * d][:, P * ch:P * ch + P], inv[:, d, 1, ch, :], ident[:, :])
                            mm.then_inc(x0_turned, 1)
                        for l in range(1, len(LEVELS)):
                            for d in range(2):
                                pe.wait_ge(mask_ready, 14 * h + 2 * l + d + 1)
                                if l == 1:
                                    pe.wait_ge(x0_ready, 2 * h + d + 1)
                                else:
                                    pe.wait_ge(inv_ready, 14 * h + 2 * (l - 1) + d + 1)
                                for ch in range(C):
                                    mm = pe.matmul(bank[3 * d][:, P * ch:P * ch + P], masked[:, d, ch, :], inv[:, d, 0, ch, :],
                                                   start=True, stop=True)
                                mm.then_inc(bx_ready, 1)
                            modulation_part(i, 3 * half_ + (l - 1) // 2, 2 * ((l - 1) % 2))
                            for d in range(2):
                                pe.wait_ge(bx_copied, 12 * h + 2 * (l - 1) + d + 1)
                                for ch in range(C) if l < len(LEVELS) - 1 else ():
                                    pe.matmul(bank[3 * d + 1][:, P * ch:P * ch + P], inv[:, d, 1, ch, :], half[:, d, ch, :],
                                              start=True, stop=True)
                                for ch in range(C):
                                    mm = pe.matmul(bank[3 * d + 2][:, P * ch:P * ch + P], half[:, d, ch, :], inv[:, d, 1, ch, :],
                                                   start=True, stop=True)
                                mm.then_inc(xbx_ready, 1)
                            modulation_part(i, 3 * half_ + (l - 1) // 2, 2 * ((l - 1) % 2) + 1)
                        pe.wait_ge(inv_ready, 14 * h + 14)
                        for s in range(C):
                            for d in range(2) if s else ():
                                o = slice(P * ORDER[d][s], P * ORDER[d][s] + P)
                                pe.wait_ge(state_ready, 6 * h + 2 * (s - 1) + d + 1)
                                pe.matmul(bank[3 * d][:, 0:P], kh[:, o], state_b[:, d, :], start=True, stop=True).then_inc(
                                    carried_ready, 1)
                            for d in range(2):
                                ch = ORDER[d][s]
                                if s == 0:
                                    z = vb[:, ch, ds(h, 1), :].rearrange("p o e -> p (o e)")
                                else:
                                    pe.wait_ge(z_ready, 6 * h + 2 * (s - 1) + d + 1)
                                    z = z_b[:, d, :]
                                pe.matmul(bank[3 * d][:, P:2 * P], inv[:, d, 1, ch, :], z, start=True, stop=True).then_inc(
                                    xz_ready, 1)
                            for d in range(2):
                                ch = ORDER[d][s]
                                o = slice(P * ch, P * ch + P)
                                if s:
                                    pe.wait_ge(o_step, 14 * h + max(0, 4 * (s - 1) - 2) + (1 if s == 1 else 2) * (d + 1))
                                    pe.matmul(bank[3 * d + 1][:, 0:P], qh[:, o], state_b[:, d, :], start=True, stop=True)
                                pe.wait_ge(v_ready, 8 * h + 2 * s + d + 1)
                                mm = pe.matmul(bank[3 * d + 1][:, P:2 * P], bc[:, half_, 512 * d + P * ch:512 * d + P * ch + P],
                                               vn_b[:, d, :], start=True, stop=True)
                                if s < C - 1:
                                    mm = pe.matmul(bank[3 * d + 2][:, 0:P], ktok[:, ch, :], vd_b[:, d, :], start=True, stop=True)
                                mm.then_inc(outer_ready, 1)

            def project_c(part):
                n0 = 32 + 18 * part
                for k, (g, tiles) in enumerate(zip(IN_GROUPS[1][5 * part:5 * part + 5], (4, 4, 4, 4, 2))):
                    if k == 4:
                        project(1, g, n0, turned=False, t0=N_CTX)
                    else:
                        project(1, g, n0, turned=k < 3, t0=N_CTX if k == 0 else 0)
                    n0 += tiles

            def hgrn(part):
                with pe.Fori(0, 4) as i:
                    h = 4 * part + i
                    q = q1[:, ds(i, 1), :].rearrange("p o t -> p (o t)")
                    pe.wait_ge(f_ready, 6 * h + 6)
                    pe.wait_ge(cp_done, 8 * h)
                    for l in range(-1, len(LEVELS)):
                        if l >= 1:
                            pe.wait_ge(qp_updated, 7 * h + l)
                            pe.wait_ge(ks_updated, 7 * h + l)
                        if l >= 2:
                            pe.wait_ge(cp_done, 8 * h + l - 1)
                        for d in range(2):
                            for ch in range(2):
                                o = slice(P * ch, P * ch + P)
                                a = P * (2 * d + ch)
                                mm = pe.matmul(bank[2 + (l + 1) % 3][:, a:a + P], ks[:, d, N_CTX + P * ch:N_CTX + P * ch + P],
                                               q[:, o] if l < 0 else qp[:, d, o], start=True, stop=True)
                        mm.then_inc(level_ready, 1)
                    pe.wait_ge(ks_updated, 7 * h + 7)
                    pe.wait_ge(state1_step, 6 * h)
                    for d in range(2):
                        for s in range(3):
                            o = P * ORDER[d][s]
                            mm = pe.transpose(bank[5 + d][:, P * s:P * s + P], ks[:, d, o:o + P], ident[:, :])
                        mm.then_inc(kd_turned, 1)
                    for d in range(2):
                        pe.wait_ge(kd_ready, 2 * h + d + 1)
                        for s in range(3):
                            v = v1[:, ORDER[d][s], ds(i, 1), :].rearrange("p o e -> p (o e)")
                            mm = pe.matmul(bank[5 + d][:, P * s:P * s + P], kd1[:, d, s, :], v, start=True, stop=True)
                        mm.then_inc(update1_ready, 1)
                    pe.wait_ge(cp_done, 8 * h + 8)
                    pe.wait_ge(qp_updated, 7 * h + 7)
                    pe.wait_ge(state1_step, 6 * h + 6)
                    pe.wait_ge(o1_copied, h)
                    for ch in range(2):
                        v = v1[:, 2 + ch, ds(i, 1), :].rearrange("p o e -> p (o e)")
                        o = bank[7][:, P * ch:P * ch + P]
                        for d in range(2):
                            pe.matmul(o, att1[:, d, ch, :], v, start=(d == 0), stop=False)
                        for d in range(2):
                            s = ORDER[d].index(2 + ch)
                            mm = pe.matmul(o, qp[:, d, P * ch:P * ch + P], state1[:, d, s - 1, :], start=False, stop=(d == 1))
                    mm.then_inc(o1_ready, 1)

            def final():
                for n, (ch, b) in enumerate((ch, b) for ch in range(2) for b in range(2)):
                    pe.wait_ge(u_ready, 4 * J + 4 * b + 4)
                    for j in range(4):
                        mm = pe.transpose(bank[4 + n][:, P * j:P * j + P],
                                          uT[:, 4 * b + j, N_CTX + P * ch:N_CTX + P * ch + P], ident[:, :])
                    mm.then_inc(out_turned, 1)

            def finish_heads(layer, n_heads, chunks):
                for h in range(n_heads):
                    pe.wait_ge(y_ready, 8 * layer + h + 1)
                    if h >= 4:
                        pe.wait_ge(feats_ready, 8 * layer + h - 3)
                    for ch in range(chunks):
                        mm = pe.transpose(bank[h % 4][:, P * ch:P * ch + P], featsT[:, h, P * ch:P * ch + P], ident[:, :])
                    mm.then_inc(y_turned, 1)

            def mix_out(layer, toks, t0):
                at = slot_at["out", layer, 0, 0]
                slot_arrived(pe, at)
                slot_arrived(pe, at + 1)
                pe.wait_ge(feats_ready, 8 * layer + 8)
                for j in range(J):
                    if j >= 4:
                        pe.wait_ge(x_updated, 16 * layer + j - 3)
                    for h in range(8):
                        mm = pe.matmul(bank[4 + j % 4][:, t0:], slot(at + h // 4, 4)[:, h % 4, j::J], featsT[:, h, 0:toks],
                                       start=(h == 0), stop=(h == 7))
                    mm.then_inc(out_summed, 1)

            project_b()
            delta()
            finish_heads(0, 8, C)
            mix_out(0, T, 0)

            def route(layer):
                c0, t0 = seen(layer)
                for k in range(J):
                    pe.wait_ge(u_ready, J * (2 * layer + 1) + k + 1)
                    mm = pe.matmul(bank[1][0:E, t0:], w_r[:, k, :], uT[:, k, t0:], start=(k == 0), stop=(k == J - 1))
                mm.then_inc(logits_summed, 1)
                pe.wait_ge(logits_copied, layer + 1)
                for ch in range(c0, C):
                    mm = pe.transpose(bank[2][:, E * (ch - c0):E * (ch - c0) + E], r_rows[:, P * ch:P * ch + P],
                                      ident[0:E, 0:E])
                mm.then_inc(logits_turned, 1)
                for m, (ch, b) in enumerate((ch, b) for ch in range(c0, C) for b in range(2)):
                    if m >= 4:
                        pe.wait_ge(tok_copied, 8 * layer + m - 3)
                    for j in range(4):
                        mm = pe.transpose(bank[4 + m % 4][:, P * j:P * j + P], uT[:, 4 * b + j, P * ch:P * ch + P], ident[:, :])
                    mm.then_inc(tok_turned, 1)
                pe.wait_ge(iota_ready, layer + 1)
                pe.wait_ge(chosen, layer + 1)
                tk = taken[:, :, :].rearrange("p c e -> p (c e)")[:, E * c0:]
                m = E * (C - c0)
                pe.matmul(bank[3][:, E * c0:E * C], before, tk, start=True, stop=True)
                pe.matmul(bank[3][:, E * C + E * c0:2 * E * C], ones[:, :], tk, start=True, stop=True).then_inc(counted, 1)

            def experts(layer):
                c0, t0 = seen(layer)

                def turn(n, half_):
                    pe.wait_ge(xs_in[half_], 16 * n)
                    for j in range(J):
                        mm = pe.transpose(bank[j // 4][:, P * (j % 4):P * (j % 4) + P], xs[:, half_, P * j:P * j + P], ident[:, :])
                    mm.then_inc(xs_turned, 1)

                pe.wait_ge(tabled, layer + 1)
                first, end = pairs_of(pe, layer)
                turn(first + layer + 1, 0)
                with pe.Fori(first, end) as m:
                    for half_ in range(2):
                        i = 2 * m + half_
                        s1, s3, s2 = expert_slots[half_]
                        pe.wait_ge(he_copied, 2 * layer + 2 * i + 2)
                        pe.wait_ge(gated, i)
                        for s_, b in ((s1, 2), (s3, 3)):
                            pe.wait_ge(expert_in[s_], 16 * m + 16)
                            w = slot(s_, J)
                            for f in range(FT):
                                for k in range(J):
                                    mm = pe.matmul(bank[b][:, P * f:P * f + P], w[:, k, f::FT], he[:, half_, k, :],
                                                   start=(k == 0), stop=(k == J - 1))
                        mm.then_inc(up_summed, 1)
                        turn(m + 1 if half_ == 0 else m + 2 + layer, 1 - half_)
                        pe.wait_ge(gated, i + 1)
                        pe.wait_ge(expert_in[s2], 16 * m + 16)
                        pe.wait_ge(ye_copied, 2 * i)
                        w = slot(s2, FT)
                        for b in range(2):
                            for f in range(FT):
                                mm = pe.matmul(bank[4 + b][:, :], act_e[:, f, :], w[:, f, 512 * b:512 * b + 512],
                                               start=(f == 0), stop=(f == FT - 1))
                        mm.then_inc(down_summed, 1)
                for ch in range(c0, C):
                    pe.wait_ge(both_ready, C * layer + ch - c0 + 1)
                    for j in range(J):
                        mm = pe.transpose(bank[j][:, P * ch:P * ch + P], back[0][:, ch, j::J], ident[:, :])
                        if ch == C - 1:
                            mm.then_inc(both_turned, 1)

            norm(1, 0)
            route(0)
            experts(0)
            norm(2, 0)
            for k in range(J):
                pe.wait_ge(u_ready, 2 * J + k + 1)
            project_c(0)
            pe.wait_ge(group_taken, 32 + 18)
            pe.wait_ge(att1_zeroed, 1)
            hgrn(0)
            project_c(1)
            pe.wait_ge(group_taken, 32 + 36)
            hgrn(1)
            finish_heads(1, 8, 2)
            mix_out(1, N_LAT, N_CTX)
            norm(3, N_CTX)
            route(1)
            experts(1)
            norm(4, N_CTX)
            final()


INPUTS = ("x", "c", "ctx", "c_ctx", "w_mod", "b_mod", "norm_mix", "norm_ffn", "norm_final", "ab_w_in", "ab_i_bias",
          "ab_f_bias", "ab_conv", "ab_a_log", "ab_dt_bias", "ab_norm_a", "ab_norm_b", "ab_w_out", "c_w_in", "c_f_bias",
          "c_lb_raw", "c_norm", "c_w_out", "w_router", "router_bias", "w1", "w3", "w2")


def kernel(**inputs):
    import numpy as np
    import concourse.bacc as bacc
    from concourse.bass_utils import run_bass_kernel_spmd

    nc = bacc.Bacc("TRN2", target_bir_lowering=False, num_devices=1)
    arrays, args = {}, {}
    for name in INPUTS:
        a = np.ascontiguousarray(inputs[name])
        arrays[f"in_{name}"] = a
        args[name] = nc.dram_tensor(f"in_{name}", a.shape, mybir.dt.from_np(a.dtype), kind="ExternalInput").ap()
    out = nc.dram_tensor("out_y", (1, N_LAT, D), F32, kind="ExternalOutput").ap()
    hybrid_block(nc, out=out, **args)
    return run_bass_kernel_spmd(nc, [arrays], core_ids=[0]).results[0]["out_y"]
```

```python
from contextlib import ExitStack

import concourse.bass as bass
from concourse import mybir

F32 = mybir.dt.float32
I32 = mybir.dt.int32
ALU = mybir.AluOpType
ACT = mybir.ActivationFunctionType
AX = mybir.AxisListType
ds = bass.ds

P = 128
D = 1024
J = D // P
N_CTX = 256
N_LAT = 256
T = N_CTX + N_LAT
C = T // P
C_CTX = N_CTX // P
H_A = 4
H_C = 8
CONV = 5
E = 16
GROUPS = 4
F = 512
FT = F // P
WORK = 12334
EPS = 1e-6
FAR = 1e30
N_PARAMS = 8
N_TURNED = 16
PASSES = 24
MOD_QK, MOD_DELTA, MOD_LAST = 4, 8, 20
RING = 6
ORDER = ([0, 1, 2, 3], [1, 0, 3, 2])
IN_GROUPS = ([0, 1, 2, 3, 7, 4, 5, 6], [0, 2, 4, 6, 8, 1, 3, 5, 7, 9])
LEVELS = [1, 2, 4, 8, 16, 32, 64]
GATE_I, GATE_F, GATE_B, GATE_A = range(4)
Q_G, Q_WI, Q_EM, Q_AS, Q_NGC, Q_EGC, Q_NEGC, Q_EKD, Q_BETA, Q_BKD = range(10)


def hybrid_block(nc, x, c, ctx, c_ctx, w_mod, b_mod, norm_mix, norm_ffn, norm_final,
                 ab_w_in, ab_i_bias, ab_f_bias, ab_conv, ab_a_log, ab_dt_bias, ab_norm_a, ab_norm_b,
                 ab_w_out, c_w_in, c_f_bias, c_lb_raw, c_norm, c_w_out, w_router, router_bias,
                 w1, w3, w2, out):
    with ExitStack() as stack:
        def sb(name, shape, dt=F32):
            return stack.enter_context(nc.sbuf_tensor(name, shape, dt))

        def sem(name):
            return stack.enter_context(nc.semaphore(name))

        bank = [stack.enter_context(nc.psum_tensor(f"bank{i}", [P, 512], F32)) for i in range(8)]

        ring = [sb(f"ring{i}", [P, 4096]) for i in range(RING)]
        xT = sb("xT", [P, J, T])
        uT = sb("uT", [P, J, T])
        featsT = sb("featsT", [P, 8, T])
        ident = sb("ident", [P, P])
        ones = sb("ones", [P, P])
        ahead = sb("ahead", [P, 2, P])
        level = sb("level", [P, 2, len(LEVELS), P])
        slot_of = sb("slot_of", [P, C, 2], I32)
        craw = sb("craw", [P, 2, J])
        csil = sb("csil", [P, J, 2])
        modv = sb("modv", [P, 2, 6, 2, J])
        bmod = sb("bmod", [P, 2, 6, J])
        nmix = sb("nmix", [P, 2, J])
        nffn = sb("nffn", [P, 2, J])
        nfin = sb("nfin", [P, J])
        coef = sb("coef", [P, 2, J])
        rstd = sb("rstd", [P, T])
        gbias = sb("gbias", [H_A, 4, 2])
        ends = sb("ends", [H_A, 4, 2, C])
        cols = sb("cols", [P, 10 * 32])
        taps_w = sb("taps_w", [P, CONV, 12])
        gain_h = sb("gain_h", [P, 8])
        gain_c = sb("gain_c", [P, 8])
        ssq = sb("ssq", [P, 8 * C])
        small = sb("small", [P, 48])
        epsv = sb("epsv", [P, 1])
        forget = sb("forget", [P, 4, 2, H_C])
        w_r = sb("w_r", [P, J, E])
        bias_r = sb("bias_r", [P, E])
        steps = sb("steps", [1, 2, PASSES + 4], I32)
        work = sb("work", [P, WORK])

        def area(start, *shape):
            n = 1
            for s in shape:
                n *= s
            flat = work[:, start:start + n]
            names = "abcd"[:len(shape)]
            if len(shape) == 1:
                return flat
            return flat.rearrange("p (%s) -> p %s" % (" ".join(names), " ".join(names)),
                                  **{k: v for k, v in zip(names, shape)})

        modrow = rstd[0:2, :]
        modvs = modv[:, :, :, :, :].rearrange("p l v w j -> p (l v) w j")
        gate = featsT[:, :, :].rearrange("p h (c e) -> p h c e", c=C)
        qT = area(0, H_A, T)
        kT = area(2048, H_A, T)
        va = area(4096, C, H_A, P + 1)
        vb = area(4096, C, H_A, P)
        bc = area(6160, 2, 1032)
        qh = area(8224, T)
        kh = area(8736, T)
        w_gate = featsT[:, 0, 0:J * 32].rearrange("p (k n) -> p k n", k=J)
        grow = rstd[0:32, :]
        grow4 = area(8224, 4, 2, T)[0:H_A]
        rows_low = featsT[0:H_A, :, :].rearrange("h (k d) t -> h k d t", d=2)
        rows_high = area(4096, 4, 2, T)[0:H_A]

        def row(kind):
            return rows_low[:, kind, :, :] if kind < 4 else rows_high[:, kind - 4, :, :]

        ka = area(9248, 6, P)
        cell = area(10016, 2, 3, P + 1)
        num = area(10790, 8, P + 1)
        hsum = area(11822, C, P)
        raw = area(6160, 2, 2, 260)
        taps = area(7200, 2, 512)
        turned_v = area(9248, 2, 512)
        ktok = area(9248, C, P)
        lower = area(9760, 2, C, P)
        state_b = area(10784, 2, P)
        z_b = area(11040, 2, P)
        vn_b = area(11296, 2, P)
        vd_b = area(11552, 2, P)
        osum = area(11808, C, P)
        u_flat = uT[:, :, :].rearrange("p a b -> p (a b)")
        inv = u_flat[:, 0:2048].rearrange("p (d x c e) -> p d x c e", d=2, x=2, c=C)
        masked = u_flat[:, 2048:3072].rearrange("p (d c e) -> p d c e", d=2, c=C)
        half = u_flat[:, 3072:4096].rearrange("p (d c e) -> p d c e", d=2, c=C)
        x_in = uT[:, :, :].rearrange("p a b -> p (a b)").rearrange("p (a b) -> p a b", a=C)

        q1 = area(0, 4, N_LAT)
        z1 = area(1024, 2, 4, T)
        v1 = area(5120, C, 4, P)
        decay = area(7168, 2, T)
        ks = area(8192, 2, T)
        qp = area(9216, 2, N_LAT)
        tot = area(9728, 2, T)
        att1 = area(10752, 2, 2, P)
        kd1 = area(7168, 2, 3, P)
        state1 = area(11264, 2, 3, P)
        o1 = area(12032, 2, P)
        out_sb = area(0, 2, D)

        h_tok = featsT[:, :, :].rearrange("p h t -> p (h t)").rearrange("p (c j e) -> p c j e", c=C, j=J)
        h_row = featsT[:, :, :].rearrange("p h t -> p (h t)").rearrange("p (c n) -> p c n", c=C)
        back = (h_row, uT[:, :, :].rearrange("p a b -> p (a b)").rearrange("p (c n) -> p c n", c=C))
        he = area(0, 2, J, P)
        xs = area(2048, 2, D)
        act_e = area(5120, FT, P)
        silu_e = area(5632, FT, P)
        ye = area(6144, 2, D)
        table = area(8440, PASSES + 2)
        r_rows = area(8500, T)[0:E]
        scores = area(9012, C, E)
        sel = area(9076, C, E)
        first = area(9140, C, E)
        second = area(9204, C, E)
        tmp = area(9268, C, E)
        tmp2 = area(9332, C, E)
        taken = area(9396, C, E)
        rank = area(9460, C, E)
        pairs = area(9524, C * GROUPS, 6)
        g_score = area(9620, C, GROUPS)
        g_pick = area(9636, C, GROUPS)
        top = area(9652, C)
        low = area(9656, C)
        count = area(9660, E)
        n_pass = area(9676, E)
        upto_e = area(9692, E)
        start_e = area(9708, E)
        pos = area(9724, C, 2)
        wts = area(9732, C, 2)
        total = area(9740, C)
        ids_f = area(10170, (PASSES + 2), E)
        before = area(10600, P)
        iota = area(10728, P)

        slot_in = [sem(f"slot_in{i}") for i in range(RING)]
        x_loaded = sem("x_loaded")
        c_loaded = sem("c_loaded")
        ident_ready = sem("ident_ready")
        params_loaded = sem("params_loaded")
        const_step = sem("const_step")
        consts_ready = sem("consts_ready")
        x_turned = sem("x_turned")
        turned_loaded = sem("turned_loaded")
        group_taken = sem("group_taken")
        taps_step = sem("taps_step")
        conv_done = sem("conv_done")
        gates_summed = sem("gates_summed")
        gates_copied = sem("gates_copied")
        gates_moved = sem("gates_moved")
        row_dve = sem("row_dve")
        row_act = sem("row_act")
        rows_ready = sem("rows_ready")
        rows_stored = sem("rows_stored")
        cols_turned = sem("cols_turned")
        cols_act = sem("cols_act")
        cols_dve = sem("cols_dve")
        va_ones = sem("va_ones")
        qk_staged = sem("qk_staged")
        bc_loaded = [sem(f"bc_loaded{i}") for i in range(2)]
        scores_ready = sem("scores_ready")
        kh_turned = sem("kh_turned")
        ka_ready = sem("ka_ready")
        arg_ready = sem("arg_ready")
        exp_ready = sem("exp_ready")
        w_ready = sem("w_ready")
        update_ready = sem("update_ready")
        cell_step = sem("cell_step")
        intra_ready = sem("intra_ready")
        inter_ready = sem("inter_ready")
        intra_copied = sem("intra_copied")
        joined = sem("joined")
        head_step = sem("head_step")
        raw_zeroed = sem("raw_zeroed")
        silu_done = sem("silu_done")
        v_turned = sem("v_turned")
        v_taken = sem("v_taken")
        qk_squared = sem("qk_squared")
        qk_summed = sem("qk_summed")
        qk_root = sem("qk_root")
        qk_step = sem("qk_step")
        qk_normed = sem("qk_normed")
        ktok_ready = sem("ktok_ready")
        lower_ready = sem("lower_ready")
        att_ready = sem("att_ready")
        mask_ready = sem("mask_ready")
        x0_turned = sem("x0_turned")
        x0_ready = sem("x0_ready")
        bx_ready = sem("bx_ready")
        bx_copied = sem("bx_copied")
        xbx_ready = sem("xbx_ready")
        inv_ready = sem("inv_ready")
        carried_ready = sem("carried_ready")
        z_ready = sem("z_ready")
        xz_ready = sem("xz_ready")
        v_ready = sem("v_ready")
        outer_ready = sem("outer_ready")
        state_ready = sem("state_ready")
        o_step = sem("o_step")
        ms_ready = sem("ms_ready")
        ms_root = sem("ms_root")
        y_step = sem("y_step")
        y_ready = sem("y_ready")
        y_turned = sem("y_turned")
        feats_ready = sem("feats_ready")
        out_summed = sem("out_summed")
        x_updated = sem("x_updated")
        forget_step = sem("forget_step")
        forget_act = sem("forget_act")
        sig_ready = sem("sig_ready")
        f_ready = sem("f_ready")
        tot_step = sem("tot_step")
        level_ready = sem("level_ready")
        qp_updated = sem("qp_updated")
        ks_updated = sem("ks_updated")
        cp_done = sem("cp_done")
        att1_zeroed = sem("att1_zeroed")
        kd_turned = sem("kd_turned")
        kd_ready = sem("kd_ready")
        update1_ready = sem("update1_ready")
        state1_step = sem("state1_step")
        o1_ready = sem("o1_ready")
        o1_copied = sem("o1_copied")
        out_turned = sem("out_turned")
        out_copied = sem("out_copied")
        out_stored = sem("out_stored")
        head_done = sem("head_done")
        xT_act = sem("xT_act")
        xT_dve = sem("xT_dve")
        csil_ready = sem("csil_ready")
        mod_summed = sem("mod_summed")
        row_copied = sem("row_copied")
        mod_spread = sem("mod_spread")
        tile_summed = sem("tile_summed")
        mod_ready = sem("mod_ready")
        coef_step = sem("coef_step")
        coef_ready = sem("coef_ready")
        sq_ready = sem("sq_ready")
        ssq_ready = sem("ssq_ready")
        root_ready = sem("root_ready")
        rstd_step = sem("rstd_step")
        xn_ready = sem("xn_ready")
        u_ready = sem("u_ready")

        expert_in = [sem(f"expert_in{i}") for i in range(RING)]
        logits_summed = sem("logits_summed")
        scored = sem("scored")
        logits_copied = sem("logits_copied")
        logits_turned = sem("logits_turned")
        route_step = sem("route_step")
        chosen = sem("chosen")
        counted = sem("counted")
        rows_chosen = sem("rows_chosen")
        tabled = sem("tabled")
        tok_turned = sem("tok_turned")
        tok_copied = sem("tok_copied")
        iota_ready = sem("iota_ready")
        pass_filled = sem("pass_filled")
        tok_stored = sem("tok_stored")
        xs_in = [sem(f"xs_in{i}") for i in range(2)]
        xs_turned = sem("xs_turned")
        ye_stored = sem("ye_stored")
        back_in = [sem(f"back_in{i}") for i in range(C)]
        weighed = sem("weighed")
        both_ready = sem("both_ready")
        both_turned = sem("both_turned")
        he_copied = sem("he_copied")
        up_summed = sem("up_summed")
        silu_ready = sem("silu_ready")
        gated = sem("gated")
        down_summed = sem("down_summed")
        ye_copied = sem("ye_copied")

        counted_by_pe = (inter_ready, outer_ready, bx_ready, intra_ready, update_ready, update1_ready, xz_ready,
                         down_summed, o1_ready, kh_turned, carried_ready)
        counted_by_dve = (state1_step, cell_step, head_done, joined, cp_done, o1_copied, gated, o_step, state_ready)
        counted_by_act = (row_copied, intra_copied, ka_ready, ye_copied, ye_stored)
        counted_by_pool = (mask_ready,)

        def one_up(eng, semaphores):
            for s in semaphores:
                eng.nop().then_inc(s, 1)

        def by_feature(w):
            return w.rearrange("(p k) n -> p k n", k=J)

        slots = []
        mods = [("mod", q // 12, q % 12, 0, by_feature(w_mod[q // 12])[:, :, 512 * (q % 12):512 * (q % 12) + 512])
                for q in range(24)]
        slots += mods[:MOD_QK]
        for layer in range(2):
            wi = by_feature((ab_w_in if layer == 0 else c_w_in)[0])
            groups = IN_GROUPS[layer]
            slots += [("in", layer, g, 0, wi[:, :, 512 * g:512 * g + 512]) for g in groups]
            wo = (ab_w_out if layer == 0 else c_w_out)[0].rearrange("(h p) n -> p h n", p=P)
            slots += mods[MOD_QK:MOD_LAST] if layer == 0 else []
            slots += [("out", layer, h, 0, wo[:, 4 * h:4 * h + 4, :]) for h in range(2)]
            slots += mods[MOD_LAST:] if layer == 0 else []
        slot_at = {s[:4]: n for n, s in reversed(list(enumerate(slots)))}

        def slot(n, k):
            return ring[n % RING][:, :].rearrange("p (k m) -> p k m", k=k)

        def slot_arrived(eng, n, turn=0):
            eng.wait_ge(slot_in[n % RING], 16 * (n // RING + 1) + 16 * turn)

        def shift(n):
            return modv[:, n // 2, 0 if n % 2 == 0 else 3, :, :]

        def slot_free(eng, n):
            kind, layer, g = slots[n][:3]
            if kind == "mod":
                eng.wait_ge(mod_summed, 12 * layer + g + 1)
            elif kind == "in" and layer == 0:
                eng.wait_ge(tile_summed, 4 * (IN_GROUPS[0].index(g) + 1))
            elif kind == "in":
                k = IN_GROUPS[1].index(g)
                eng.wait_ge(tile_summed, 32 + 18 * (k // 5) + (4, 8, 12, 16, 18)[k % 5])
            elif kind == "out":
                eng.wait_ge(out_summed, 8 * layer + 8)

        pass_in = nc.dram_tensor("pass_in", [P * PASSES, D], F32, kind="Internal").ap()
        pass_out = nc.dram_tensor("pass_out", [P * PASSES, D], F32, kind="Internal").ap()
        row_dram = nc.dram_tensor("row_dram", [2, H_A, 1032], F32, kind="Internal").ap()

        def col(q, d, ch, h):
            return cols[:, ds(32 * q + 16 * d + 4 * ch + h, 1)]

        def tot_at(l):
            return T - (T >> (l - 1))

        def by_block(t, l):
            return t.rearrange("p (j two r) -> p j two r", two=2, r=1 << l)

        def totals_of(d, l, lat=False):
            t = decay[:, d, :] if l == 0 else tot[:, d, tot_at(l):tot_at(l) + (T >> l)]
            t = t.rearrange("p (j two) -> p j two", two=2)
            return t[:, N_CTX >> (l + 1):, :] if lat else t

        expert_slots = [[(slot_at["in", 1, 0, 0] + 3 * half + k) % RING for k in range(3)] for half in range(2)]
        assert slot_at["in", 1, 0, 0] % RING == len(slots) % RING

        def seen(layer):
            return C_CTX * layer, N_CTX * layer

        def pairs_of(eng, layer):
            lo, hi = E // 2, PASSES // 2
            end = eng.value_load(steps[0:1, layer, PASSES + 2:PASSES + 3], min_val=lo * (layer + 1), max_val=hi * (layer + 1))
            if layer == 0:
                return 0, end
            return eng.value_load(steps[0:1, 0, PASSES + 2:PASSES + 3], min_val=lo, max_val=hi), end

        def within(eng, i, first):
            if isinstance(first, int):
                return i
            return eng.snap(nc.s_assert_within(i - 2 * first, 0, PASSES - 1,
                                               skip_runtime_bounds_check_because="a layer has no more than PASSES passes"))

        block = stack.enter_context(nc.Block())

        @block.sync
        def _(sp):
            for half, src in ((0, ctx), (1, x)):
                sp.dma_start(x_in[:, 2 * half:2 * half + 2, :],
                             src[0].rearrange("(a p) d -> p a d", p=P)).then_inc(x_loaded, 16)

            def load(n):
                if n >= RING:
                    slot_free(sp, n - RING)
                sp.dma_start(slot(n, slots[n][4].shape[1]), slots[n][4]).then_inc(slot_in[n % RING], 16)

            for n in range(slot_at["in", 1, 0, 0]):
                if n == RING:
                    sp.wait_ge(mod_spread, 32 * MOD_QK)
                load(n)
            filler = level[:, :, :, :].rearrange("p d l t -> p (d l t)")[:, 0:D]
            for rows in (pass_in, pass_out):
                for n in range(PASSES):
                    sp.dma_start(rows[P * n:P * n + P, :], filler).then_inc(pass_filled, 16)
            def load_expert(layer, e, half, what):
                w, k = ((w1, J), (w3, J), (w2, FT))[what]
                r = expert_slots[half][what]
                if isinstance(e, int):
                    src = w[layer, e]
                else:
                    src = w[layer, ds(e, 1)].rearrange("o d f -> (o d) f")
                sp.dma_start(ring[r][:, :], src.rearrange("(p k) f -> p (k f)", k=k)).then_inc(expert_in[r], 16)

            def experts(layer, last_slot):
                for what in range(3):
                    slot_free(sp, last_slot - RING + 1 + what)
                    load_expert(layer, 0, 0, what)
                for what in range(3):
                    slot_free(sp, last_slot - RING + 4 + what)
                sp.wait_ge(tabled, layer + 1)
                sp.wait_ge(tok_stored, 16 * (8 + 4 * layer))
                for half in range(2):
                    sp.dma_start(xs[:, half, :], pass_in[P * half:P * half + P, :]).then_inc(xs_in[half], 16)
                e = sp.value_load(steps[0:1, layer, 1:2], min_val=0, max_val=E - 1)
                for what in range(3):
                    load_expert(layer, e, 1, what)
                first, end = pairs_of(sp, layer)
                with sp.Fori(first + 1, end) as m:
                    for half in range(2):
                        e = sp.value_load(steps[0:1, layer, ds(within(sp, 2 * m + half, first), 1)], min_val=0, max_val=E - 1)
                        sp.wait_ge(xs_turned, 2 * m + half - 1 + layer)
                        sp.dma_start(xs[:, half, :], pass_in[ds(within(sp, 2 * m + half, first) * P, P), :]).then_inc(
                            xs_in[half], 16)
                        sp.wait_ge(up_summed, 2 * m + half - 1)
                        for what in range(2):
                            load_expert(layer, e, half, what)
                        sp.wait_ge(down_summed, 1 + 2 * m + half - 1)
                        load_expert(layer, e, half, 2)
                sp.wait_ge(xs_turned, 2 * end + layer)
                sp.dma_start(xs[:, 0, :], pass_in[0:P, :]).then_inc(xs_in[0], 16)

            experts(0, 33)
            sp.wait_ge(x_updated, 9)
            for n in range(34, 46):
                if n - RING >= 34:
                    slot_free(sp, n - RING)
                sp.dma_start(slot(n, slots[n][4].shape[1]), slots[n][4]).then_inc(slot_in[n % RING], 16)
            experts(1, 45)
            for ch in range(2):
                sp.wait_ge(out_copied, 2 * ch + 2)
                sp.dma_start(out[0, P * ch:P * ch + P, :], out_sb[:, ch, :]).then_inc(out_stored, 16)
            sp.wait_ge(out_stored, 32)

        @block.gpsimd
        def _(pool):
            one_up(pool, counted_by_pool)
            n_step = [0]

            def step(ins):
                ins.then_inc(const_step, 1)
                n_step[0] += 1

            def after_step():
                pool.wait_ge(const_step, n_step[0])

            step(pool.memset(ident[:, :], 0.0))
            after_step()
            pool.affine_select(out=ident[:, :], in_=ident[:, :], compare_op=ALU.not_equal, fill=1.0,
                               base=0, pattern=[[-1, P]], channel_multiplier=1).then_inc(ident_ready, 1)
            pool.memset(ones[:, :], 1.0)
            step(pool.memset(ahead[:, :, :], 0.0))
            step(pool.memset(level[:, :, :, :], 0.0))
            after_step()
            for b in LEVELS:
                v = level[:, :, LEVELS.index(b), :].rearrange("p d (j h r) -> p d j h r", h=2, r=b)
                step(pool.memset(v[:, 0, :, 1, :], 1.0))
                step(pool.memset(v[:, 1, :, 0, :], 1.0))
            step(pool.affine_select(out=ahead[:, 0, :], in_=ahead[:, 0, :], compare_op=ALU.is_ge, fill=-FAR,
                                    base=0, pattern=[[1, P]], channel_multiplier=-1))
            step(pool.affine_select(out=ahead[:, 1, :], in_=ahead[:, 1, :], compare_op=ALU.is_ge, fill=-FAR,
                                    base=0, pattern=[[-1, P]], channel_multiplier=1))
            after_step()
            for b in LEVELS:
                n = P // (2 * b)
                v = level[:, :, LEVELS.index(b), :].rearrange("p d (j h r) -> p d j h r", h=2, r=b)
                for d, lo in ((0, 0), (1, b)):
                    part = v[:, d, :, 1 - d, :]
                    step(pool.affine_select(out=part, in_=part, compare_op=ALU.is_ge, fill=0.0, base=-lo,
                                            pattern=[[-2 * b, n], [0, b]], channel_multiplier=1))
            after_step()
            for b in LEVELS:
                n = P // (2 * b)
                v = level[:, :, LEVELS.index(b), :].rearrange("p d (j h r) -> p d j h r", h=2, r=b)
                for d, lo in ((0, 0), (1, b)):
                    part = v[:, d, :, 1 - d, :]
                    step(pool.affine_select(out=part, in_=part, compare_op=ALU.is_ge, fill=0.0, base=lo + b - 1,
                                            pattern=[[2 * b, n], [0, b]], channel_multiplier=-1))
            after_step()
            pool.memset(epsv[:, :], EPS)
            pool.memset(ssq[:, :], 0.0).then_inc(consts_ready, 1)
            turned = [(gbias[:, 0, :], ab_i_bias[0].rearrange("d h -> h d")),
                      (gbias[:, 1, :], ab_f_bias[0].rearrange("d h -> h d")),
                      (gbias[:, 2, :], ab_dt_bias[0].rearrange("d h -> h d")),
                      (gbias[:, 3, :], ab_a_log[0].rearrange("d h -> h d")),
                      (gain_h[:, 0:4], ab_norm_a[0].rearrange("(h p) -> p h", p=P)),
                      (gain_h[:, 4:8], ab_norm_b[0].rearrange("(h p) -> p h", p=P)),
                      (gain_c[:, :], c_norm[0].rearrange("(h p) -> p h", p=P))]
            for d in range(2):
                turned += [(forget[:, 0, d, :], c_f_bias[0, d].rearrange("(h p) -> p h", p=P)),
                           (forget[:, 2, d, :], c_lb_raw[0, d].rearrange("(h p) -> p h", p=P))]
            turned += [(taps_w[:, k, :], ab_conv[0, k].rearrange("(g p) -> p g", p=P)) for k in range(CONV)]
            for dst, src in turned:
                pool.dma_start(dst, src, allow_slow_non_contiguous=True).then_inc(turned_loaded, 16)
            assert len(turned) == N_TURNED

            def stage_heads():
                with pool.Fori(0, H_A) as h:
                    pool.wait_ge(kh_turned, 1 + h)
                    pool.tensor_copy(kh, kT[:, ds(h, 1), :].rearrange("p a t -> p (a t)")).then_inc(qk_staged, 1)
                    pool.wait_ge(inter_ready, 1 + 2 * h)
                    pool.tensor_copy(qh, qT[:, ds(h, 1), :].rearrange("p a t -> p (a t)")).then_inc(qk_staged, 1)

            pool.wait_ge(cols_turned, 1)
            pool.wait_ge(rows_stored, 64)
            pool.memset(va[:, :, :, P:P + 1], 1.0).then_inc(va_ones, 1)
            pool.wait_ge(group_taken, 12)
            stage_heads()

            def delta():
                with pool.Fori(0, H_A) as h:
                    pool.wait_ge(carried_ready, 1 + 6 * h)
                    pool.tensor_copy(kh, kT[:, ds(h, 1), :].rearrange("p a t -> p (a t)")).then_inc(qk_staged, 1)
                    pool.wait_ge(outer_ready, 1 + 8 * h)
                    pool.tensor_copy(qh, qT[:, ds(h, 1), :].rearrange("p a t -> p (a t)")).then_inc(qk_staged, 1)
                    for l in range(len(LEVELS)):
                        for d in range(2):
                            if l == 0:
                                pool.wait_ge(lower_ready, 8 * h + 4 * d + 4)
                                pool.wait_ge(bx_ready, 1 + 12 * h)
                            elif l == 1:
                                pool.wait_ge(inv_ready, 14 * h + d + 1)
                            else:
                                pool.wait_ge(bx_ready, 1 + 12 * h + 2 * (l - 2) + d + 1)
                            pool.tensor_tensor(masked[:, d, :, :], lower[:, d, :, :],
                                               level[:, d, l, :].unsqueeze(1).broadcast_to([P, C, P]),
                                               ALU.mult).then_inc(mask_ready, 1)

            pool.wait_ge(bc_loaded[0], 16 * 3)
            pool.wait_ge(head_done, 1 + H_A)
            pool.wait_ge(intra_ready, 1 + H_A)
            for b in range(2):
                for o in (0, 258):
                    ins = pool.memset(raw[:, b, :, o:o + 2], 0.0)
            ins.then_inc(raw_zeroed, 1)
            for j in range(8):
                if j == 0:
                    pool.wait_ge(tile_summed, 32)
                pool.wait_ge(silu_done, j + 1)
                t = (qT, kT)[j // 4][:, j % 4, :]
                pool.tensor_tensor(uT[:, j, :], t, t, ALU.mult).then_inc(qk_squared, 1)
            pool.wait_ge(qk_normed, 8)
            delta()

            def experts(layer):
                c0 = seen(layer)[0]
                pool.wait_ge(x_updated, 2 * J * layer + J)
                pool.iota(iota, [[1, P]], base=0, channel_multiplier=0, allow_small_or_imprecise_dtypes=True)
                pool.affine_select(out=before, in_=ones[:, :], compare_op=ALU.is_gt, fill=0.0,
                                   base=0, pattern=[[1, P]], channel_multiplier=-1).then_inc(iota_ready, 1)
                pool.wait_ge(rows_chosen, layer + 1)
                pool.wait_ge(pass_filled, 16 * 2 * PASSES)
                for ch in range(c0, C):
                    pool.wait_ge(tok_copied, 8 * layer + 2 * (ch - c0) + 2)
                    for k in range(2):
                        pool.indirect_dma_start(pass_in[:, :], bass.IndirectOffsetOnAxis(ap=slot_of[:, ch, k:k + 1], axis=0),
                                                h_row[:, ch, :], None).then_inc(tok_stored, 16)
                pool.wait_ge(tabled, layer + 1)
                end = pairs_of(pool, layer)[1]
                pool.wait_ge(ye_stored, 1 + 32 * end)
                pool.tensor_tensor(small[:, 46:47], epsv[:, :], epsv[:, :], ALU.mult)
                pool.wait_ge(tok_stored, 16 * (8 + 4 * layer))
                for ch in range(c0, C):
                    for k in range(2):
                        pool.indirect_dma_start(back[k][:, ch, :], None, pass_out[:, :],
                                                bass.IndirectOffsetOnAxis(ap=slot_of[:, ch, k:k + 1], axis=0)).then_inc(
                                                    back_in[ch], 16)

            def hgrn(part):
                with pool.Fori(0, 4) as i:
                    h = 4 * part + i
                    pool.wait_ge(f_ready, 6 * h + 6)
                    pool.wait_ge(state1_step, 1 + 6 * h)

                    def totals(l):
                        src = decay if l == 1 else tot[:, :, tot_at(l - 1):]
                        n = T >> l
                        if l > 1:
                            pool.wait_ge(tot_step, 7 * h + l - 1)
                        pool.tensor_tensor(tot[:, :, tot_at(l):tot_at(l) + n], src[:, :, 0:2 * n:2], src[:, :, 1:2 * n:2],
                                           ALU.mult).then_inc(tot_step, 1)

                    totals(1)
                    totals(2)
                    for l in range(len(LEVELS)):
                        if l:
                            pool.wait_ge(tot_step, 7 * h + l)
                        for d in range(2):
                            pool.wait_ge(level_ready, 16 * h + 2 * l + d + 3)
                            if l:
                                pool.wait_ge(ks_updated, 14 * h + 2 * (l - 1) + d + 1)
                            blocks, decays = by_block(ks[:, d, :], l), totals_of(d, l)
                            pool.tensor_tensor(blocks[:, :, d, :], blocks[:, :, d, :],
                                               decays[:, :, 1 - d:2 - d].broadcast_to([P, T >> (l + 1), 1 << l]),
                                               ALU.mult).then_inc(ks_updated, 1)
                        if l + 3 <= len(LEVELS):
                            totals(l + 3)

            experts(0)
            pool.wait_ge(x_updated, 16)
            pool.memset(att1[:, :, :, :], 0.0).then_inc(att1_zeroed, 1)
            hgrn(0)
            hgrn(1)
            experts(1)

        @block.scalar
        def _(act):
            one_up(act, counted_by_act)
            loads = [(bmod[:, 0, :, :], b_mod[0].rearrange("(s p j) -> p s j", s=6, j=J)),
                     (bmod[:, 1, :, :], b_mod[1].rearrange("(s p j) -> p s j", s=6, j=J)),
                     (nmix[:, :, :], norm_mix.rearrange("l (p j) -> p l j", j=J)),
                     (nffn[:, :, :], norm_ffn.rearrange("l (p j) -> p l j", j=J)),
                     (nfin[:, :], norm_final.rearrange("(p j) -> p j", j=J)),
                     (w_r[:, :, :], by_feature(w_router)),
                     (bias_r[:, :], router_bias.unsqueeze(0).broadcast_to([P, E])),
                     (w_gate[:, :, :], by_feature(ab_w_in[0])[:, :, 4096:4128])]
            assert len(loads) == N_PARAMS
            act.dma_start(craw[:, 0, :], c[0].rearrange("(p j) -> p j", j=J)).then_inc(c_loaded, 16)
            act.dma_start(craw[:, 1, :], c_ctx.rearrange("(p j) -> p j", j=J)).then_inc(c_loaded, 16)
            act.wait_ge(c_loaded, 32)
            act.activation(csil[:, :, :], craw[:, :, :].rearrange("p w j -> p j w"), ACT.Silu).then_inc(csil_ready, 1)
            for j in range(0, J, 2):
                act.wait_ge(x_turned, j + 1)
                act.activation(xT[:, j, :], bank[j % 4][:, :], ACT.Copy).then_inc(xT_act, 1)

            def load_parameters():
                for dst, src in loads:
                    act.dma_start(dst, src).then_inc(params_loaded, 16)

            def squares(n, t0):
                for j in range(J):
                    if n == 0 and j == 0:
                        act.wait_ge(x_turned, J)
                        act.wait_ge(xT_act, J // 2)
                        act.wait_ge(xT_dve, J // 2)
                    if n:
                        act.wait_ge(x_updated, J * (n - 1) + j + 1)
                    act.activation(uT[:, j, t0:], xT[:, j, t0:], ACT.Square).then_inc(sq_ready, 1)

            def root(n, t0):
                act.wait_ge(rstd_step, 2 * n + 1)
                act.activation(rstd[:, t0:], rstd[:, t0:], ACT.Sqrt).then_inc(root_ready, 1)

            def modulate(n, t0):
                for j in range(J):
                    act.wait_ge(xn_ready, J * n + j + 1)
                    act.wait_ge(coef_ready, n + 1)
                    for who, a, b in ((1, t0, N_CTX), (0, N_CTX, T)):
                        if a < b:
                            ins = act.activation(uT[:, j, a:b], uT[:, j, a:b], ACT.Identity,
                                                 scale=coef[:, who, j:j + 1], bias=shift(n)[:, who, j:j + 1])
                    ins.then_inc(u_ready, 1)

            def norm(n, t0):
                squares(n, t0)
                root(n, t0)
                modulate(n, t0)

            def modulation_row(q, b, v, o, row=modrow):
                act.wait_ge(mod_summed, q + 1)
                if not isinstance(q, int) or q >= MOD_QK:
                    act.wait_ge(mod_spread, 32 * q)
                act.activation(row, bank[b][0:2, :], ACT.Copy).then_inc(row_copied, 1)
                act.wait_ge(row_copied, 1 + q + 1)
                for w in range(2):
                    act.dma_start(modvs[o:o + 64, v, w, :], row[w:w + 1, :].rearrange(
                        "w (p v j) -> w p v j", j=J, v=1)).then_inc(mod_spread, 16)

            def modulation(start, end):
                for q in range(start, end):
                    modulation_row(q, 6 + q % 2, ds(q // 2, 1), 64 * (q % 2))

            def take(n, dst, func=ACT.Copy, scale=1.0):
                act.wait_ge(tile_summed, n + 1)
                act.activation(dst, bank[n % 2][:, :], func, scale=scale).then_inc(group_taken, 1)

            def take_queries_keys(start, end):
                for n in range(start, end):
                    take(n, (qT, kT)[n // 4][:, n % 4, :], scale=(P ** -0.5, 1.0)[n // 4])

            def gate_rows():
                act.wait_ge(gates_summed, 1)
                act.activation(grow[:, :], bank[2][0:32, :], ACT.Copy).then_inc(gates_copied, 1)
                act.wait_ge(gates_copied, 1)
                for kind in range(4):
                    for d in range(2):
                        act.dma_start(grow4[:, kind, d, :], grow[8 * kind + 4 * d:8 * kind + 4 * d + 4, :]).then_inc(gates_moved, 16)
                take_queries_keys(0, 2)
                act.wait_ge(gates_moved, 16 * 8)
                act.activation(row(6), grow4[:, GATE_B, :, :], ACT.Sigmoid).then_inc(row_act, 1)
                act.wait_ge(turned_loaded, 16 * N_TURNED)
                act.activation(gbias[:, 3, :], gbias[:, 3, :], ACT.Exp).then_inc(row_act, 1)
                act.wait_ge(row_dve, 5)
                act.activation(rows_low[:, 0:2, :, :], rows_low[:, 0:2, :, :], ACT.Exp, scale=-1.0).then_inc(row_act, 1)
                act.wait_ge(row_act, 3)
                act.activation(rows_low[:, 0:2, :, :], rows_low[:, 0:2, :, :], ACT.Ln, bias=1.0).then_inc(row_act, 1)

            def store_rows():
                act.wait_ge(rows_ready, 1)
                for kind, which, end in ((0, 7, 0), (1, 4, 3)):
                    act.dma_start(row_dram[kind, :, 0:2 * T], row(which).rearrange("h d t -> h (d t)")).then_inc(
                        rows_stored, 16)
                    act.dma_start(row_dram[kind, :, 2 * T:2 * T + 8], ends[:, end, :, :].rearrange("h d c -> h (d c)")).then_inc(
                        rows_stored, 16)

            def gate_cols():
                act.wait_ge(cols_turned, 1)
                src = bank[3][:, 0:224]
                act.activation(cols[:, 32 * Q_G:32 * Q_G + 32], src[:, 0:32], ACT.Copy).then_inc(cols_act, 1)
                act.activation(cols[:, 32 * Q_NGC:32 * Q_NGC + 32], src[:, 128:160], ACT.Copy, scale=-1.0).then_inc(cols_act, 1)
                act.activation(cols[:, 32 * Q_BETA:32 * Q_BETA + 32], src[:, 192:224], ACT.Copy).then_inc(cols_act, 1)
                act.activation(cols[:, 32 * Q_WI:32 * Q_WI + 96], src[:, 32:128], ACT.Exp).then_inc(cols_act, 1)
                act.activation(cols[:, 32 * Q_EGC:32 * Q_EGC + 32], src[:, 128:160], ACT.Exp).then_inc(cols_act, 1)
                act.activation(cols[:, 32 * Q_EKD:32 * Q_EKD + 32], src[:, 160:192], ACT.Exp).then_inc(cols_act, 1)

            def mlstm():
                with act.Fori(0, H_A // 2) as i:
                    for half in range(2):
                        h = 2 * i + half
                        act.wait_ge(intra_ready, 1 + h)
                        act.wait_ge(cell_step, 1 + 6 * h)
                        act.dma_start(bc[:, 1 - half, :], row_dram[0, ds(2 * i + 1 if half == 0 else 2 - 2 * i, 1), :].broadcast_to(
                            [P, 1032])).then_inc(bc_loaded[1 - half], 16)
                        act.wait_ge(bc_loaded[half], 16 * i + 16)
                        act.activation(bc[:, half, 1024:1032], bc[:, half, 1024:1032], ACT.Exp).then_inc(exp_ready, 1)
                        act.wait_ge(kh_turned, 1 + h + 1)
                        act.wait_ge(update_ready, 1 + 2 * h)
                        for d in range(2):
                            for step in range(3):
                                ch = ORDER[d][step]
                                act.activation(ka[:, 3 * d + step, :], bank[3][:, P * ch:P * ch + P], ACT.Copy,
                                               scale=col(Q_AS, d, ch, h)).then_inc(ka_ready, 1)
                        for d in range(2):
                            act.wait_ge(arg_ready, 8 * h + 4 * d + 4)
                            part = bc[:, half, 512 * d:512 * d + 512]
                            act.activation(part, part, ACT.Exp).then_inc(exp_ready, 1)
                        act.wait_ge(intra_ready, 1 + h + 1)
                        act.wait_ge(head_done, 1 + h)
                        for b in range(3):
                            n = 3 if b < 2 else 2
                            act.activation(num[:, 3 * b:3 * b + n, :],
                                           bank[b][:, 0:129 * n].rearrange("p (n e) -> p n e", n=n),
                                           ACT.Copy).then_inc(intra_copied, 1)

            squares(0, 0)
            load_parameters()
            root(0, 0)
            for q in range(MOD_QK):
                modulation_row(q, 6 + q % 2, ds(q // 2, 1), 64 * (q % 2), work[0:2, 512 * q:512 * q + 512])
            modulate(0, 0)
            gate_rows()
            take_queries_keys(2, 8)
            store_rows()
            gate_cols()
            act.wait_ge(rows_stored, 64)
            act.dma_start(bc[:, 0, :], row_dram[0, 0:1, :].broadcast_to([P, 1032])).then_inc(bc_loaded[0], 16)
            act.wait_ge(va_ones, 1)
            for n in range(4):
                act.wait_ge(tile_summed, 8 + n + 1)
                act.activation(va[:, n, :, 0:P], bank[n % 2][:, :].rearrange("p (h e) -> p h e", h=H_A),
                               ACT.Copy).then_inc(group_taken, 1)
            for n in range(4):
                act.wait_ge(tile_summed, 12 + n + 1)
                act.activation(gate[:, 0:4, n, :], bank[n % 2][:, :].rearrange("p (h e) -> p h e", h=H_A),
                               ACT.Sigmoid).then_inc(group_taken, 1)
            mlstm()

            def project_b():
                act.wait_ge(head_done, 1 + H_A)
                act.wait_ge(qk_staged, 2 * H_A)
                for n in range(4):
                    act.wait_ge(tile_summed, 16 + n + 1)
                    act.activation(gate[:, 4:8, n, :], bank[n % 2][:, :].rearrange("p (h e) -> p h e", h=H_A),
                                   ACT.Silu).then_inc(group_taken, 1)
                act.wait_ge(raw_zeroed, 1)

                def silu(m):
                    act.wait_ge(conv_done, m + 1)
                    if m >= 10:
                        act.wait_ge(v_turned, m - 9)
                    dst = qT[:, m, :] if m < 4 else kT[:, m - 4, :] if m < 8 else turned_v[:, m % 2, :]
                    act.activation(dst, taps[:, m % 2, :], ACT.Silu).then_inc(silu_done, 1)

                def v_out(m):
                    act.wait_ge(v_turned, m - 7)
                    act.activation(vb[:, :, m - 8, :], bank[2 + m % 2][:, :].rearrange("p (c e) -> p c e", c=C),
                                   ACT.Copy).then_inc(v_taken, 1)

                for m in range(12):
                    act.wait_ge(tile_summed, 20 + m + 1)
                    if m >= 2:
                        act.wait_ge(conv_done, m - 1)
                    act.activation(raw[:, m % 2, :, 2:258], bank[m % 2][:, :].rearrange("p (s t) -> p s t", s=2),
                                   ACT.Copy).then_inc(group_taken, 1)
                    if m >= 1:
                        silu(m - 1)
                    if m >= 10:
                        v_out(m - 2)
                silu(11)
                v_out(10)
                v_out(11)
                for j in range(8):
                    act.wait_ge(qk_summed, j + 1)
                    act.activation(uT[:, j, :], bank[j][:, :], ACT.Sqrt, bias=epsv[:, 0:1]).then_inc(qk_root, 1)
                act.dma_start(bc[:, 0, :], row_dram[1, 0:1, :].broadcast_to([P, 1032])).then_inc(bc_loaded[0], 16)
                modulation(MOD_QK, MOD_DELTA)

            def delta_row(i, s_):
                modulation_row(MOD_DELTA + RING * i + s_, 6 + s_ % 2, ds(MOD_DELTA // 2 + 3 * i + s_ // 2, 1), 64 * (s_ % 2))

            def delta():
                with act.Fori(0, H_A // 2) as i:
                    for half_ in range(2):
                        h = 2 * i + half_
                        act.wait_ge(head_done, 1 + H_A + h)
                        act.dma_start(bc[:, 1 - half_, :], row_dram[1, ds(2 * i + 1 if half_ == 0 else 2 - 2 * i, 1), :].broadcast_to(
                            [P, 1032])).then_inc(bc_loaded[1 - half_], 16)
                        act.wait_ge(bc_loaded[half_], (48, 32)[half_] + 16 * i + 16)
                        act.activation(bc[:, half_, 1024:1032], bc[:, half_, 1024:1032], ACT.Exp).then_inc(exp_ready, 1)
                        act.wait_ge(kh_turned, 1 + H_A + h + 1)
                        act.activation(ktok, bank[2][:, :].rearrange("p (c e) -> p c e", c=C), ACT.Copy).then_inc(ktok_ready, 1)
                        for d in range(2):
                            act.wait_ge(arg_ready, 32 + 8 * h + 4 * d + 4)
                            part = bc[:, half_, 512 * d:512 * d + 512]
                            act.activation(part, part, ACT.Exp).then_inc(exp_ready, 1)
                        for d in range(2):
                            act.wait_ge(x0_turned, 2 * h + d + 1)
                            act.activation(inv[:, d, 0, :, :], bank[3 * d][:, :].rearrange("p (c e) -> p c e", c=C),
                                           ACT.Copy).then_inc(x0_ready, 1)
                        for l in range(1, len(LEVELS)):
                            for d in range(2):
                                act.wait_ge(bx_ready, 1 + 12 * h + 2 * (l - 1) + d + 1)
                                act.activation(half[:, d, :, :], bank[3 * d][:, :].rearrange("p (c e) -> p c e", c=C),
                                               ACT.Copy).then_inc(bx_copied, 1)
                            if l in (3, 5):
                                delta_row(i, 3 * half_ + (l - 3) // 2)
                        delta_row(i, 3 * half_ + 2)
                        for s in range(C):
                            for d in range(2):
                                ch = ORDER[d][s]
                                act.wait_ge(xz_ready, 1 + 8 * h + 2 * s + d + 1)
                                xz = bank[3 * d][:, P:2 * P]
                                act.activation(vn_b[:, d, :], xz, ACT.Copy, scale=col(Q_BETA, d, ch, h))
                                act.activation(vd_b[:, d, :], xz, ACT.Copy, scale=col(Q_BKD, d, ch, h)).then_inc(v_ready, 1)

            def finish_heads(layer, n_heads, gain, toks):
                if layer == 0:
                    act.wait_ge(bc_loaded[0], 16 * 6)
                act.wait_ge(ms_ready, layer + 1)
                act.activation(ssq[:, :], ssq[:, :], ACT.Sqrt).then_inc(ms_root, 1)
                for h in range(n_heads):
                    act.wait_ge(y_turned, 8 * layer + h + 1)
                    act.activation(featsT[:, h, 0:toks], bank[h % 4][:, 0:toks], ACT.Copy,
                                   scale=gain[:, h:h + 1]).then_inc(feats_ready, 1)

            def experts(layer):
                c0, t0 = seen(layer)
                act.wait_ge(logits_summed, layer + 1)
                act.activation(r_rows[:, t0:], bank[1][0:E, t0:], ACT.Copy).then_inc(logits_copied, 1)
                act.wait_ge(logits_turned, layer + 1)
                act.activation(scores[:, c0:, :], bank[2][:, 0:E * (C - c0)].rearrange("p (c e) -> p c e", e=E),
                               ACT.Sigmoid).then_inc(scored, 1)
                for n, (ch, b) in enumerate((ch, b) for ch in range(c0, C) for b in range(2)):
                    act.wait_ge(tok_turned, 8 * layer + n + 1)
                    act.activation(h_tok[:, ch, 4 * b:4 * b + 4, :], bank[4 + n % 4][:, :].rearrange("p (j e) -> p j e", e=P),
                                   ACT.Copy).then_inc(tok_copied, 1)
                if layer == 0:
                    modulation(MOD_LAST, 24)

                def he_out(i, half):
                    act.wait_ge(xs_turned, layer + i + 1)
                    for b in range(2):
                        act.activation(he[:, half, 4 * b:4 * b + 4, :], bank[b][:, :].rearrange("p (j e) -> p j e", e=P),
                                       ACT.Copy).then_inc(he_copied, 1)

                act.wait_ge(tabled, layer + 1)
                first, end = pairs_of(act, layer)
                he_out(2 * first, 0)
                with act.Fori(first, end) as m:
                    for half_ in range(2):
                        i = 2 * m + half_
                        act.wait_ge(up_summed, i + 1)
                        act.activation(silu_e[:, :, :], bank[2][:, :].rearrange("p (k e) -> p k e", e=P), ACT.Silu).then_inc(
                            silu_ready, 1)
                        he_out(i + 1, 1 - half_)
                        act.wait_ge(down_summed, 1 + i + 1)
                        act.wait_ge(ye_stored, 1 + 32 * m)
                        for b in range(2):
                            act.activation(ye[:, half_, 512 * b:512 * b + 512], bank[4 + b][:, :], ACT.Copy).then_inc(
                                ye_copied, 1)
                        act.wait_ge(ye_copied, 1 + 2 * i + 2)
                        act.dma_start(pass_out[ds(within(act, i, first) * P, P), :], ye[:, half_, :]).then_inc(ye_stored, 16)
                for ch in range(c0, C):
                    act.wait_ge(back_in[ch], 32 * (1 if ch < C_CTX else layer + 1))
                    act.activation(back[0][:, ch, :], back[0][:, ch, :], ACT.Copy, scale=wts[:, ch, 0:1]).then_inc(weighed, 1)

            project_b()
            delta()
            finish_heads(0, 8, gain_h, T)
            def project_c(part):
                n0 = 32 + 18 * part
                for n in range(18):
                    act.wait_ge(tile_summed, n0 + n + 1)
                    b = bank[n % 2]
                    kind, m = ("q", n) if n < 4 else ("z", n - 4) if n < 12 else ("v", n - 12) if n < 16 else ("g", n - 16)
                    if kind == "q":
                        ins = act.activation(q1[:, m, :], b[:, N_CTX:], ACT.Silu)
                    elif kind == "z":
                        ins = act.activation(z1[:, m // 4, m % 4, :], b[:, :], ACT.Copy)
                    elif kind == "v":
                        ins = act.activation(v1[:, m, :, :], b[:, :].rearrange("p (h e) -> p h e", h=4), ACT.Copy)
                    else:
                        ins = act.activation(featsT[:, 4 * part:4 * part + 4, P * m:P * m + P],
                                             b[:, :].rearrange("p (h e) -> p h e", h=4), ACT.Silu)
                    ins.then_inc(group_taken, 1)

            def hgrn(part):
                with act.Fori(0, 4) as i:
                    h = 4 * part + i
                    act.activation(small[:, 44:45], epsv[:, :], ACT.Sigmoid).then_inc(sig_ready, 1)
                    act.wait_ge(update1_ready, 1 + 2 * h)
                    for d in range(2):
                        z = z1[:, d, ds(i, 1), :].rearrange("p o t -> p (o t)")
                        act.activation(decay[:, d, :], z, ACT.Sigmoid, bias=forget[:, 0, d, ds(h, 1)]).then_inc(sig_ready, 1)
                        act.activation(ks[:, d, :], z, ACT.Sigmoid, scale=-1.0, bias=forget[:, 1, d, ds(h, 1)]).then_inc(sig_ready, 1)
                    for d in range(2):
                        act.wait_ge(kd_turned, 2 * h + d + 1)
                        act.activation(kd1[:, d, :, :], bank[5 + d][:, 0:384].rearrange("p (s e) -> p s e", s=3),
                                       ACT.Copy).then_inc(kd_ready, 1)

            def final_norm():
                for j in range(J):
                    act.wait_ge(x_updated, 3 * J + j + 1)
                    act.activation(uT[:, j, N_CTX:], xT[:, j, N_CTX:], ACT.Square).then_inc(sq_ready, 1)
                act.wait_ge(rstd_step, 9)
                act.activation(rstd[:, N_CTX:], rstd[:, N_CTX:], ACT.Sqrt).then_inc(root_ready, 1)
                for j in range(J):
                    act.wait_ge(xn_ready, 4 * J + j + 1)
                    act.activation(uT[:, j, N_CTX:], uT[:, j, N_CTX:], ACT.Copy, scale=nfin[:, j:j + 1]).then_inc(u_ready, 1)
                for ch in range(2):
                    for b in range(2):
                        act.wait_ge(out_turned, 2 * ch + b + 1)
                        act.activation(out_sb[:, ch, :].rearrange("p (e j) -> p j e", j=J)[:, 4 * b:4 * b + 4, :],
                                       bank[4 + 2 * ch + b][:, :].rearrange("p (j e) -> p j e", e=P), ACT.Copy).then_inc(out_copied, 1)

            norm(1, 0)
            experts(0)
            act.wait_ge(forget_step, 1)
            act.activation(forget[:, 3, :, :], forget[:, 3, :, :], ACT.Exp).then_inc(forget_act, 1)
            norm(2, 0)
            project_c(0)
            hgrn(0)
            act.wait_ge(head_done, 1 + 12)
            project_c(1)
            hgrn(1)
            finish_heads(1, 8, gain_c, N_LAT)
            norm(3, N_CTX)
            experts(1)
            final_norm()

        @block.vector
        def _(dve):
            one_up(dve, counted_by_dve)
            for j in range(1, J, 2):
                dve.wait_ge(x_turned, j + 1)
                dve.tensor_copy(xT[:, j, :], bank[j % 4][:, :]).then_inc(xT_dve, 1)

            def modulation(start, end):
                dve.wait_ge(mod_spread, 64 * end)
                dve.wait_ge(params_loaded, 16 * N_PARAMS)
                biases = bmod[:, :, :, :].rearrange("p l v j -> p (l v) j")
                for w in range(2):
                    ins = dve.tensor_tensor(modvs[:, start:end, w, :], modvs[:, start:end, w, :], biases[:, start:end, :], ALU.add)
                ins.then_inc(mod_ready, 1)

            def coefficients(n, gain, s):
                dve.wait_ge(mod_ready, (1, 2, 2, 3)[n])
                if n:
                    dve.wait_ge(u_ready, J * n)
                dve.tensor_scalar(coef[:, :, :], modv[:, n // 2, s, :, :], 1.0, None, ALU.add).then_inc(coef_step, 1)
                dve.wait_ge(coef_step, n + 1)
                dve.tensor_tensor(coef[:, :, :], coef[:, :, :], gain.unsqueeze(1).broadcast_to([P, 2, J]),
                                  ALU.mult).then_inc(coef_ready, 1)

            def norm(n, t0):
                dve.wait_ge(ssq_ready, n + 1)
                if n == 0:
                    dve.wait_ge(consts_ready, 1)
                dve.tensor_scalar(rstd[:, t0:], bank[0][:, t0:], 1.0 / D, EPS, ALU.mult, ALU.add).then_inc(rstd_step, 1)
                dve.wait_ge(root_ready, n + 1)
                dve.reciprocal(rstd[:, t0:], rstd[:, t0:]).then_inc(rstd_step, 1)
                dve.wait_ge(rstd_step, 2 * n + 2)
                for j in range(J):
                    dve.tensor_tensor(uT[:, j, t0:], xT[:, j, t0:], rstd[:, t0:], ALU.mult).then_inc(xn_ready, 1)

            def gate_rows():
                n = [0]

                def step(ins):
                    ins.then_inc(row_dve, 1)
                    n[0] += 1
                    dve.wait_ge(row_dve, n[0])

                def last(ins):
                    ins.then_inc(row_dve, 1)
                    n[0] += 1

                dve.wait_ge(gates_moved, 16 * 8)
                dve.wait_ge(turned_loaded, 16 * N_TURNED)
                dve.wait_ge(consts_ready, 1)
                fa, ia, aa = grow4[:, GATE_F, :, :], grow4[:, GATE_I, :, :], grow4[:, GATE_A, :, :]
                for d in range(2):
                    last(dve.tensor_scalar(fa[:, d, :], fa[:, d, :], gbias[:, 1, d:d + 1], -1.0, ALU.add, ALU.mult))
                    last(dve.tensor_scalar(aa[:, d, :], aa[:, d, :], gbias[:, 2, d:d + 1], None, ALU.add))
                dve.wait_ge(row_dve, n[0])
                dve.scalar_tensor_tensor(row(0), fa, -1.0, fa, ALU.mult, ALU.max)
                last(dve.scalar_tensor_tensor(row(1), aa, -1.0, aa, ALU.mult, ALU.max))
                for d in range(2):
                    last(dve.tensor_scalar(ia[:, d, :], ia[:, d, :], gbias[:, 0, d:d + 1], None, ALU.add))
                dve.wait_ge(row_act, 4)
                step(dve.scalar_tensor_tensor(row(0), fa, 0.0, row(0), ALU.max, ALU.add))
                step(dve.scalar_tensor_tensor(row(1), aa, 0.0, row(1), ALU.max, ALU.add))
                step(dve.tensor_scalar(row(0), row(0), -1.0, None, ALU.mult))
                for d in range(2):
                    step(dve.tensor_scalar(row(1)[:, d, :], row(1)[:, d, :], gbias[:, 3, d:d + 1], -1.0,
                                           ALU.mult, ALU.mult))
                for kind, dst in ((0, 2), (1, 4)):
                    for d in range(2):
                        for ch in range(C):
                            o = slice(P * ch, P * ch + P)
                            src, to = row(kind)[:, d, o], row(dst)[:, d, o]
                            if d:
                                src, to = src[:, ::-1], to[:, ::-1]
                            last(dve.tensor_tensor_scan(to, ones[0:H_A, :], src, 0.0, ALU.mult, ALU.add))
                dve.wait_ge(row_dve, n[0])
                step(dve.tensor_tensor(row(0), ia, row(2), ALU.subtract))
                step(dve.memset(ends[:, 0, :, :], 0.0))

                def at_end(kind, d):
                    return row(kind)[:, d, (P - 1 if d == 0 else 0)::P]

                for d in range(2):
                    last(dve.tensor_copy(ends[:, 2, d, :], at_end(2, d)))
                    last(dve.tensor_copy(ends[:, 3, d, :], at_end(4, d)))
                dve.wait_ge(row_dve, n[0])
                for s in range(C):
                    for d in range(2):
                        ch = ORDER[d][s]
                        a, b = P * ch, P * ch + P
                        g, m = row(0)[:, d, a:b], row(3)[:, d, a:b]
                        if d:
                            g, m = g[:, ::-1], m[:, ::-1]
                        step(dve.tensor_tensor_scan(m, g, g, ends[:, 0, d, ch:ch + 1], ALU.max, ALU.max))
                        step(dve.tensor_copy(ends[:, 1, d, ch:ch + 1], at_end(3, d)[:, ch:ch + 1]))
                        if s < C - 1:
                            nxt = ORDER[d][s + 1]
                            step(dve.tensor_tensor(ends[:, 0, d, nxt:nxt + 1], ends[:, 1, d, ch:ch + 1],
                                                   ends[:, 2, d, ch:ch + 1], ALU.add))

                def by_chunk(kind):
                    return row(kind).rearrange("h d (c t) -> h (d c) t", c=C)

                def spread(k):
                    return ends[:, k, :, :].rearrange("h d c -> h (d c)").unsqueeze(2).broadcast_to([H_A, 2 * C, P])

                step(dve.tensor_scalar(row(7), row(3), -1.0, None, ALU.mult))
                step(dve.tensor_tensor(by_chunk(1), by_chunk(7), spread(0), ALU.add))
                step(dve.tensor_tensor(by_chunk(2), by_chunk(7), by_chunk(2), ALU.subtract))
                step(dve.tensor_tensor(by_chunk(3), by_chunk(0), spread(1), ALU.subtract))
                step(dve.tensor_tensor(by_chunk(5), spread(3), by_chunk(4), ALU.subtract))
                dve.wait_ge(row_act, 1)
                dve.tensor_tensor(ends[:, 0, :, :], ends[:, 0, :, :], ends[:, 1, :, :], ALU.subtract).then_inc(rows_ready, 1)

            def gate_cols():
                dve.wait_ge(cols_act, 6)
                dve.tensor_scalar(cols[:, 32 * Q_NEGC:32 * Q_NEGC + 32], cols[:, 32 * Q_EGC:32 * Q_EGC + 32], -1.0, None,
                                  ALU.mult).then_inc(cols_dve, 1)
                dve.tensor_tensor(cols[:, 32 * Q_BKD:32 * Q_BKD + 32], cols[:, 32 * Q_EKD:32 * Q_EKD + 32],
                                  cols[:, 32 * Q_BETA:32 * Q_BETA + 32], ALU.mult).then_inc(cols_dve, 1)
                dve.wait_ge(cols_dve, 2)

            def mlstm():
                with dve.Fori(0, H_A // 2) as i:
                    for half in range(2):
                        h = 2 * i + half
                        dve.wait_ge(bc_loaded[half], 16 * i + 16)
                        for d in range(2):
                            for ch in range(C):
                                part = bc[:, half, 512 * d + P * ch:512 * d + P * ch + P]
                                dve.scalar_tensor_tensor(part, part, col(Q_G, d, ch, h), ahead[:, d, :],
                                                         ALU.add, ALU.add).then_inc(arg_ready, 1)
                        dve.wait_ge(scores_ready, h + 1)
                        for d in range(2):
                            dve.wait_ge(exp_ready, 3 * h + 2 + d)
                            part = bc[:, half, 512 * d:512 * d + 512]
                            dve.tensor_tensor(part, part, bank[0][:, :], ALU.mult).then_inc(w_ready, 1)
                        dve.wait_ge(inter_ready, 1 + 2 * h)
                        for d in range(2):
                            dve.wait_ge(update_ready, 1 + 2 * h + d + 1)
                            for s in range(3):
                                new = bank[4 + d][:, 129 * s:129 * s + 129]
                                if s == 0:
                                    ins = dve.tensor_copy(cell[:, d, 0, :], new)
                                else:
                                    dve.wait_ge(cell_step, 1 + 6 * h + 3 * d + s)
                                    k = 1024 + 4 * d + ORDER[d][s]
                                    ins = dve.scalar_tensor_tensor(cell[:, d, s, :], cell[:, d, s - 1, :], bc[:, half, k:k + 1],
                                                                   new, ALU.mult, ALU.add)
                                ins.then_inc(cell_step, 1)
                        dve.wait_ge(intra_copied, 1 + 3 * h + 3)
                        for d in range(2):
                            dve.wait_ge(inter_ready, 1 + 2 * h + d + 1)
                            for s in range(1, C):
                                ch = ORDER[d][s]
                                u = 4 * d + ch
                                dve.scalar_tensor_tensor(num[:, u, :], bank[6 + d][:, 129 * s - 129:129 * s],
                                                         col(Q_WI, d, ch, h), num[:, u, :], ALU.mult, ALU.add).then_inc(joined, 1)
                        dve.wait_ge(joined, 1 + 6 * h + 6)
                        den = num[:, :, P:P + 1].rearrange("p u o -> p (u o)")
                        dve.scalar_tensor_tensor(small[:, 0:8], den, -1.0, den, ALU.mult, ALU.max).then_inc(head_step, 1)
                        dve.wait_ge(head_step, 12 * h + 1)
                        dve.tensor_tensor(small[:, 8:16], small[:, 0:8], cols[:, ds(32 * Q_EM + h, 8, 4)],
                                          ALU.max).then_inc(head_step, 1)
                        dve.wait_ge(head_step, 12 * h + 2)
                        dve.reciprocal(small[:, 16:24], small[:, 8:16]).then_inc(head_step, 1)
                        dve.wait_ge(head_step, 12 * h + 3)
                        for ch in range(C):
                            dve.tensor_scalar(hsum[:, ch, :], num[:, ch, 0:P], small[:, 16 + ch:17 + ch], None,
                                              ALU.mult).then_inc(head_step, 1)
                        for ch in range(C):
                            dve.wait_ge(head_step, 12 * h + 4 + ch)
                            dve.scalar_tensor_tensor(hsum[:, ch, :], num[:, 4 + ch, 0:P], small[:, 20 + ch:21 + ch],
                                                     hsum[:, ch, :], ALU.mult, ALU.add).then_inc(head_step, 1)
                        dve.wait_ge(head_step, 12 * h + 11)
                        head_out(h, 0, hsum, num, C, 12 * h + 12)

            def convolve():
                for m in range(12):
                    dve.wait_ge(group_taken, 20 + m + 1)
                    if m >= 2:
                        dve.wait_ge(silu_done, m - 1)
                    dst = taps[:, m % 2, :].rearrange("p (s t) -> p s t", s=2)
                    for k in range(CONV):
                        src = raw[:, m % 2, :, k:k + 256]
                        w = taps_w[:, k, m:m + 1]
                        if k == 0:
                            dve.tensor_scalar(dst, src, w, None, ALU.mult).then_inc(taps_step, 1)
                        else:
                            dve.wait_ge(taps_step, 4 * m + k)
                            dve.scalar_tensor_tensor(dst, src, w, dst, ALU.mult, ALU.add).then_inc(
                                taps_step if k < CONV - 1 else conv_done, 1)

            def normalise_qk():
                for j in range(8):
                    dve.wait_ge(qk_root, j + 1)
                    dve.reciprocal(uT[:, j, :], uT[:, j, :]).then_inc(qk_step, 1)
                for j in range(8):
                    dve.wait_ge(qk_step, j + 1)
                    t = (qT, kT)[j // 4][:, j % 4, :]
                    dve.scalar_tensor_tensor(t, t, (P ** -0.5, 1.0)[j // 4], uT[:, j, :], ALU.mult, ALU.mult).then_inc(qk_normed, 1)

            def delta():
                with dve.Fori(0, H_A // 2) as i:
                    for half_ in range(2):
                        h = 2 * i + half_
                        dve.wait_ge(bc_loaded[half_], (48, 32)[half_] + 16 * i + 16)
                        for d in range(2):
                            for ch in range(C):
                                part = bc[:, half_, 512 * d + P * ch:512 * d + P * ch + P]
                                dve.scalar_tensor_tensor(part, part, col(Q_NGC, d, ch, h), ahead[:, d, :],
                                                         ALU.add, ALU.add).then_inc(arg_ready, 1)
                        dve.wait_ge(scores_ready, H_A + h + 1)
                        for d in range(2):
                            dve.wait_ge(exp_ready, 12 + 3 * h + 2 + d)
                            dve.wait_ge(mask_ready, 1 + 14 * h)
                            for ch in range(C):
                                o = slice(P * ch, P * ch + P)
                                dve.scalar_tensor_tensor(lower[:, d, ch, :], bank[0][:, o], col(Q_BETA, d, ch, h),
                                                         bc[:, half_, 512 * d + P * ch:512 * d + P * ch + P],
                                                         ALU.mult, ALU.mult).then_inc(lower_ready, 1)
                        for d in range(2):
                            dve.wait_ge(lower_ready, 8 * h + 4 * d + 4)
                            part = bc[:, half_, 512 * d:512 * d + 512]
                            dve.tensor_tensor(part, part, bank[1][:, :], ALU.mult).then_inc(att_ready, 1)
                        for d in range(2):
                            dve.wait_ge(mask_ready, 1 + 14 * h + d + 1)
                            dve.wait_ge(xz_ready, 1 + 8 * h)
                            dve.tensor_tensor(inv[:, d, 1, :, :], ident[:, :].unsqueeze(1).broadcast_to([P, C, P]),
                                              masked[:, d, :, :], ALU.subtract).then_inc(inv_ready, 1)
                        for l in range(1, len(LEVELS)):
                            for d in range(2):
                                dve.wait_ge(xbx_ready, 12 * h + 2 * (l - 1) + d + 1)
                                for x_ in (0, 1) if l < len(LEVELS) - 1 else (1,):
                                    ins = dve.tensor_tensor(inv[:, d, x_, :, :], inv[:, d, x_, :, :],
                                                            bank[3 * d + 1 + x_][:, :].rearrange("p (c e) -> p c e", c=C),
                                                            ALU.subtract)
                                ins.then_inc(inv_ready, 1)
                        for s in range(C):
                            for d in range(2) if s else ():
                                ch = ORDER[d][s]
                                dve.wait_ge(carried_ready, 1 + 6 * h + 2 * (s - 1) + d + 1)
                                dve.scalar_tensor_tensor(z_b[:, d, :], bank[3 * d][:, 0:P], col(Q_NEGC, d, ch, h),
                                                         vb[:, ch, ds(h, 1), :].rearrange("p o e -> p (o e)"),
                                                         ALU.mult, ALU.add).then_inc(z_ready, 1)
                            for d in range(2):
                                ch = ORDER[d][s]
                                dve.wait_ge(outer_ready, 1 + 8 * h + 2 * s + d + 1)
                                k = 1024 + 4 * d + ch
                                if s == 0:
                                    dve.tensor_copy(state_b[:, d, :], bank[3 * d + 2][:, 0:P]).then_inc(state_ready, 1)
                                elif s < C - 1:
                                    dve.scalar_tensor_tensor(state_b[:, d, :], state_b[:, d, :], bc[:, half_, k:k + 1],
                                                             bank[3 * d + 2][:, 0:P], ALU.mult, ALU.add).then_inc(state_ready, 1)
                                n = 14 * h + max(0, 4 * s - 2) + (1 if s == 0 else 2) * d
                                within, carried = bank[3 * d + 1][:, P:2 * P], bank[3 * d + 1][:, 0:P]
                                if s in (0, 2):
                                    dve.tensor_copy(osum[:, ch, :], within).then_inc(o_step, 1)
                                else:
                                    dve.wait_ge(o_step, 1 + n)
                                    dve.tensor_tensor(osum[:, ch, :], osum[:, ch, :], within, ALU.add).then_inc(o_step, 1)
                                if s:
                                    dve.wait_ge(o_step, 1 + n + 1)
                                    dve.scalar_tensor_tensor(osum[:, ch, :], carried, col(Q_EGC, d, ch, h), osum[:, ch, :],
                                                             ALU.mult, ALU.add).then_inc(o_step, 1)
                        dve.wait_ge(o_step, 1 + 14 * h + 14)
                        head_out(h, 4, osum, lower[:, 0, :, :], C, 48 + h + 1)

            def finish_heads(layer, n_heads, chunks):
                dve.wait_ge(head_done, 1 + 8 * layer + 8)
                dve.tensor_scalar(ssq[:, :], ssq[:, :], 1.0 / P, EPS, ALU.mult, ALU.add).then_inc(ms_ready, 1)
                dve.wait_ge(ms_root, layer + 1)
                dve.reciprocal(ssq[:, :], ssq[:, :]).then_inc(y_step, 1)
                dve.wait_ge(y_step, layer + 1)
                for h in range(n_heads):
                    g = featsT[:, h, 0:P * chunks].rearrange("p (c e) -> p c e", c=chunks)
                    r = ssq[:, C * h:C * h + chunks].unsqueeze(2).broadcast_to([P, chunks, P])
                    dve.tensor_tensor(g, g, r, ALU.mult).then_inc(y_ready, 1)

            def mix_out(layer, who):
                for j in range(J):
                    dve.wait_ge(out_summed, 8 * layer + j + 1)
                    for w in who:
                        o = slice(0, N_CTX) if w else slice(N_CTX, T)
                        ins = dve.scalar_tensor_tensor(xT[:, j, o], bank[4 + j % 4][:, o], modv[:, layer, 2, w, j:j + 1],
                                                       xT[:, j, o], ALU.mult, ALU.add)
                    ins.then_inc(x_updated, 1)

            n_route_steps = [0]

            def route(layer):
                n = [n_route_steps[0]]
                c0, nc_ = seen(layer)[0], C - seen(layer)[0]

                def step(ins):
                    ins.then_inc(route_step, 1)
                    n[0] += 1
                    dve.wait_ge(route_step, n[0])

                def best(vals, out_, m):
                    t, t2 = tmp[:, c0:, 0:m], tmp2[:, c0:, 0:m]
                    step(dve.tensor_reduce(top[:, c0:], vals, AX.X, ALU.max))
                    step(dve.tensor_tensor(t, vals, top[:, c0:].unsqueeze(2).broadcast_to([P, nc_, m]), ALU.is_ge))
                    step(dve.scalar_tensor_tensor(t2, t, -64.0, iota[:, 0:m].unsqueeze(1).broadcast_to([P, nc_, m]),
                                                  ALU.mult, ALU.add))
                    step(dve.tensor_reduce(low[:, c0:], t2, AX.X, ALU.min))
                    step(dve.tensor_tensor(out_, t2, low[:, c0:].unsqueeze(2).broadcast_to([P, nc_, m]), ALU.is_equal))

                dve.wait_ge(scored, layer + 1)
                dve.wait_ge(iota_ready, layer + 1)
                sc, se = scores[:, c0:, :], sel[:, c0:, :]
                step(dve.tensor_tensor(se, sc, bias_r[:, :].unsqueeze(1).broadcast_to([P, nc_, E]), ALU.add))
                a = se.rearrange("p c (g e) -> p (c g) e", g=GROUPS)
                pr = pairs[:, GROUPS * c0:, :]
                step(dve.tensor_tensor(pr[:, :, 0:3], a[:, :, 0:3], a[:, :, 1:4], ALU.add))
                step(dve.tensor_tensor(pr[:, :, 3:5], a[:, :, 0:2], a[:, :, 2:4], ALU.add))
                step(dve.tensor_tensor(pr[:, :, 5:6], a[:, :, 0:1], a[:, :, 3:4], ALU.add))
                step(dve.tensor_reduce(g_score[:, c0:, :].rearrange("p c g -> p (c g)"), pr, AX.X, ALU.max))
                best(g_score[:, c0:, :], g_pick[:, c0:, :], GROUPS)
                gp = g_pick[:, c0:, :]
                step(dve.tensor_scalar(gp, gp, FAR, -FAR, ALU.mult, ALU.add))
                step(dve.tensor_tensor(a, a, gp.rearrange("p c g -> p (c g)").unsqueeze(2).broadcast_to(
                    [P, GROUPS * nc_, E // GROUPS]), ALU.add))
                fi, sd, tk = first[:, c0:, :], second[:, c0:, :], taken[:, c0:, :]
                best(se, fi, E)
                step(dve.scalar_tensor_tensor(se, fi, -3 * FAR, se, ALU.mult, ALU.add))
                best(se, sd, E)
                for k, oh in ((0, fi), (1, sd)):
                    step(dve.tensor_tensor(tmp[:, c0:, :], oh, sc, ALU.mult))
                    step(dve.tensor_reduce(wts[:, c0:, k], tmp[:, c0:, :], AX.X, ALU.add))
                step(dve.tensor_tensor(total[:, c0:], wts[:, c0:, 0], wts[:, c0:, 1], ALU.add))
                step(dve.reciprocal(total[:, c0:], total[:, c0:]))
                step(dve.tensor_tensor(wts[:, c0:, :], wts[:, c0:, :], total[:, c0:].unsqueeze(2).broadcast_to([P, nc_, 2]),
                                       ALU.mult))
                dve.tensor_tensor(tk, fi, sd, ALU.add).then_inc(chosen, 1)
                dve.wait_ge(counted, layer + 1)
                rk = bank[3][:, 0:E * C].rearrange("p (c e) -> p c e", e=E)
                cn = bank[3][:, E * C:2 * E * C].rearrange("p (c e) -> p c e", e=E)
                step(dve.tensor_copy(count[:, :], cn[:, c0, :]))
                step(dve.tensor_copy(rank[:, c0, :], rk[:, c0, :]))
                for ch in range(c0 + 1, C):
                    step(dve.tensor_tensor(rank[:, ch, :], rk[:, ch, :], count[:, :], ALU.add))
                    step(dve.tensor_tensor(count[:, :], count[:, :], cn[:, ch, :], ALU.add))
                step(dve.tensor_scalar(n_pass[:, :], count[:, :], 128.0, 1.0, ALU.is_gt, ALU.add))
                for m in (256.0, 384.0):
                    step(dve.scalar_tensor_tensor(n_pass[:, :], count[:, :], m, n_pass[:, :], ALU.is_gt, ALU.add))
                step(dve.tensor_tensor_scan(upto_e[:, :], ones[:, 0:E], n_pass[:, :], 0.0, ALU.mult, ALU.add))
                step(dve.tensor_tensor(start_e[:, :], upto_e[:, :], n_pass[:, :], ALU.subtract))
                step(dve.scalar_tensor_tensor(rank[:, c0:, :], start_e[:, :].unsqueeze(1).broadcast_to([P, nc_, E]), 128.0,
                                              rank[:, c0:, :], ALU.mult, ALU.add))
                for k, oh in ((0, fi), (1, sd)):
                    step(dve.tensor_tensor(tmp[:, c0:, :], oh, rank[:, c0:, :], ALU.mult))
                    step(dve.tensor_reduce(pos[:, c0:, k], tmp[:, c0:, :], AX.X, ALU.add))
                np_ = PASSES + 2
                dve.tensor_copy(slot_of[:, c0:, :], pos[:, c0:, :]).then_inc(rows_chosen, 1)
                i0 = ids_f[0:1, :, :]
                step(dve.tensor_tensor(i0, upto_e[0:1, :].unsqueeze(1).broadcast_to([1, np_, E]),
                                       iota[0:1, 0:np_].unsqueeze(2).broadcast_to([1, np_, E]), ALU.is_le))
                step(dve.tensor_reduce(table[0:1, :], i0, AX.X, ALU.add))
                step(dve.tensor_scalar(steps[:, layer, 0:np_], table[0:1, :], float(E - 1), None, ALU.min))
                step(dve.tensor_scalar(table[0:1, 0:16], iota[0:1, 0:16], 2.0, None, ALU.mult))
                step(dve.tensor_scalar(table[0:1, 0:16], table[0:1, 0:16], upto_e[0:1, E - 1:E], None, ALU.is_lt))
                step(dve.tensor_reduce(table[0:1, 16:17], table[0:1, 0:16], AX.X, ALU.add))
                if layer == 0:
                    step(dve.tensor_copy(small[0:1, 47:48], table[0:1, 16:17]))
                else:
                    step(dve.tensor_tensor(table[0:1, 16:17], table[0:1, 16:17], small[0:1, 47:48], ALU.add))
                dve.tensor_copy(steps[:, layer, np_:np_ + 1], table[0:1, 16:17]).then_inc(tabled, 1)
                n_route_steps[0] = n[0]

            def experts(layer, who):
                c0 = seen(layer)[0]
                dve.wait_ge(tabled, layer + 1)
                first, end = pairs_of(dve, layer)
                with dve.Fori(first, end) as m:
                    for half_ in range(2):
                        i = 2 * m + half_
                        dve.wait_ge(silu_ready, i + 1)
                        dve.wait_ge(down_summed, 1 + i)
                        dve.tensor_tensor(act_e[:, :, :], silu_e[:, :, :], bank[3][:, :].rearrange("p (k e) -> p k e", e=P),
                                          ALU.mult).then_inc(gated, 1)
                for ch in range(c0, C):
                    n = C * layer + ch - c0
                    dve.wait_ge(weighed, n + 1)
                    dve.wait_ge(back_in[ch], 32 * (1 if ch < C_CTX else layer + 1))
                    dve.scalar_tensor_tensor(back[0][:, ch, :], back[1][:, ch, :], wts[:, ch, 1:2], back[0][:, ch, :],
                                             ALU.mult, ALU.add).then_inc(both_ready, 1)
                for j in range(J):
                    dve.wait_ge(both_turned, J * layer + j + 1)
                    for w in who:
                        o = slice(0, N_CTX) if w else slice(N_CTX, T)
                        ins = dve.scalar_tensor_tensor(xT[:, j, o], bank[j][:, o], modv[:, layer, 5, w, j:j + 1],
                                                       xT[:, j, o], ALU.mult, ALU.add)
                    ins.then_inc(x_updated, 1)

            def head_out(h, first, summed, dead, n, steps):
                for ch in range(n):
                    ins = dve.tensor_tensor_reduce(dead[:, ch, 0:P], summed[:, ch, :], summed[:, ch, :], 1.0, 0.0,
                                                   ALU.mult, ALU.add, small[:, 24 + ch:25 + ch])
                ins.then_inc(head_step, 1)
                g = featsT[:, ds(first + h, 1), 0:P * n].rearrange("p o (c e) -> p (o c) e", c=n)
                dve.tensor_tensor(g, g, summed, ALU.mult)
                dve.wait_ge(head_step, steps)
                dve.tensor_copy(ssq[:, ds((first + h) * C, n)], small[:, 24:24 + n]).then_inc(head_done, 1)

            def lower_bounds():
                n = [0]

                def step(ins):
                    ins.then_inc(forget_step, 1)
                    n[0] += 1
                    dve.wait_ge(forget_step, n[0])

                raw_, p_ = forget[:, 2, :, :], forget[:, 3, :, :]
                step(dve.tensor_tensor(p_, raw_, raw_, ALU.subtract))
                step(dve.tensor_scalar(forget[:, 1, :, :], forget[:, 0, :, :], -1.0, None, ALU.mult))
                dve.wait_ge(forget_act, 1)
                step(dve.reciprocal(raw_, p_))
                step(dve.tensor_tensor(p_, p_, raw_, ALU.mult))
                step(dve.tensor_tensor(raw_, p_, p_, ALU.subtract))
                step(dve.tensor_scalar(p_, raw_, -1.0, 1.0, ALU.mult, ALU.add))

            def hgrn(part):
                with dve.Fori(0, 4) as i:
                    h = 4 * part + i
                    q = q1[:, ds(i, 1), :].rearrange("p o t -> p (o t)")
                    dve.wait_ge(o1_ready, 1 + h)
                    for d in range(2):
                        lb, rest = forget[:, 2, d, ds(h, 1)], forget[:, 3, d, ds(h, 1)]
                        dve.wait_ge(sig_ready, 5 * h + 2 * d + 3)
                        dve.tensor_scalar(decay[:, d, :], decay[:, d, :], rest, lb, ALU.mult, ALU.add).then_inc(f_ready, 1)
                        dve.tensor_scalar(ks[:, d, :], ks[:, d, :], rest, None, ALU.mult).then_inc(f_ready, 1)
                        dve.wait_ge(f_ready, 6 * h + 3 * d + 1)
                        dve.tensor_tensor(qp[:, d, :], q, decay[:, d, N_CTX:], ALU.mult).then_inc(f_ready, 1)
                    for l in range(len(LEVELS)):
                        if l:
                            dve.wait_ge(tot_step, 7 * h + l)
                            dve.wait_ge(cp_done, 1 + 8 * h + l + 1)
                        for d in range(2):
                            if l == 0 and d == 1:
                                dve.copy_predicated(att1[:, :, :, :].rearrange("p d c t -> p (d c) t"),
                                                    ident[:, :].bitcast(I32).unsqueeze(1).broadcast_to([P, 4, P]),
                                                    bank[2][:, :].rearrange("p (a t) -> p a t", a=4)).then_inc(cp_done, 1)
                                dve.wait_ge(cp_done, 1 + 8 * h + 1)
                            dve.wait_ge(level_ready, 16 * h + 2 * l + d + 3)
                            if l:
                                dve.wait_ge(qp_updated, 14 * h + 2 * (l - 1) + d + 1)
                            blocks, totals = by_block(qp[:, d, :], l), totals_of(d, l, lat=True)
                            dve.tensor_tensor(blocks[:, :, 1 - d, :], blocks[:, :, 1 - d, :],
                                              totals[:, :, d:d + 1].broadcast_to([P, N_LAT >> (l + 1), 1 << l]),
                                              ALU.mult).then_inc(qp_updated, 1)
                        dve.copy_predicated(att1[:, :, :, :],
                                            level[:, :, l, :].bitcast(I32).unsqueeze(2).broadcast_to([P, 2, 2, P]),
                                            bank[2 + (l + 1) % 3][:, :].rearrange("p (d c t) -> p d c t", d=2, c=2)).then_inc(
                                                cp_done, 1)
                    for d in range(2):
                        dve.wait_ge(update1_ready, 1 + 2 * h + d + 1)
                        for s in range(3):
                            new = bank[5 + d][:, P * s:P * s + P]
                            if s == 0:
                                ins = dve.tensor_copy(state1[:, d, 0, :], new)
                            else:
                                dve.wait_ge(state1_step, 1 + 6 * h + 3 * d + s)
                                k = tot_at(7) + ORDER[d][s]
                                ins = dve.scalar_tensor_tensor(state1[:, d, s, :], state1[:, d, s - 1, :], tot[:, d, k:k + 1],
                                                               new, ALU.mult, ALU.add)
                            ins.then_inc(state1_step, 1)
                    dve.wait_ge(o1_ready, 1 + h + 1)
                    dve.tensor_copy(o1[:, :, :], bank[7][:, 0:2 * P].rearrange("p (c e) -> p c e", c=2)).then_inc(o1_copied, 1)
                    dve.wait_ge(o1_copied, 1 + h + 1)
                    head_out(h, 0, o1, state1[:, 0, :, :], 2, 52 + h + 1)

            norm(0, 0)
            modulation(0, MOD_QK // 2)
            coefficients(0, nmix[:, 0, :], 1)
            gate_rows()
            gate_cols()
            mlstm()
            convolve()
            normalise_qk()
            delta()
            finish_heads(0, 8, C)
            modulation(MOD_QK // 2, MOD_LAST // 2)
            dve.wait_ge(mod_ready, 2)
            mix_out(0, (0, 1))
            coefficients(1, nffn[:, 0, :], 4)
            norm(1, 0)
            route(0)
            experts(0, (0, 1))
            lower_bounds()
            modulation(MOD_LAST // 2, 12)
            coefficients(2, nmix[:, 1, :], 1)
            norm(2, 0)
            hgrn(0)
            hgrn(1)
            finish_heads(1, 8, 2)
            mix_out(1, (0,))
            coefficients(3, nffn[:, 1, :], 4)
            norm(3, N_CTX)
            route(1)
            experts(1, (0,))
            norm(4, N_CTX)

        @block.tensor
        def _(pe):
            one_up(pe, counted_by_pe)
            pe.wait_ge(ident_ready, 1)
            pe.wait_ge(x_loaded, 32)
            for j in range(J):
                if j >= 4:
                    pe.wait_ge((xT_act, xT_dve)[j % 2], j // 2 - 1)
                for t in range(C):
                    mm = pe.transpose(bank[j % 4][:, P * t:P * t + P], x_in[:, t, j::J], ident[:, :])
                mm.then_inc(x_turned, 1)

            def modulation_part(q, b, at, i, part):
                if part == 0:
                    pe.wait_ge(slot_in[at % RING], 16 * (at // RING + 1) + 16 * i)
                    if not isinstance(q, int) or q >= 2:
                        pe.wait_ge(row_copied, 1 + q - 1)
                for k in (2 * part, 2 * part + 1):
                    mm = pe.matmul(bank[b][0:2, :], csil[:, k, :], slot(at, J)[:, k, :], start=(k == 0), stop=(k == J - 1))
                if part == 3:
                    mm.then_inc(mod_summed, 1)

            def modulation(start, end):
                for q in range(start, end):
                    for part in range(4):
                        modulation_part(q, 6 + q % 2, slot_at["mod", q // 12, q % 12, 0], 0, part)

            def norm(n, t0):
                pe.wait_ge(consts_ready, 1)
                for j in range(J):
                    pe.wait_ge(sq_ready, J * n + j + 1)
                    mm = pe.matmul(bank[0][:, t0:], ones[:, :], uT[:, j, t0:], start=(j == 0), stop=(j == J - 1))
                mm.then_inc(ssq_ready, 1)

            pe.wait_ge(csil_ready, 1)
            norm(0, 0)
            modulation(0, MOD_QK)

            def project(layer, g, n0, turned, t0=0, u_from=None):
                at = slot_at["in", layer, g, 0]
                slot_arrived(pe, at)
                w = slot(at, J)
                tiles = range(4) if turned or t0 == 0 else range(t0 // P, C)
                for m, n in enumerate(tiles):
                    if n0 + m >= 2:
                        pe.wait_ge(group_taken, n0 + m - 1)
                    for k in range(J):
                        if m == 0 and u_from is not None:
                            pe.wait_ge(u_ready, u_from + k + 1)
                        if turned:
                            mm = pe.matmul(bank[(n0 + m) % 2][:, t0:], w[:, k, P * n:P * n + P], uT[:, k, t0:],
                                           start=(k == 0), stop=(k == J - 1))
                        else:
                            mm = pe.matmul(bank[(n0 + m) % 2][:, :], uT[:, k, P * n:P * n + P], w[:, k, :],
                                           start=(k == 0), stop=(k == J - 1))
                    mm.then_inc(tile_summed, 1)

            def gate_rows():
                pe.wait_ge(params_loaded, 16 * N_PARAMS)
                for k in range(J):
                    pe.wait_ge(u_ready, k + 1)
                    mm = pe.matmul(bank[2][0:32, :], w_gate[:, k, :], uT[:, k, :], start=(k == 0), stop=(k == J - 1))
                mm.then_inc(gates_summed, 1)

            def gate_cols():
                pe.wait_ge(rows_ready, 1)
                pe.wait_ge(row_act, 1)
                for kind in range(7):
                    for d in range(2):
                        for ch in range(C):
                            o = 32 * kind + 16 * d + 4 * ch
                            mm = pe.transpose(bank[3][:, o:o + H_A], row(kind)[:, d, P * ch:P * ch + P],
                                              ident[0:H_A, 0:H_A])
                mm.then_inc(cols_turned, 1)

            def mlstm():
                pe.wait_ge(group_taken, 16)
                pe.wait_ge(cols_dve, 2)
                with pe.Fori(0, H_A // 2) as i:
                    for half in range(2):
                        h = 2 * i + half

                        def v(ch):
                            return va[:, ch, ds(h, 1), :].rearrange("p o e -> p (o e)")

                        q = qT[:, ds(h, 1), :].rearrange("p o t -> p (o t)")
                        pe.wait_ge(qk_staged, 2 * h + 1)
                        pe.wait_ge(joined, 1 + 6 * h)
                        pe.wait_ge(intra_copied, 1 + 3 * h)
                        pe.wait_ge(ka_ready, 1 + 6 * h)
                        for ch in range(C):
                            o = slice(P * ch, P * ch + P)
                            mm = pe.matmul(bank[0][:, o], kh[:, o], q[:, o], start=True, stop=True)
                        mm.then_inc(scores_ready, 1)
                        for ch in range(C):
                            mm = pe.transpose(bank[3][:, P * ch:P * ch + P], kh[:, P * ch:P * ch + P], ident[:, :])
                        mm.then_inc(kh_turned, 1)
                        pe.wait_ge(cell_step, 1 + 6 * h)
                        for d in range(2):
                            pe.wait_ge(ka_ready, 1 + 6 * h + 3 * d + 3)
                            for s in range(3):
                                mm = pe.matmul(bank[4 + d][:, 129 * s:129 * s + 129], ka[:, 3 * d + s, :], v(ORDER[d][s]),
                                               start=True, stop=True)
                            mm.then_inc(update_ready, 1)
                        pe.wait_ge(w_ready, 2 * h + 2)
                        for d in range(2):
                            for ch in range(C):
                                u = 4 * d + ch
                                o = 512 * d + P * ch
                                mm = pe.matmul(bank[u // 3][:, 129 * (u % 3):129 * (u % 3) + 129], bc[:, half, o:o + P], v(ch),
                                               start=True, stop=True)
                        mm.then_inc(intra_ready, 1)
                        pe.wait_ge(qk_staged, 2 * h + 2)
                        for d in range(2):
                            pe.wait_ge(cell_step, 1 + 6 * h + 3 * d + 3)
                            for s in range(1, C):
                                ch = ORDER[d][s]
                                mm = pe.matmul(bank[6 + d][:, 129 * s - 129:129 * s], qh[:, P * ch:P * ch + P],
                                               cell[:, d, s - 1, :], start=True, stop=True)
                            mm.then_inc(inter_ready, 1)

            gate_rows()
            for k in range(J):
                pe.wait_ge(u_ready, k + 1)
            for n, g in enumerate(IN_GROUPS[0][:4]):
                if n == 2:
                    gate_cols()
                project(0, g, 4 * n, turned=n < 2)
            mlstm()

            def project_b():
                for m, g in enumerate(IN_GROUPS[0][4:]):
                    if m == 0:
                        pe.wait_ge(intra_copied, 1 + 12)
                        project(0, g, 16, turned=False)
                        continue
                    project(0, g, 16 + 4 * m, turned=True)
                for m in range(4):
                    pe.wait_ge(silu_done, 8 + m + 1)
                    if m >= 2:
                        pe.wait_ge(v_taken, m - 1)
                    for ch in range(C):
                        mm = pe.transpose(bank[2 + m % 2][:, P * ch:P * ch + P], turned_v[:, m % 2, P * ch:P * ch + P],
                                          ident[:, :])
                    mm.then_inc(v_turned, 1)
                pe.wait_ge(v_taken, 4)
                pe.wait_ge(group_taken, 32)
                for j in range(8):
                    pe.wait_ge(qk_squared, j + 1)
                    pe.matmul(bank[j][:, :], ones[:, :], uT[:, j, :], start=True, stop=True).then_inc(qk_summed, 1)

            def delta_part(i, s_, part):
                modulation_part(MOD_DELTA + RING * i + s_, 6 + s_ % 2, slot_at["mod", 0, MOD_DELTA, 0] + s_, i, part)

            def delta():
                pe.wait_ge(qk_root, 8)
                modulation(MOD_QK, MOD_DELTA)
                with pe.Fori(0, H_A // 2) as i:
                    for half_ in range(2):
                        h = 2 * i + half_
                        q = qT[:, ds(h, 1), :].rearrange("p o t -> p (o t)")
                        pe.wait_ge(qk_staged, 2 * H_A + 2 * h + 1)
                        pe.wait_ge(o_step, 1 + 14 * h)
                        pe.wait_ge(state_ready, 1 + 6 * h)
                        for ch in range(C):
                            o = slice(P * ch, P * ch + P)
                            pe.matmul(bank[0][:, o], kh[:, o], kh[:, o], start=True, stop=True)
                        for ch in range(C):
                            o = slice(P * ch, P * ch + P)
                            mm = pe.matmul(bank[1][:, o], kh[:, o], q[:, o], start=True, stop=True)
                        mm.then_inc(scores_ready, 1)
                        for ch in range(C):
                            mm = pe.transpose(bank[2][:, P * ch:P * ch + P], kh[:, P * ch:P * ch + P], ident[:, :])
                        mm.then_inc(kh_turned, 1)
                        pe.wait_ge(att_ready, 2 * h + 2)
                        pe.wait_ge(ktok_ready, h + 1)
                        for d in range(2):
                            pe.wait_ge(inv_ready, 14 * h + d + 1)
                            for ch in range(C):
                                mm = pe.transpose(bank[3 * d][:, P * ch:P * ch + P], inv[:, d, 1, ch, :], ident[:, :])
                            mm.then_inc(x0_turned, 1)
                        for l in range(1, len(LEVELS)):
                            for d in range(2):
                                pe.wait_ge(mask_ready, 1 + 14 * h + 2 * l + d + 1)
                                if l == 1:
                                    pe.wait_ge(x0_ready, 2 * h + d + 1)
                                else:
                                    pe.wait_ge(inv_ready, 14 * h + 2 * (l - 1) + d + 1)
                                for ch in range(C):
                                    mm = pe.matmul(bank[3 * d][:, P * ch:P * ch + P], masked[:, d, ch, :], inv[:, d, 0, ch, :],
                                                   start=True, stop=True)
                                mm.then_inc(bx_ready, 1)
                            delta_part(i, 3 * half_ + (l - 1) // 2, 2 * ((l - 1) % 2))
                            for d in range(2):
                                pe.wait_ge(bx_copied, 12 * h + 2 * (l - 1) + d + 1)
                                for ch in range(C) if l < len(LEVELS) - 1 else ():
                                    pe.matmul(bank[3 * d + 1][:, P * ch:P * ch + P], inv[:, d, 1, ch, :], half[:, d, ch, :],
                                              start=True, stop=True)
                                for ch in range(C):
                                    mm = pe.matmul(bank[3 * d + 2][:, P * ch:P * ch + P], half[:, d, ch, :], inv[:, d, 1, ch, :],
                                                   start=True, stop=True)
                                mm.then_inc(xbx_ready, 1)
                            delta_part(i, 3 * half_ + (l - 1) // 2, 2 * ((l - 1) % 2) + 1)
                        pe.wait_ge(inv_ready, 14 * h + 14)
                        pe.wait_ge(qk_staged, 2 * H_A + 2 * h + 2)
                        for s in range(C):
                            for d in range(2) if s else ():
                                o = slice(P * ORDER[d][s], P * ORDER[d][s] + P)
                                pe.wait_ge(state_ready, 1 + 6 * h + 2 * (s - 1) + d + 1)
                                pe.matmul(bank[3 * d][:, 0:P], kh[:, o], state_b[:, d, :], start=True, stop=True).then_inc(
                                    carried_ready, 1)
                            for d in range(2):
                                ch = ORDER[d][s]
                                if s == 0:
                                    z = vb[:, ch, ds(h, 1), :].rearrange("p o e -> p (o e)")
                                else:
                                    pe.wait_ge(z_ready, 6 * h + 2 * (s - 1) + d + 1)
                                    z = z_b[:, d, :]
                                pe.matmul(bank[3 * d][:, P:2 * P], inv[:, d, 1, ch, :], z, start=True, stop=True).then_inc(
                                    xz_ready, 1)
                            for d in range(2):
                                ch = ORDER[d][s]
                                o = slice(P * ch, P * ch + P)
                                if s:
                                    pe.wait_ge(o_step, 1 + 14 * h + max(0, 4 * (s - 1) - 2) + (1 if s == 1 else 2) * (d + 1))
                                    pe.matmul(bank[3 * d + 1][:, 0:P], qh[:, o], state_b[:, d, :], start=True, stop=True)
                                pe.wait_ge(v_ready, 8 * h + 2 * s + d + 1)
                                mm = pe.matmul(bank[3 * d + 1][:, P:2 * P], bc[:, half_, 512 * d + P * ch:512 * d + P * ch + P],
                                               vn_b[:, d, :], start=True, stop=True)
                                if s < C - 1:
                                    mm = pe.matmul(bank[3 * d + 2][:, 0:P], ktok[:, ch, :], vd_b[:, d, :], start=True, stop=True)
                                mm.then_inc(outer_ready, 1)

            def project_c(part):
                n0 = 32 + 18 * part
                for k, (g, tiles) in enumerate(zip(IN_GROUPS[1][5 * part:5 * part + 5], (4, 4, 4, 4, 2))):
                    if k == 4:
                        project(1, g, n0, turned=False, t0=N_CTX)
                    else:
                        project(1, g, n0, turned=k < 3, t0=N_CTX if k == 0 else 0, u_from=2 * J if part + k == 0 else None)
                    n0 += tiles

            def hgrn(part):
                with pe.Fori(0, 4) as i:
                    h = 4 * part + i
                    q = q1[:, ds(i, 1), :].rearrange("p o t -> p (o t)")
                    pe.wait_ge(f_ready, 6 * h + 6)
                    pe.wait_ge(cp_done, 1 + 8 * h)
                    for l in range(-1, len(LEVELS)):
                        if l >= 2:
                            pe.wait_ge(cp_done, 1 + 8 * h + l - 1)
                        for d in range(2):
                            if l >= 1:
                                pe.wait_ge(qp_updated, 14 * h + 2 * (l - 1) + d + 1)
                                pe.wait_ge(ks_updated, 14 * h + 2 * (l - 1) + d + 1)
                            for ch in range(2):
                                o = slice(P * ch, P * ch + P)
                                a = P * (2 * d + ch)
                                mm = pe.matmul(bank[2 + (l + 1) % 3][:, a:a + P], ks[:, d, N_CTX + P * ch:N_CTX + P * ch + P],
                                               q[:, o] if l < 0 else qp[:, d, o], start=True, stop=True)
                            mm.then_inc(level_ready, 1)
                    pe.wait_ge(state1_step, 1 + 6 * h)
                    for d in range(2):
                        pe.wait_ge(ks_updated, 14 * h + 13 + d)
                        for s in range(3):
                            o = P * ORDER[d][s]
                            mm = pe.transpose(bank[5 + d][:, P * s:P * s + P], ks[:, d, o:o + P], ident[:, :])
                        mm.then_inc(kd_turned, 1)
                    for d in range(2):
                        pe.wait_ge(kd_ready, 2 * h + d + 1)
                        for s in range(3):
                            v = v1[:, ORDER[d][s], ds(i, 1), :].rearrange("p o e -> p (o e)")
                            mm = pe.matmul(bank[5 + d][:, P * s:P * s + P], kd1[:, d, s, :], v, start=True, stop=True)
                        mm.then_inc(update1_ready, 1)
                    pe.wait_ge(cp_done, 1 + 8 * h + 8)
                    pe.wait_ge(qp_updated, 14 * h + 14)
                    pe.wait_ge(state1_step, 1 + 6 * h + 6)
                    pe.wait_ge(o1_copied, 1 + h)
                    for ch in range(2):
                        v = v1[:, 2 + ch, ds(i, 1), :].rearrange("p o e -> p (o e)")
                        o = bank[7][:, P * ch:P * ch + P]
                        for d in range(2):
                            pe.matmul(o, att1[:, d, ch, :], v, start=(d == 0), stop=False)
                        for d in range(2):
                            s = ORDER[d].index(2 + ch)
                            mm = pe.matmul(o, qp[:, d, P * ch:P * ch + P], state1[:, d, s - 1, :], start=False, stop=(d == 1))
                    mm.then_inc(o1_ready, 1)

            def final():
                for n, (ch, b) in enumerate((ch, b) for ch in range(2) for b in range(2)):
                    pe.wait_ge(u_ready, 4 * J + 4 * b + 4)
                    for j in range(4):
                        mm = pe.transpose(bank[4 + n][:, P * j:P * j + P],
                                          uT[:, 4 * b + j, N_CTX + P * ch:N_CTX + P * ch + P], ident[:, :])
                    mm.then_inc(out_turned, 1)

            def finish_heads(layer, n_heads, chunks):
                for h in range(n_heads):
                    pe.wait_ge(y_ready, 8 * layer + h + 1)
                    if h >= 4:
                        pe.wait_ge(feats_ready, 8 * layer + h - 3)
                    for ch in range(chunks):
                        mm = pe.transpose(bank[h % 4][:, P * ch:P * ch + P], featsT[:, h, P * ch:P * ch + P], ident[:, :])
                    mm.then_inc(y_turned, 1)

            def mix_out(layer, toks, t0):
                at = slot_at["out", layer, 0, 0]
                slot_arrived(pe, at)
                slot_arrived(pe, at + 1)
                pe.wait_ge(feats_ready, 8 * layer + 8)
                for j in range(J):
                    if j >= 4:
                        pe.wait_ge(x_updated, 16 * layer + j - 3)
                    for h in range(8):
                        mm = pe.matmul(bank[4 + j % 4][:, t0:], slot(at + h // 4, 4)[:, h % 4, j::J], featsT[:, h, 0:toks],
                                       start=(h == 0), stop=(h == 7))
                    mm.then_inc(out_summed, 1)

            project_b()
            delta()
            finish_heads(0, 8, C)
            mix_out(0, T, 0)

            def route(layer):
                c0, t0 = seen(layer)
                for k in range(J):
                    pe.wait_ge(u_ready, J * (2 * layer + 1) + k + 1)
                    mm = pe.matmul(bank[1][0:E, t0:], w_r[:, k, :], uT[:, k, t0:], start=(k == 0), stop=(k == J - 1))
                mm.then_inc(logits_summed, 1)
                pe.wait_ge(logits_copied, layer + 1)
                for ch in range(c0, C):
                    mm = pe.transpose(bank[2][:, E * (ch - c0):E * (ch - c0) + E], r_rows[:, P * ch:P * ch + P],
                                      ident[0:E, 0:E])
                mm.then_inc(logits_turned, 1)
                for m, (ch, b) in enumerate((ch, b) for ch in range(c0, C) for b in range(2)):
                    if m >= 4:
                        pe.wait_ge(tok_copied, 8 * layer + m - 3)
                    for j in range(4):
                        mm = pe.transpose(bank[4 + m % 4][:, P * j:P * j + P], uT[:, 4 * b + j, P * ch:P * ch + P], ident[:, :])
                    mm.then_inc(tok_turned, 1)
                if layer == 0:
                    pe.wait_ge(tok_copied, 8)
                    modulation(MOD_LAST, MOD_LAST + 1)
                pe.wait_ge(iota_ready, layer + 1)
                pe.wait_ge(chosen, layer + 1)
                tk = taken[:, :, :].rearrange("p c e -> p (c e)")[:, E * c0:]
                m = E * (C - c0)
                pe.matmul(bank[3][:, E * c0:E * C], before, tk, start=True, stop=True)
                pe.matmul(bank[3][:, E * C + E * c0:2 * E * C], ones[:, :], tk, start=True, stop=True).then_inc(counted, 1)
                if layer == 0:
                    modulation(MOD_LAST + 1, 24)

            def experts(layer):
                c0, t0 = seen(layer)

                def turn(n, half_):
                    pe.wait_ge(xs_in[half_], 16 * n)
                    for j in range(J):
                        mm = pe.transpose(bank[j // 4][:, P * (j % 4):P * (j % 4) + P], xs[:, half_, P * j:P * j + P], ident[:, :])
                    mm.then_inc(xs_turned, 1)

                pe.wait_ge(tabled, layer + 1)
                first, end = pairs_of(pe, layer)
                turn(first + layer + 1, 0)
                with pe.Fori(first, end) as m:
                    for half_ in range(2):
                        i = 2 * m + half_
                        s1, s3, s2 = expert_slots[half_]
                        pe.wait_ge(he_copied, 2 * layer + 2 * i + 2)
                        pe.wait_ge(gated, 1 + i)
                        for s_, b in ((s1, 2), (s3, 3)):
                            pe.wait_ge(expert_in[s_], 16 * m + 16)
                            w = slot(s_, J)
                            for f in range(FT):
                                for k in range(J):
                                    mm = pe.matmul(bank[b][:, P * f:P * f + P], w[:, k, f::FT], he[:, half_, k, :],
                                                   start=(k == 0), stop=(k == J - 1))
                        mm.then_inc(up_summed, 1)
                        turn(m + 1 if half_ == 0 else m + 2 + layer, 1 - half_)
                        pe.wait_ge(gated, 1 + i + 1)
                        pe.wait_ge(expert_in[s2], 16 * m + 16)
                        pe.wait_ge(ye_copied, 1 + 2 * i)
                        w = slot(s2, FT)
                        for b in range(2):
                            for f in range(FT):
                                mm = pe.matmul(bank[4 + b][:, :], act_e[:, f, :], w[:, f, 512 * b:512 * b + 512],
                                               start=(f == 0), stop=(f == FT - 1))
                        mm.then_inc(down_summed, 1)
                for ch in range(c0, C):
                    pe.wait_ge(both_ready, C * layer + ch - c0 + 1)
                    for j in range(J):
                        mm = pe.transpose(bank[j][:, P * ch:P * ch + P], back[0][:, ch, j::J], ident[:, :])
                        if ch == C - 1:
                            mm.then_inc(both_turned, 1)

            norm(1, 0)
            route(0)
            experts(0)
            norm(2, 0)
            project_c(0)
            pe.wait_ge(group_taken, 32 + 18)
            pe.wait_ge(att1_zeroed, 1)
            hgrn(0)
            project_c(1)
            pe.wait_ge(group_taken, 32 + 36)
            hgrn(1)
            finish_heads(1, 8, 2)
            mix_out(1, N_LAT, N_CTX)
            norm(3, N_CTX)
            route(1)
            experts(1)
            norm(4, N_CTX)
            final()


INPUTS = ("x", "c", "ctx", "c_ctx", "w_mod", "b_mod", "norm_mix", "norm_ffn", "norm_final", "ab_w_in", "ab_i_bias",
          "ab_f_bias", "ab_conv", "ab_a_log", "ab_dt_bias", "ab_norm_a", "ab_norm_b", "ab_w_out", "c_w_in", "c_f_bias",
          "c_lb_raw", "c_norm", "c_w_out", "w_router", "router_bias", "w1", "w3", "w2")


def kernel(**inputs):
    import numpy as np
    import concourse.bacc as bacc
    from concourse.bass_utils import run_bass_kernel_spmd

    nc = bacc.Bacc("TRN2", target_bir_lowering=False, num_devices=1)
    arrays, args = {}, {}
    for name in INPUTS:
        a = np.ascontiguousarray(inputs[name])
        arrays[f"in_{name}"] = a
        args[name] = nc.dram_tensor(f"in_{name}", a.shape, mybir.dt.from_np(a.dtype), kind="ExternalInput").ap()
    out = nc.dram_tensor("out_y", (1, N_LAT, D), F32, kind="ExternalOutput").ap()
    hybrid_block(nc, out=out, **args)
    return run_bass_kernel_spmd(nc, [arrays], core_ids=[0]).results[0]["out_y"]
```
